# Optimizing a Trainium2 kernel written in Bass

```python
import math
import jax, jax.numpy as jnp
from jax import lax
import numpy as np

D_MODEL = 1024
BATCH = 1
SEQ = 512
DEPTH = 2

HEAD_DIM = 64
N_NSA_HEADS = 4
N_SSD_HEADS = 8
N_FOX_HEADS = 4
D_NSA = N_NSA_HEADS * HEAD_DIM
D_SSD = N_SSD_HEADS * HEAD_DIM
D_FOX = N_FOX_HEADS * HEAD_DIM
D_MIX = D_NSA + D_SSD + D_FOX
NSA_N_KV_TENSORS = 6
NSA_CMP_BLOCK = 32
NSA_CMP_STRIDE = 16
NSA_SLC_BLOCK = 64
NSA_TOP_N = 16
NSA_WINDOW = 512
NSA_Q_BLOCK = 64
SSD_GROUPS = 2
SSD_D_STATE = 64
SSD_CONV = 4
SSD_CHUNK = 128
SSD_CONV_DIM = D_SSD + 2 * SSD_GROUPS * SSD_D_STATE
FOX_Q_BLOCK = 128
D_FF = 2816
N_EXPERTS = 8
TOP_K = 2
MOE_BLOCK = 128
N_DENSE = (DEPTH + 1) // 2
N_MOE = DEPTH // 2
RMS_EPS = 1e-6
IN_SIZES = (D_NSA, NSA_N_KV_TENSORS * HEAD_DIM, 3 * N_NSA_HEADS,
            D_SSD, SSD_CONV_DIM, N_SSD_HEADS,
            D_FOX, D_FOX, D_FOX, N_FOX_HEADS)
D_IN = sum(IN_SIZES)

kernel_name = 'hybrid_nsa_ssd_fox_moe_block'

def rms_norm(x, g):
    x32 = x.astype(jnp.float32)
    y = x32 * lax.rsqrt(jnp.mean(x32 * x32, axis=-1, keepdims=True) + RMS_EPS)
    return (y * g.astype(jnp.float32)).astype(x.dtype)

def masked_softmax(s, mask):
    s = jnp.where(mask, s.astype(jnp.float32), -jnp.inf)
    m = jnp.max(s, axis=-1, keepdims=True)
    e = jnp.exp(s - jnp.where(jnp.isfinite(m), m, 0.0))
    return e / jnp.maximum(jnp.sum(e, axis=-1, keepdims=True), jnp.finfo(jnp.float32).tiny)

def swiglu(h, w1, w3, w2):
    return (jax.nn.silu(h @ w1) * (h @ w3)) @ w2

def nsa_mixer(q, kv, gates, q_norm, k_norm, pe_k, pe_v, w_ck, w_cv):
    bsz, s = q.shape[0], q.shape[1]
    scale = HEAD_DIM ** -0.5
    q = rms_norm(q, q_norm)
    n_cmp = (s - NSA_CMP_BLOCK) // NSA_CMP_STRIDE + 1
    n_slc = s // NSA_SLC_BLOCK
    top_n = min(NSA_TOP_N, n_slc)
    c_start = jnp.arange(n_cmp) * NSA_CMP_STRIDE
    cmp_idx = c_start[:, None] + jnp.arange(NSA_CMP_BLOCK)[None, :]

    def compress(t, pe, w):
        blocks = t[:, cmp_idx] + pe
        return blocks.reshape(bsz, n_cmp, NSA_CMP_BLOCK * HEAD_DIM) @ w

    kc = rms_norm(compress(kv[:, :, 0], pe_k, w_ck), k_norm)
    vc = compress(kv[:, :, 1], pe_v, w_cv)
    ks = rms_norm(kv[:, :, 2], k_norm).reshape(bsz, n_slc, NSA_SLC_BLOCK, HEAD_DIM)
    vs = kv[:, :, 3].reshape(bsz, n_slc, NSA_SLC_BLOCK, HEAD_DIM)
    kw = jnp.pad(rms_norm(kv[:, :, 4], k_norm), ((0, 0), (NSA_WINDOW, 0), (0, 0)))
    vw = jnp.pad(kv[:, :, 5], ((0, 0), (NSA_WINDOW, 0), (0, 0)))
    n_start = jnp.arange(n_slc) * NSA_SLC_BLOCK
    overlap = ((c_start[:, None] < n_start[None, :] + NSA_SLC_BLOCK)
               & (c_start[:, None] + NSA_CMP_BLOCK > n_start[None, :])).astype(jnp.float32)
    cmp_end = c_start + NSA_CMP_BLOCK - 1
    g = jax.nn.sigmoid(gates.astype(jnp.float32))
    bidx = jnp.arange(bsz)[:, None, None]
    blk_ids = jnp.arange(n_slc)

    def block(i):
        q0 = i * NSA_Q_BLOCK
        t = q0 + jnp.arange(NSA_Q_BLOCK)
        qb = lax.dynamic_slice_in_dim(q, q0, NSA_Q_BLOCK, axis=1)
        gb = lax.dynamic_slice_in_dim(g, q0, NSA_Q_BLOCK, axis=1)
        s_c = jnp.einsum('bqhd,bcd->bhqc', qb, kc) * scale
        p_c = masked_softmax(s_c, cmp_end[None, :] <= t[:, None])
        o_c = jnp.einsum('bhqc,bcd->bqhd', p_c.astype(vc.dtype), vc)
        imp = jnp.einsum('bhqc,cn->bqn', p_c, overlap)
        avail = n_start[None, :] <= t[:, None]
        forced = (blk_ids[None, :] == (t // NSA_SLC_BLOCK)[:, None]) | (blk_ids[None, :] == 0)
        score = jnp.where(avail[None], jnp.where(forced[None], jnp.inf, imp), -jnp.inf)
        _, sel = lax.top_k(score, top_n)
        kg = ks[bidx, sel].reshape(bsz, NSA_Q_BLOCK, top_n * NSA_SLC_BLOCK, HEAD_DIM)
        vg = vs[bidx, sel].reshape(bsz, NSA_Q_BLOCK, top_n * NSA_SLC_BLOCK, HEAD_DIM)
        pos = (sel[..., None] * NSA_SLC_BLOCK + jnp.arange(NSA_SLC_BLOCK)).reshape(
            bsz, NSA_Q_BLOCK, top_n * NSA_SLC_BLOCK)
        s_s = jnp.einsum('bqhd,bqkd->bhqk', qb, kg) * scale
        p_s = masked_softmax(s_s, (pos <= t[None, :, None])[:, None])
        o_s = jnp.einsum('bhqk,bqkd->bqhd', p_s.astype(vg.dtype), vg)
        kwb = lax.dynamic_slice_in_dim(kw, q0, NSA_WINDOW + NSA_Q_BLOCK, axis=1)
        vwb = lax.dynamic_slice_in_dim(vw, q0, NSA_WINDOW + NSA_Q_BLOCK, axis=1)
        s_pos = q0 - NSA_WINDOW + jnp.arange(NSA_WINDOW + NSA_Q_BLOCK)
        mask_w = ((s_pos[None, :] <= t[:, None]) & (s_pos[None, :] > t[:, None] - NSA_WINDOW)
                  & (s_pos[None, :] >= 0))
        s_w = jnp.einsum('bqhd,bkd->bhqk', qb, kwb) * scale
        p_w = masked_softmax(s_w, mask_w)
        o_w = jnp.einsum('bhqk,bkd->bqhd', p_w.astype(vwb.dtype), vwb)
        out = gb[..., 0:1] * o_c + gb[..., 1:2] * o_s + gb[..., 2:3] * o_w
        return out.astype(q.dtype)

    out = lax.map(block, jnp.arange(s // NSA_Q_BLOCK))
    return out.transpose(1, 0, 2, 3, 4).reshape(bsz, s, D_NSA)

def ssd_chunked_scan(x, dt, a, b_in, c_in):
    bsz, s, h, p = x.shape
    n = b_in.shape[-1]
    rep = h // b_in.shape[2]
    nc = s // SSD_CHUNK
    ln = SSD_CHUNK
    b_h = jnp.repeat(b_in, rep, axis=2).reshape(bsz, nc, ln, h, n)
    c_h = jnp.repeat(c_in, rep, axis=2).reshape(bsz, nc, ln, h, n)
    xdt = (x * dt[..., None]).reshape(bsz, nc, ln, h, p)
    a_cs = jnp.cumsum((dt * a).reshape(bsz, nc, ln, h).transpose(0, 3, 1, 2), axis=-1)
    causal = jnp.tril(jnp.ones((ln, ln), dtype=bool))
    decay_in = jnp.exp(jnp.where(causal, a_cs[..., :, None] - a_cs[..., None, :], -jnp.inf))
    scores = jnp.einsum('bclhn,bcshn->bhcls', c_h, b_h) * decay_in
    y_diag = jnp.einsum('bhcls,bcshp->bclhp', scores, xdt)
    decay_to_end = jnp.exp(a_cs[..., -1:] - a_cs)
    chunk_states = jnp.einsum('bclhn,bhcl,bclhp->bchpn', b_h, decay_to_end, xdt)
    chunk_decay = jnp.exp(a_cs[..., -1])

    def step(state, inp):
        st, dec = inp
        return state * dec[..., None, None] + st, state

    init = jnp.zeros((bsz, h, p, n), x.dtype)
    _, prev = lax.scan(step, init, (jnp.moveaxis(chunk_states, 1, 0), jnp.moveaxis(chunk_decay, 2, 0)))
    prev = jnp.moveaxis(prev, 0, 1)
    y_off = jnp.einsum('bclhn,bchpn,bhcl->bclhp', c_h, prev, jnp.exp(a_cs))
    return (y_diag + y_off).reshape(bsz, s, h, p)

def ssd_mixer(z, xbc, dt_raw, conv_w, conv_b, dt_bias, a_log, d_skip, norm_g):
    bsz, s = z.shape[0], z.shape[1]
    xbc = lax.conv_general_dilated(xbc, conv_w[:, None, :], window_strides=(1,),
                                   padding=((SSD_CONV - 1, 0),),
                                   dimension_numbers=('NWC', 'WIO', 'NWC'),
                                   feature_group_count=SSD_CONV_DIM) + conv_b
    xbc = jax.nn.silu(xbc).astype(jnp.float32)
    xs = xbc[..., :D_SSD].reshape(bsz, s, N_SSD_HEADS, HEAD_DIM)
    b_in = xbc[..., D_SSD:D_SSD + SSD_GROUPS * SSD_D_STATE].reshape(bsz, s, SSD_GROUPS, SSD_D_STATE)
    c_in = xbc[..., D_SSD + SSD_GROUPS * SSD_D_STATE:].reshape(bsz, s, SSD_GROUPS, SSD_D_STATE)
    dt = jax.nn.softplus(dt_raw.astype(jnp.float32) + dt_bias.astype(jnp.float32))
    a = -jnp.exp(a_log.astype(jnp.float32))
    y = ssd_chunked_scan(xs, dt, a, b_in, c_in) + xs * d_skip.astype(jnp.float32)[:, None]
    y = y.reshape(bsz, s, D_SSD) * jax.nn.silu(z.astype(jnp.float32))
    return rms_norm(y, norm_g).astype(z.dtype)

def fox_mixer(q, k, v, f_logit, q_norm, k_norm, f_bias):
    bsz, s = q.shape[0], q.shape[1]
    scale = HEAD_DIM ** -0.5
    q = rms_norm(q, q_norm)
    k = rms_norm(k, k_norm)
    log_f = jax.nn.log_sigmoid(f_logit.astype(jnp.float32) + f_bias.astype(jnp.float32))
    c = jnp.cumsum(log_f, axis=1).transpose(0, 2, 1)
    s_idx = jnp.arange(s)

    def block(i):
        q0 = i * FOX_Q_BLOCK
        t = q0 + jnp.arange(FOX_Q_BLOCK)
        qb = lax.dynamic_slice_in_dim(q, q0, FOX_Q_BLOCK, axis=1)
        cq = lax.dynamic_slice_in_dim(c, q0, FOX_Q_BLOCK, axis=2)
        logits = (jnp.einsum('bqhd,bkhd->bhqk', qb, k).astype(jnp.float32) * scale
                  + cq[..., None] - c[:, :, None, :])
        p = masked_softmax(logits, s_idx[None, :] <= t[:, None])
        return jnp.einsum('bhqk,bkhd->bqhd', p.astype(v.dtype), v)

    out = lax.map(block, jnp.arange(s // FOX_Q_BLOCK))
    return out.transpose(1, 0, 2, 3, 4).reshape(bsz, s, D_FOX)

def moe_ffn(h, w_router, w1, w3, w2):
    bsz, s, d = h.shape
    n_tok = bsz * s
    xt = h.reshape(n_tok, d)
    logits = (xt @ w_router).astype(jnp.float32)
    top_v, top_i = lax.top_k(logits, TOP_K)
    gates = jax.nn.softmax(top_v, axis=-1)
    n_rows = n_tok * TOP_K
    flat_e = top_i.reshape(-1)
    flat_tok = jnp.arange(n_rows) // TOP_K
    flat_g = gates.reshape(-1)
    order = jnp.argsort(flat_e)
    e_sorted = flat_e[order]
    tok_sorted = flat_tok[order]
    counts = jnp.bincount(flat_e, length=N_EXPERTS)
    padded = ((counts + MOE_BLOCK - 1) // MOE_BLOCK) * MOE_BLOCK
    start = jnp.cumsum(counts) - counts
    pend = jnp.cumsum(padded)
    pstart = pend - padded
    dest = pstart[e_sorted] + (jnp.arange(n_rows) - start[e_sorted])
    n_blk = -(-n_rows // MOE_BLOCK) + N_EXPERTS
    x_pad = jnp.zeros((n_blk * MOE_BLOCK, d), h.dtype).at[dest].set(xt[tok_sorted])
    blk_e = jnp.minimum(jnp.searchsorted(pend, jnp.arange(n_blk) * MOE_BLOCK, side='right'),
                        N_EXPERTS - 1)

    def expert_block(args):
        xb, e = args
        return swiglu(xb, w1[e], w3[e], w2[e])

    y_pad = lax.map(expert_block, (x_pad.reshape(n_blk, MOE_BLOCK, d), blk_e)).reshape(-1, d)
    y_rows = y_pad[dest] * flat_g[order][:, None].astype(h.dtype)
    out = jnp.zeros((n_tok, d), h.dtype).at[tok_sorted].add(y_rows)
    return out.reshape(bsz, s, d)

def setup_inputs(seed: int = 0) -> dict:
    key = jax.random.key(seed)
    ks = jax.random.split(key, 32)
    f32 = jnp.float32

    def nrm(k, shape, scale):
        return jax.random.normal(k, shape, f32) * scale

    def gain(k, shape):
        return 1.0 + 0.02 * jax.random.normal(k, shape, f32)

    dt = jnp.exp(jax.random.uniform(ks[11], (DEPTH, N_SSD_HEADS), f32, math.log(1e-3), math.log(1e-1)))
    f_init = jax.random.uniform(ks[17], (DEPTH, N_FOX_HEADS), f32, 0.9, 0.999)
    return {
        'x': nrm(ks[0], (BATCH, SEQ, D_MODEL), 1.0),
        'attn_norm': gain(ks[1], (DEPTH, D_MODEL)),
        'w_in': nrm(ks[2], (DEPTH, D_MODEL, D_IN), D_MODEL ** -0.5),
        'nsa_q_norm': gain(ks[3], (DEPTH, HEAD_DIM)),
        'nsa_k_norm': gain(ks[4], (DEPTH, HEAD_DIM)),
        'nsa_cmp_pe_k': nrm(ks[5], (DEPTH, NSA_CMP_BLOCK, HEAD_DIM), 0.1),
        'nsa_cmp_pe_v': nrm(ks[6], (DEPTH, NSA_CMP_BLOCK, HEAD_DIM), 0.1),
        'nsa_cmp_w_k': nrm(ks[7], (DEPTH, NSA_CMP_BLOCK * HEAD_DIM, HEAD_DIM), (NSA_CMP_BLOCK * HEAD_DIM) ** -0.5),
        'nsa_cmp_w_v': nrm(ks[8], (DEPTH, NSA_CMP_BLOCK * HEAD_DIM, HEAD_DIM), (NSA_CMP_BLOCK * HEAD_DIM) ** -0.5),
        'ssd_conv_w': nrm(ks[9], (DEPTH, SSD_CONV, SSD_CONV_DIM), SSD_CONV ** -0.5),
        'ssd_conv_b': nrm(ks[10], (DEPTH, SSD_CONV_DIM), 0.02),
        'ssd_dt_bias': dt + jnp.log(-jnp.expm1(-dt)),
        'ssd_a_log': jnp.log(jax.random.uniform(ks[12], (DEPTH, N_SSD_HEADS), f32, 1.0, 16.0)),
        'ssd_d': gain(ks[13], (DEPTH, N_SSD_HEADS)),
        'ssd_norm': gain(ks[14], (DEPTH, D_SSD)),
        'fox_q_norm': gain(ks[15], (DEPTH, HEAD_DIM)),
        'fox_k_norm': gain(ks[16], (DEPTH, HEAD_DIM)),
        'fox_f_bias': jnp.log(f_init) - jnp.log1p(-f_init),
        'w_out': nrm(ks[18], (DEPTH, D_MIX, D_MODEL), D_MIX ** -0.5),
        'ffn_norm': gain(ks[19], (DEPTH, D_MODEL)),
        'ffn_w1': nrm(ks[20], (N_DENSE, D_MODEL, D_FF), D_MODEL ** -0.5),
        'ffn_w3': nrm(ks[21], (N_DENSE, D_MODEL, D_FF), D_MODEL ** -0.5),
        'ffn_w2': nrm(ks[22], (N_DENSE, D_FF, D_MODEL), D_FF ** -0.5),
        'moe_router': nrm(ks[23], (N_MOE, D_MODEL, N_EXPERTS), D_MODEL ** -0.5),
        'moe_w1': nrm(ks[24], (N_MOE, N_EXPERTS, D_MODEL, D_FF), D_MODEL ** -0.5),
        'moe_w3': nrm(ks[25], (N_MOE, N_EXPERTS, D_MODEL, D_FF), D_MODEL ** -0.5),
        'moe_w2': nrm(ks[26], (N_MOE, N_EXPERTS, D_FF, D_MODEL), D_FF ** -0.5),
    }

def reference(x, attn_norm, w_in, nsa_q_norm, nsa_k_norm, nsa_cmp_pe_k, nsa_cmp_pe_v,
              nsa_cmp_w_k, nsa_cmp_w_v, ssd_conv_w, ssd_conv_b, ssd_dt_bias, ssd_a_log, ssd_d,
              ssd_norm, fox_q_norm, fox_k_norm, fox_f_bias, w_out, ffn_norm, ffn_w1, ffn_w3,
              ffn_w2, moe_router, moe_w1, moe_w3, moe_w2):
    bsz, s, _ = x.shape
    split_pts = np.cumsum(IN_SIZES)[:-1].tolist()
    for layer in range(DEPTH):
        h = rms_norm(x, attn_norm[layer])
        proj = h @ w_in[layer]
        (q_n, kv_n, g_n, z, xbc, dt_raw, q_f, k_f, v_f, f_f) = jnp.split(proj, split_pts, axis=-1)
        o_nsa = nsa_mixer(q_n.reshape(bsz, s, N_NSA_HEADS, HEAD_DIM),
                          kv_n.reshape(bsz, s, NSA_N_KV_TENSORS, HEAD_DIM),
                          g_n.reshape(bsz, s, N_NSA_HEADS, 3),
                          nsa_q_norm[layer], nsa_k_norm[layer], nsa_cmp_pe_k[layer],
                          nsa_cmp_pe_v[layer], nsa_cmp_w_k[layer], nsa_cmp_w_v[layer])
        o_ssd = ssd_mixer(z, xbc, dt_raw, ssd_conv_w[layer], ssd_conv_b[layer], ssd_dt_bias[layer],
                          ssd_a_log[layer], ssd_d[layer], ssd_norm[layer])
        o_fox = fox_mixer(q_f.reshape(bsz, s, N_FOX_HEADS, HEAD_DIM),
                          k_f.reshape(bsz, s, N_FOX_HEADS, HEAD_DIM),
                          v_f.reshape(bsz, s, N_FOX_HEADS, HEAD_DIM),
                          f_f, fox_q_norm[layer], fox_k_norm[layer], fox_f_bias[layer])
        x = x + jnp.concatenate([o_nsa, o_ssd, o_fox], axis=-1) @ w_out[layer]
        h = rms_norm(x, ffn_norm[layer])
        idx = layer // 2
        if layer % 2 == 0:
            x = x + swiglu(h, ffn_w1[idx], ffn_w3[idx], ffn_w2[idx])
        else:
            x = x + moe_ffn(h, moe_router[idx], moe_w1[idx], moe_w3[idx], moe_w2[idx])
    return x


_drawn_inputs = setup_inputs


def setup_inputs(seed=0):
    import zlib

    import numpy as np

    out = dict(_drawn_inputs(seed))
    spreads = {}
    factors = {'nsa_q_norm': 8.0,
     'nsa_k_norm': 5.707,
     'nsa_cmp_pe_k': 4.923,
     'fox_q_norm': 4.276,
     'fox_k_norm': 6.655}
    for name, (base, spread) in spreads.items():
        noise = np.random.default_rng([zlib.crc32(name.encode()), seed]).standard_normal(out[name].shape)
        drawn = base * np.exp(spread * noise) if base else spread * noise
        out[name] = __import__('jax').numpy.asarray(drawn.astype(out[name].dtype))
    for name, factor in factors.items():
        out[name] = (out[name] * factor).astype(out[name].dtype)
    return out
```

```python
import concourse.bass as bass
from concourse import mybir
from concourse.alu_op_type import AluOpType as ALU

F32 = mybir.dt.float32
F32R = mybir.dt.float32r
BF16 = mybir.dt.bfloat16
I32 = mybir.dt.int32
ACT = mybir.ActivationFunctionType
AX = mybir.AxisListType

P = 128
DEPTH = 2
SEQ = 512
DM = 1024
NT = SEQ // P
KT = DM // P
HD = 64
NQ = 4
NF = 4
NS = 8
D_IN = 2712
D_FF = 2816
NE = 8
CMP_BLK, CMP_STRIDE = 32, 16
NC = (SEQ - CMP_BLK) // CMP_STRIDE + 1
EPS = 1e-6
TINY = 1.1754943508222875e-38
NEG = -1e30
BIG_ID = 1 << 20

C_Q, C_KV, C_G, C_Z, C_XBC, C_DT = 0, 256, 640, 652, 1164, 1932
N_XBC = 768
N_TOK = D_IN - N_XBC
O_DT = C_XBC
O_QF = O_DT + NS
O_KF = O_QF + 256
O_VF = O_KF + 256
O_FF = O_VF + 256
W_IN = [(C_XBC, 384, True, 0), (C_XBC + 384, 384, True, 3),
        (C_DT, 390, False, O_DT), (C_DT + 390, 390, False, O_DT + 390),
        (0, 388, False, 0), (388, 388, False, 388), (776, 388, False, 776)]
NW_IN = len(W_IN)
WO_N = 256
NW_OUT = DM // WO_N
WBUF = 392
XM = N_XBC // P

FFC = 256
NCH = D_FF // FFC
FK = FFC // P
NB = 2
PASSES_E = SEQ // (NB * P)
NPASS = NE * PASSES_E
SLOTS = NE * SEQ
R_CW, R_CB, R_QN, R_KN, R_QF, R_KF, R_PE = 0, 24, 30, 31, 32, 33, 34
NR = R_PE + CMP_BLK


def build_program(nc, x, attn_norm, w_in, nsa_q_norm, nsa_k_norm, pe_k, pe_v, w_ck, w_cv,
                  conv_w, conv_b, dt_bias, a_log, ssd_d, ssd_norm, fox_q_norm, fox_k_norm,
                  fox_f_bias, w_out, ffn_norm, ffn_w1, ffn_w3, ffn_w2, router, moe_w1, moe_w3,
                  moe_w2, out, depth=DEPTH, do_ffn=True):
    top = [nc.sbuf_base + (-nc.sbuf_base) % 32]

    def place(name, shape, dtype=F32, at=None):
        size = mybir.dt.size(dtype)
        for n in shape[1:]:
            size *= n
        size += -size % 32
        start = top[0] if at is None else at
        if at is None:
            top[0] += size
        else:
            region_end[0] = max(region_end[0], start + size)
        return nc.alloc_sbuf_tensor_at("b_" + name, shape, dtype, offset=start), start + size

    region_end = [0]

    def fixed(name, shape, dtype=F32):
        return place(name, shape, dtype)[0]

    ident = fixed("ident", [P, P])
    upper = fixed("upper", [P, P])
    supper = fixed("supper", [P, P])
    ones = fixed("ones", [P, P])
    ident_b = fixed("ident_b", [P, P], BF16)
    causal_b = fixed("causal_b", [P, P], BF16)
    causal_tb = fixed("causal_tb", [P, P], BF16)
    cmp_b = fixed("cmp_b", [P, NT, 32], BF16)
    cmp_01 = fixed("cmp_01", [P, NT, 32])
    iota_e = fixed("iota_e", [P, NE])
    iota_i = fixed("iota_i", [P, NE], I32)
    iota_m = fixed("iota_m", [P, NE])
    e0_dense = fixed("e0_dense", [P, NE])
    base_e = fixed("base_e", [P, NE])
    e0 = fixed("e0", [P, NE])
    base_p = fixed("base_p", [P, NE, 2])
    minus_half = fixed("minus_half", [P, 64])
    is_moe = fixed("is_moe", [P, 1])
    is_dense = fixed("is_dense", [P, 1])
    empty_slot = fixed("empty_slot", [P, SLOTS // P + NB, 2], I32)
    g_row = fixed("g_row", [P, DM])
    ssd_g = fixed("ssd_g", [P, 512])
    prow = fixed("prow", [P, 28])
    stack = fixed("stack", [NR, P])
    cols = fixed("cols", [P, NR])
    qcol = fixed("qcol", [66, 2])
    ss_x = fixed("ss_x", [P, NT])
    rs_x = fixed("rs_x", [P, NT])
    ss_f = fixed("ss_f", [P, NT, 8])
    rs_f = fixed("rs_f", [P, NT, 8])
    ss_n = fixed("ss_n", [P, NT, 6])
    rs_n = fixed("rs_n", [P, NT, 6])
    g12 = fixed("g12", [P, NT, 12])
    e12 = fixed("e12", [P, NT, 12])
    dt_t = fixed("dt_t", [P, NT, NS])
    dta = fixed("dta", [P, NT, NS])
    logf = fixed("logf", [P, NT, NF])
    logf_before = fixed("logf_before", [P, NT, NF])
    neg_a = fixed("neg_a", [P, NS])
    acs = fixed("acs", [P, NT, NS])
    to_end = fixed("to_end", [P, NT, NS])
    e_acs = fixed("e_acs", [P, NT, NS])
    e_end = fixed("e_end", [P, NT, NS])
    e_tot = fixed("e_tot", [P, NT, NS])
    gate_e = fixed("gate_e", [P, NT, 12])
    neg_max = fixed("neg_max", [P, 2, 8])
    sums = fixed("sums", [P, 2, 8])
    sum_f = fixed("sum_f", [P, NT, NF])
    sum_n = fixed("sum_n", [P, NT, NQ, 3])
    neg_max_c = fixed("neg_max_c", [P, NQ])
    coef = fixed("coef", [P, NQ, 3])
    ss_y = fixed("ss_y", [P, NT])
    rs_y = fixed("rs_y", [P, NT])
    lg = fixed("lg", [P, NT, NE])
    eq = fixed("eq", [P, NT, NE])
    oh1 = fixed("oh1", [P, NT, NE])
    oh2 = fixed("oh2", [P, NT, NE])
    member = fixed("member", [P, NT, NE])
    member_before = fixed("member_before", [P, NT + 1, NE])
    place_e = fixed("place_e", [P, NT, NE])
    top_v = fixed("top_v", [P, NT, 2])
    gates = fixed("gates", [P, NT, 2])
    first = fixed("first", [P, NT, 2])
    dest = fixed("dest", [P, NT, 2])
    dest_i = fixed("dest_i", [P, 2, NT], I32)
    rows_i = fixed("rows_i", [P, 2, NT, 2], I32)
    left = fixed("left", [P, NE, 2])
    left_i = fixed("left_i", [P, NPASS], I32)
    router_sb = fixed("router_sb", [P, KT, NE])
    base = top[0]

    XH, o = place("XH", [P, NT, DM], at=base)
    proj, o2 = place("proj", [P, NT, N_TOK], at=o)
    h_tok, _ = place("h_tok", [P, NT, DM], at=o)
    x_new, _ = place("x_new", [P, NT, DM], at=o)
    hT_hi, o3 = place("hT_hi", [P, KT, SEQ], F32R, at=o2)
    hT_lo, o4 = place("hT_lo", [P, KT, SEQ], F32R, at=o3)
    w_raw, o5 = place("w_raw", [P, 2, KT, WBUF], at=o4)
    w_hi, o6 = place("w_hi", [P, 2, KT, WBUF], F32R, at=o5)
    w_lo, o7 = place("w_lo", [P, 2, KT, WBUF], F32R, at=o6)
    xbcT, o8 = place("xbcT", [P, XM, SEQ + 4], at=o7)
    xcT, o9 = place("xcT", [P, XM, SEQ], at=o8)
    qa, o10 = place("qa", [P, NT, NF, 66], at=o9)
    ka, o11 = place("ka", [P, NT, NF, 66], at=o10)
    qn, o12 = place("qn", [P, NT, 6, HD], at=o11)
    assert o12 <= nc.sbuf_usable_end, (o12, nc.sbuf_usable_end)
    sq_f = XH[:, :, 0:512]
    sq_n = XH[:, :, 512:896]
    qT_f, a1 = place("qT_f", [66, NF, SEQ], at=o5)
    kT_f, a2 = place("kT_f", [66, NF, SEQ], at=a1)
    qT_n, a3 = place("qT_n", [HD, 6, SEQ], at=a2)
    wcT, a4 = place("wcT", [P, CMP_BLK, HD], at=a3)
    prob, a5 = place("prob", [P, 2, SEQ], at=a4)
    probT, a6 = place("probT", [P, 2, SEQ], at=a5)
    assert a6 <= o7, (a6, o7)
    xs_tok, b1 = place("xs_tok", [P, NT, 512], at=o2)
    b_tok, b2 = place("b_tok", [P, NT, P], at=b1)
    u_dta, b3 = place("u_dta", [P, NS, P], at=b2)
    decay, b4 = place("decay", [P, NS, P], at=b3)
    xdt, b5 = place("xdt", [P, 512], at=b4)
    xdtd, b6 = place("xdtd", [P, 512], at=b5)
    xs_d, b7 = place("xs_d", [P, 512], at=b6)
    state, b8 = place("state", [P, 256], at=b7)
    kvT, b9 = place("kvT", [P, SEQ], at=b8)
    assert b9 <= o4, (b9, o4)
    kv_pe, c1 = place("kv_pe", [P, 2, CMP_BLK, CMP_STRIDE], at=o7)
    kc_n, c2 = place("kc_n", [NC, HD], at=c1)
    kc_sq, c3 = place("kc_sq", [NC, HD], at=c2)
    vc, c4 = place("vc", [NC, HD], at=c3)
    kcT, c5 = place("kcT", [HD, NC], at=c4)
    ss_c, c6 = place("ss_c", [NC, 1], at=c5)
    rs_c, c7 = place("rs_c", [NC, 1], at=c6)
    y_t, c8 = place("y_t", [P, 512], at=c7)
    p_cmp, c9 = place("p_cmp", [P, NQ, 32], at=c8)
    pT_cmp, c10 = place("pT_cmp", [NC, NQ, P], at=c9)
    o_acc, c11 = place("o_acc", [P, 256], at=c10)
    o_part, c12 = place("o_part", [P, 256], at=c11)
    assert c12 <= o8, (c12, o8)
    hT_f = place("hT_f", [P, KT, SEQ], at=o5)[0]
    f_w13, f1 = place("f_w13", [P, 2, KT, 2, FFC], at=base)
    f_w2, f2 = place("f_w2", [P, 2, FK, DM], at=f1)
    f_w13_hi, f3 = place("f_w13_hi", [P, 2, KT, 2, FFC], F32R, at=f2)
    f_w13_lo, f4 = place("f_w13_lo", [P, 2, KT, 2, FFC], F32R, at=f3)
    f_w2_hi, f5 = place("f_w2_hi", [P, 2, FK, DM], F32R, at=f4)
    f_w2_lo, f6 = place("f_w2_lo", [P, 2, FK, DM], F32R, at=f5)
    xT_hi, f7 = place("xT_hi", [P, KT, NB, P], F32R, at=f6)
    xT_lo, f8 = place("xT_lo", [P, KT, NB, P], F32R, at=f7)
    xblk, f9 = place("xblk", [P, NB, DM], at=f8)
    silu, f10 = place("silu", [P, NB, FFC], at=f9)
    gate_up, f11 = place("gate_up", [P, NB, FFC], at=f10)
    gT_hi, f12 = place("gT_hi", [P, NB, FK, P], F32R, at=f11)
    gT_lo, f13 = place("gT_lo", [P, NB, FK, P], F32R, at=f12)
    y_sb, f14 = place("y_sb", [P, NB, DM], at=f13)
    slots_next, f15 = place("slots_next", [P, NB, 2], I32, at=f14)
    slots, f16 = place("slots", [P, NB, 2], I32, at=f15)
    assert f16 <= nc.sbuf_usable_end, (f16, nc.sbuf_usable_end)
    bank = [nc.alloc_psum_tensor(f"bank{n}", [P, 512], F32) for n in range(8)]

    h_rows = nc.dram_tensor("h_rows", (SEQ, DM), F32).ap()
    slot_rows = nc.dram_tensor("slot_rows", (SLOTS + NB * P, 2), I32).ap()

    mix_sems = []

    def sem(name):
        mix_sems.append(nc.alloc_semaphore(name))
        return mix_sems[-1]

    x_loaded = [sem(f"x_loaded{i}") for i in range(NT)]
    x_again = [sem(f"x_again{i}") for i in range(NT)]
    wraw_loaded = [sem(f"wraw_loaded{i}") for i in range(2)]
    (grow_loaded, params_loaded, wcmp_loaded, router_loaded, stored) = map(
        sem, ("grow_loaded", "params_loaded", "wcmp_loaded", "router_loaded", "stored"))
    (cols_t, cols_ready, x_squared, ms_ready, rs_ready, h_ready, xt_done, xt_hi, xt_lo, w_hi_done, w_lo_done,
     unit_done, proj_out, conv_done, silu_done) = map(sem, (
         "cols_t", "cols_ready", "x_squared", "ms_ready", "rs_ready", "h_ready", "xt_done", "xt_hi", "xt_lo",
         "w_hi_done", "w_lo_done", "unit_done", "proj_out", "conv_done", "silu_done"))
    (soft_in, soft_exp, soft_ln, soft_done, head_sq, head_ms, head_rs, fox_ready, nsa_ready, sums_done, acs_ready,
     decays_ready, z_ready, tr_done, tr_out) = map(sem, (
         "soft_in", "soft_exp", "soft_ln", "soft_done", "head_sq", "head_ms", "head_rs", "fox_ready", "nsa_ready",
         "sums_done", "acs_ready", "decays_ready", "z_ready", "tr_done", "tr_out"))
    (u_ready, xdt_ready, ssd_scores, ssd_diff, ssd_exp, ssd_m, ssd_y, ssd_new, state_ready, y_gated, y_squared, y_ms,
     y_rs) = map(sem, (
         "u_ready", "xdt_ready", "ssd_scores", "ssd_diff", "ssd_exp", "ssd_m", "ssd_y", "ssd_new", "state_ready",
         "y_gated", "y_squared", "y_ms", "y_rs"))
    (scores_done, max_ready, exp_done, pT_done, pT_out_act, pT_out_dve, o_done, o_read) = map(sem, (
        "scores_done", "max_ready", "exp_done", "pT_done", "pT_out_act", "pT_out_dve", "o_done", "o_read"))
    (pe_added, kc_done, kc_ms, kc_rs, kc_ready, kcT_done, kcT_out, c_scores, c_shift, c_exp, c_prob, cT_done, cT_out,
     c_out, gate_exp, mixed) = map(sem, (
         "pe_added", "kc_done", "kc_ms", "kc_rs", "kc_ready", "kcT_done", "kcT_out", "c_scores", "c_shift", "c_exp",
         "c_prob", "cT_done", "cT_out", "c_out", "gate_exp", "mixed"))
    (res_added, logits_done, routed, ranks_done, dest_ready, gate_diff, gate_e2, dve_step, pe_step,
     pool_step) = map(sem, (
         "res_added", "logits_done", "routed", "ranks_done", "dest_ready", "gate_diff", "gate_e2", "dve_step",
         "pe_step", "pool_step"))
    def keep(name):
        return nc.alloc_semaphore(name)

    clearing, pool_past = keep("clearing"), keep("pool_past")
    setup_done, setup_dve, layer_done, layer_go = keep("setup_done"), keep("setup_dve"), keep("layer_done"), keep("layer_go")
    scattered, slots_loaded, x_gathered, y_added = (keep("scattered"), keep("slots_loaded"), keep("x_gathered"),
                                                    keep("y_added"))
    f_loaded = [keep(f"f_loaded{s}") for s in range(2)]
    f_hi, f_lo, f_used2 = keep("f_hi"), keep("f_lo"), keep("f_used2")
    h13_done = [keep(f"h13_done{b}") for b in range(NB)]
    silu_out = [keep(f"silu_out{b}") for b in range(NB)]
    gu_ready = [keep(f"gu_ready{b}") for b in range(NB)]
    gT_done, gT_hi_done, gT_lo_done = keep("gT_done"), keep("gT_hi_done"), keep("gT_lo_done")
    y_out = [keep(f"y_out{b}") for b in range(NB)]
    x_tr, x_hi, x_lo = keep("x_tr"), keep("x_hi"), keep("x_lo")
    slots_taken = keep("slots_taken")

    units = []
    for j, (_, w, channels, off) in enumerate(W_IN):
        for m in range(w // P if channels else NT):
            units.append((j, m, channels, off, w))
    unit_of = [[u for u, x_ in enumerate(units) if x_[0] == j] for j in range(NW_IN)]
    att = [(i, i, h, None, O_VF + HD * h, HD * h) for i in range(NT) for h in range(NF)]
    att += [(NT + i, i, h, 4 + br, C_KV + HD * (3 + 2 * br), 256 * br + HD * h)
            for i in range(NT) for h in range(NQ) for br in range(2)]
    NU = len(att)
    by_act = [i in (1, 2) for _, i, *_ in att]
    nth_out = [sum(by_act[:u + 1]) if by_act[u] else u + 1 - sum(by_act[:u + 1]) for u in range(NU)]
    last_of = [max(u for u in range(NU) if att[u][0] == g) for g in range(2 * NT)]
    first_of = [min(u for u in range(NU) if att[u][0] == g) for g in range(2 * NT)]
    z_col = slice(C_Z, C_Z + 512)

    def x_rows(t, src):
        return src[t * P:(t + 1) * P, :]

    def bc(ap, *shape):
        return ap.to_broadcast([P, *shape])

    w_in_v = w_in.rearrange("l (k p) n -> p (l k) n", p=P)
    w_out_v = w_out.rearrange("l (k p) n -> p (l k) n", p=P)
    w_ck_v = w_ck.rearrange("l (j d) n -> d (l j) n", d=HD)
    w_cv_v = w_cv.rearrange("l (j d) n -> d (l j) n", d=HD)
    cw_v = conv_w.rearrange("l t (m c) -> (l t m) c", c=P)
    cb_v = conv_b.rearrange("l (m c) -> (l m) c", c=P)
    pk_v = pe_k.rearrange("l j d -> (l j) d")
    pv_v = pe_v.rearrange("l j d -> (l j) d")
    slot_v = slot_rows.rearrange("(b p) c -> p b c", p=P)
    dense13 = [w.rearrange("l (k p) n -> p (l k) n", p=P) for w in (ffn_w1, ffn_w3)]
    moe13 = [w.rearrange("l e (k p) n -> p (l e k) n", p=P) for w in (moe_w1, moe_w3)]
    dense2 = ffn_w2.rearrange("l (k p) n -> p (l k) n", p=P)
    moe2 = moe_w2.rearrange("l e (k p) n -> p (l e k) n", p=P)

    block_cm = nc.Block()
    block = block_cm.__enter__()

    @block.sync
    def _(sp):
        def load_x(layer, dst, sems):
            with sp.If(layer < 1):
                for t in range(NT):
                    sp.dma_start(dst[:, t, :], x_rows(t, x)).then_inc(sems[t], 16)
                sp.nop()
            with sp.Else():
                for t in range(NT):
                    sp.dma_start(dst[:, t, :], x_rows(t, out)).then_inc(sems[t], 16)
                sp.nop()

        def load_ffn(w13, w2, q, c, s, krow, frow, first):
            sp.wait_ge(f_lo, (q * NCH + c - 1) * 3 if not first else q * NCH * 3)
            for n in range(2):
                sp.dma_start(f_w13[:, s, :, n, :], w13[n][:, krow, bass.ds(c * FFC, FFC)]).then_inc(f_loaded[s], 16)
            sp.dma_start(f_w2[:, s], w2[:, bass.ds(frow + c * FK, FK), :]).then_inc(f_loaded[s], 16)

        with sp.Fori(0, depth) as layer:
            load_x(layer, XH, x_loaded)
            sp.dma_start(g_row[:], attn_norm[bass.ds(layer, 1), :].partition_broadcast(P)).then_inc(grow_loaded, 16)
            for j, (col, w, _, _) in enumerate(W_IN):
                if j >= 2:
                    sp.wait_ge(w_lo_done, j - 1)
                sp.dma_start(w_raw[:, j % 2, :, 0:w], w_in_v[:, bass.ds(layer * KT, KT), col:col + w]).then_inc(
                    wraw_loaded[j % 2], 16)
                if j == 0:
                    small = [
                        (stack[R_CW:R_CB, :], cw_v[bass.ds(layer * 24, 24), :]),
                        (stack[R_CB:R_QN, :], cb_v[bass.ds(layer * 6, 6), :]),
                        (stack[R_QN:R_KN, 0:HD], nsa_q_norm[bass.ds(layer, 1), :]),
                        (stack[R_KN:R_QF, 0:HD], nsa_k_norm[bass.ds(layer, 1), :]),
                        (stack[R_QF:R_KF, 0:HD], fox_q_norm[bass.ds(layer, 1), :]),
                        (stack[R_KF:R_PE, 0:HD], fox_k_norm[bass.ds(layer, 1), :]),
                        (stack[R_PE:NR, 0:HD], pk_v[bass.ds(layer * CMP_BLK, CMP_BLK), :]),
                        (stack[R_PE:NR, HD:P], pv_v[bass.ds(layer * CMP_BLK, CMP_BLK), :]),
                        (prow[:, 0:8], dt_bias[bass.ds(layer, 1), :].partition_broadcast(P)),
                        (prow[:, 8:16], a_log[bass.ds(layer, 1), :].partition_broadcast(P)),
                        (prow[:, 16:24], ssd_d[bass.ds(layer, 1), :].partition_broadcast(P)),
                        (prow[:, 24:28], fox_f_bias[bass.ds(layer, 1), :].partition_broadcast(P)),
                        (ssd_g[:], ssd_norm[bass.ds(layer, 1), :].partition_broadcast(P)),
                        (router_sb[:], router.rearrange("l (k p) n -> p (l k) n", p=P)),
                    ]
                    sp.wait_ge(setup_done, 1)
                    for dst, src in small:
                        sp.dma_start(dst, src).then_inc(params_loaded, 16)
                    sp.dma_start(slot_v, empty_slot[:]).then_inc(router_loaded, 16)
            sp.wait_ge(unit_done, len(units))
            sp.dma_start(wcT[0:HD], w_ck_v[:, bass.ds(layer * CMP_BLK, CMP_BLK), :]).then_inc(wcmp_loaded, 16)
            sp.dma_start(wcT[HD:P], w_cv_v[:, bass.ds(layer * CMP_BLK, CMP_BLK), :]).then_inc(wcmp_loaded, 16)
            sp.wait_ge(h_ready, NT)
            sp.dma_start(g_row[:], ffn_norm[bass.ds(layer, 1), :].partition_broadcast(P)).then_inc(grow_loaded, 16)
            for n in range(NW_OUT):
                j = NW_IN + n
                sp.wait_ge(w_lo_done, j - 1)
                sp.dma_start(w_raw[:, j % 2, :, 0:WO_N], w_out_v[:, bass.ds(layer * KT, KT), n * WO_N:(n + 1) * WO_N]
                             ).then_inc(wraw_loaded[j % 2], 16)
                if n == 0:
                    sp.wait_ge(mixed, 9)
                    load_x(layer, x_new, x_again)
            sp.wait_ge(res_added, NW_OUT * NT)
            for t in range(NT):
                sp.dma_start(x_rows(t, out), x_new[:, t, :]).then_inc(stored, 16)
            sp.wait_ge(h_ready, 2 * NT)
            for t in range(NT):
                sp.dma_start(x_rows(t, h_rows), XH[:, t, :]).then_inc(stored, 16)
            sp.wait_ge(stored, 2 * NT * 16)
            sp.wait_ge(dest_ready, 1)
            if do_ffn:
              with sp.Fori(0, layer * (NPASS - PASSES_E) + PASSES_E) as p:
                q = layer * PASSES_E + p
                n_left = sp.value_load(left_i[0:1, bass.ds(p, 1)], min_val=0, max_val=SEQ)
                with sp.If(n_left > 0):
                    def chunks(w13, w2, krow, frow):
                        load_ffn(w13, w2, q, 0, 0, krow, frow, True)
                        load_ffn(w13, w2, q, 1, 1, krow, frow, True)
                        with sp.Fori(1, NCH // 2) as half:
                            load_ffn(w13, w2, q, half * 2, 0, krow, frow, False)
                            load_ffn(w13, w2, q, half * 2 + 1, 1, krow, frow, False)
                        load_ffn(w13, w2, q, NCH - 1, 0, krow, frow, False)
                    with sp.If(layer < 1):
                        chunks(dense13, dense2, slice(0, KT), 0)
                        sp.nop()
                    with sp.Else():
                        e = sp.snap(p // PASSES_E)
                        chunks(moe13, moe2, bass.ds(e * KT, KT), e * (NCH * FK))
                        sp.nop()
                    sp.nop()
                with sp.Else():
                    sp.wait_ge(f_lo, q * NCH * 3)
                    for s in range(2):
                        sp.sem_inc(f_loaded[s], (NCH + 1 - s) // 2 * 48)
                sp.nop()
            sp.wait_ge(layer_done, (layer + 1) * 4)
            sp.sem_inc(clearing, 1)
            sp.sem_clear(range(mix_sems[0].num, mix_sems[-1].num + 1))
            sp.sem_inc(layer_go, 1)

    @block.gpsimd
    def _(pool):
        def step(ins, count=[0]):
            count[0] += 1
            ins.then_inc(setup_dve, 1)
            pool.wait_ge(setup_dve, count[0])

        step(nc.gpsimd.memset(ones[:], 1.0))
        nc.gpsimd.affine_select(upper[:], ones[:], [[1, P]], ALU.is_ge, 0.0, base=0, channel_multiplier=-1)
        nc.gpsimd.affine_select(supper[:], ones[:], [[1, P]], ALU.is_gt, 0.0, base=0, channel_multiplier=-1)
        step(nc.gpsimd.affine_select(ident[:], ones[:], [[-1, P]], ALU.is_equal, 0.0, base=0, channel_multiplier=1))
        nc.gpsimd.tensor_copy(ident_b[:], ident[:])
        nc.gpsimd.memset(cmp_01[:], 1.0)
        step(nc.gpsimd.memset(causal_b[:], 0.0))
        step(nc.gpsimd.memset(causal_tb[:], 0.0))
        step(nc.gpsimd.memset(cmp_b[:], 0.0))
        nc.gpsimd.affine_select(causal_b[:], causal_b[:], [[-1, P]], ALU.is_ge, NEG, base=0, channel_multiplier=1)
        nc.gpsimd.affine_select(causal_tb[:], causal_tb[:], [[1, P]], ALU.is_ge, NEG, base=0, channel_multiplier=-1)
        for dst, fill in ((cmp_b, NEG), (cmp_01, 0.0)):
            nc.gpsimd.affine_select(dst[:], dst[:], [[P, NT], [-CMP_STRIDE, 32]], ALU.is_ge, fill,
                                    base=1 - CMP_BLK, channel_multiplier=1)
        nc.gpsimd.memset(minus_half[:], -0.5)
        nc.gpsimd.memset(stack[:], 1.0)
        nc.gpsimd.memset(is_moe[:], 0.0)
        nc.gpsimd.memset(is_dense[:], 1.0)
        nc.gpsimd.memset(empty_slot[:].bitcast(F32), 0.0)
        nc.gpsimd.memset(member_before[:], 0.0)
        nc.gpsimd.memset(logf_before[:], 0.0)
        nc.gpsimd.iota(iota_i[:], [[1, NE]], base=0, channel_multiplier=0)
        for c in range(2):
            last = nc.gpsimd.iota(rows_i[:, c, :, 0], [[P, NT]], base=0, channel_multiplier=1)
        step(last)
        nc.gpsimd.iota(empty_slot[:, :, 0], [[0, SLOTS // P + NB]], base=BIG_ID, channel_multiplier=0)
        step(nc.gpsimd.tensor_copy(iota_e[:], iota_i[:]))
        nc.gpsimd.tensor_scalar(iota_m[:], iota_e[:], -float(NE), None, ALU.add)
        nc.gpsimd.tensor_scalar(base_e[:], iota_e[:], float(SEQ), None, ALU.mult)
        for half in range(PASSES_E):
            nc.gpsimd.memset(base_p[:, :, half], float(half * NB * P))
        step(nc.gpsimd.tensor_scalar(e0[:], iota_e[:], 0.0, None, ALU.is_equal))
        nc.gpsimd.nop().then_inc(setup_done, 1)

        with pool.Fori(0, depth) as layer:
            n_step = [0]

            def link(ins):
                n_step[0] += 1
                ins.then_inc(pool_step, 1)
                pool.wait_ge(pool_step, n_step[0])

            def power(dst, src, n, wait, count, done, rows=P):
                pool.wait_ge(wait, count)
                nc.gpsimd.tensor_tensor(dst, src, minus_half[0:rows, 0:n], ALU.pow).then_inc(done, 1)

            power(rs_x[:], ss_x[:], NT, ms_ready, 1, rs_ready)
            pool.wait_ge(h_ready, NT)
            pool.wait_ge(proj_out, unit_of[3][-1] + 1)
            nc.gpsimd.tensor_tensor(sq_f, proj[:, :, O_QF:O_QF + 512], proj[:, :, O_QF:O_QF + 512],
                                    ALU.mult).then_inc(head_sq, 1)
            power(rs_f[:].rearrange("p t h -> p (t h)"), ss_f[:].rearrange("p t h -> p (t h)"), 32, head_ms, 1, head_rs)
            pool.wait_ge(proj_out, unit_of[5][-1] + 1)
            nc.gpsimd.tensor_tensor(sq_n[:, :, 0:256], proj[:, :, 0:256], proj[:, :, 0:256], ALU.mult)
            kvw = proj[:, :, C_KV + 128:C_KV + 384].rearrange("p t (a b) -> p t a b", a=2)[:, :, :, 0:HD]
            nc.gpsimd.tensor_tensor(sq_n[:, :, 256:384].rearrange("p t (a b) -> p t a b", a=2), kvw, kvw,
                                    ALU.mult).then_inc(head_sq, 1)
            power(rs_n[:].rearrange("p t h -> p (t h)"), ss_n[:].rearrange("p t h -> p (t h)"), 24, head_ms, 2, head_rs)
            for c in range(NT):
                xs_c = xs_tok[:, c, :].rearrange("p (h d) -> p h d", h=NS)

                def v(t):
                    return t[:].rearrange("p (h d) -> p h d", h=NS)
                if c == 0:
                    pool.wait_ge(soft_done, 1)
                    pool.wait_ge(decays_ready, 1)
                    pool.wait_ge(tr_out, NT + 1)
                else:
                    pool.wait_ge(ssd_scores, c)
                nc.gpsimd.tensor_tensor(u_dta[:], bc(upper[:].unsqueeze(1), NS, P), bc(dta[:, c, :].unsqueeze(2), NS, P),
                                        ALU.mult).then_inc(u_ready, 1)
                if c:
                    pool.wait_ge(ssd_y, c)
                    pool.wait_ge(y_gated, c)
                link(nc.gpsimd.tensor_tensor(v(xdt), xs_c, bc(dt_t[:, c, :].unsqueeze(2), NS, HD), ALU.mult))
                nc.gpsimd.tensor_tensor(v(xdtd), v(xdt), bc(e_end[:, c, :].unsqueeze(2), NS, HD), ALU.mult)
                nc.gpsimd.tensor_tensor(v(xs_d), xs_c, bc(prow[:, 16:24].unsqueeze(2), NS, HD), ALU.mult
                                        ).then_inc(xdt_ready, 1)
            power(rs_y[:], ss_y[:], NT, y_ms, 1, y_rs)
            power(rs_c[:], ss_c[:], 1, kc_ms, 1, kc_rs, NC)
            power(rs_x[:], ss_x[:], NT, ms_ready, 2, rs_ready)
            pool.wait_ge(router_loaded, 16)
            pool.wait_ge(dest_ready, 1)
            for c in range(2):
                for t in range(NT):
                    pool.indirect_dma_start(slot_rows, bass.IndirectOffsetOnAxis(dest_i[:, c, t:t + 1], 0),
                                            rows_i[:, c, t, :], None, bounds_check=SLOTS - 1, oob_is_err=False
                                            ).then_inc(scattered, 16)
            pool.wait_ge(stored, 2 * NT * 16)
            pool.wait_ge(scattered, (layer + 1) * (2 * NT * 16))
            pool.sem_inc(pool_past, 1)

            def fetch(p, n):
                pool.dma_start(slots_next[:], slot_v[:, bass.ds(p * NB, NB), :]).then_inc(slots_loaded, 16)
                pool.wait_ge(slots_loaded, (n + 1) * 16)
                pool.sem_inc(pool_past, 1)
                for b in range(NB):
                    pool.indirect_dma_start(xblk[:, b, :], None, h_rows,
                                            bass.IndirectOffsetOnAxis(slots_next[:, b, 0:1], 0),
                                            bounds_check=SEQ - 1, oob_is_err=False).then_inc(x_gathered, 16)

            if do_ffn:
              link(nc.gpsimd.memset(xblk[:], 0.0))
              fetch(0, layer * (PASSES_E + 1))
              with pool.Fori(0, layer * (NPASS - PASSES_E) + PASSES_E) as p:
                q = layer * PASSES_E + p
                pool.wait_ge(x_tr, (q + 1) * (KT // 2))
                pool.wait_ge(slots_taken, q + 1)
                fetch(p + 1, layer * (PASSES_E + 1) + p + 1)
                for b in range(NB):
                    pool.wait_ge(y_out[b], q + 1)
                pool.sem_inc(pool_past, 1)
                for b in range(NB):
                    pool.indirect_dma_start(out, bass.IndirectOffsetOnAxis(slots[:, b, 0:1], 0), y_sb[:, b, :], None,
                                            bounds_check=SEQ - 1, oob_is_err=False, compute_op=ALU.add
                                            ).then_inc(y_added, 16)
                pool.nop()
              pool.wait_ge(y_added, (layer * NPASS + PASSES_E) * 32)
              pool.wait_ge(x_gathered, (layer * (NPASS + 1) + PASSES_E + 1) * 32)
            pool.sem_inc(layer_done, 1)
            pool.wait_ge(layer_go, layer + 1)
            pool.nop()

    @block.tensor
    def _(pe):
        mm, tr = nc.tensor.matmul, nc.tensor.transpose

        def three(dst, ah, al, bh, bl, start, stop):
            mm(dst, ah, bh, start=start, stop=False)
            mm(dst, ah, bl, start=False, stop=False)
            return mm(dst, al, bh, start=False, stop=stop)

        pe.wait_ge(setup_done, 1)
        with pe.Fori(0, depth) as layer:
            n_xt, n_step = [0], [0]

            def finish(ins):
                n_step[0] += 1
                ins.then_inc(pe_step, 1)
                pe.wait_ge(pe_step, n_step[0])

            def transpose_tokens(src, read=xt_lo):
                for k in range(KT):
                    n = n_xt[0]
                    if n >= 2:
                        pe.wait_ge(read, n - 1)
                    for t in range(NT):
                        last = tr(bank[n % 2][:, t * P:(t + 1) * P], src[:, t, k * P:(k + 1) * P], ident[:])
                    last.then_inc(xt_done, 1)
                    n_xt[0] += 1

            pe.wait_ge(h_ready, NT)
            transpose_tokens(h_tok)
            pe.wait_ge(params_loaded, 14 * 16)
            tr(bank[7][:, 0:NR], stack[:], ident[0:NR, 0:NR]).then_inc(cols_t, 1)
            pe.wait_ge(xt_lo, KT)
            for u, (j, m, channels, off, w) in enumerate(units):
                s = j % 2
                if u == unit_of[j][0]:
                    pe.wait_ge(w_lo_done, j + 1)
                if u >= 4:
                    pe.wait_ge(proj_out, u - 3)
                b = bank[2 + u % 4]
                ms = slice(m * P, (m + 1) * P)
                for k in range(KT):
                    if channels:
                        last = three(b[:], w_hi[:, s, k, ms], w_lo[:, s, k, ms], hT_hi[:, k, :], hT_lo[:, k, :],
                                     k == 0, k == KT - 1)
                    else:
                        last = three(b[:, 0:w], hT_hi[:, k, ms], hT_lo[:, k, ms], w_hi[:, s, k, 0:w],
                                     w_lo[:, s, k, 0:w], k == 0, k == KT - 1)
                last.then_inc(unit_done, 1)
            pe.wait_ge(soft_done, 1)
            mm(bank[6][:, 0:32], upper[:], dta[:].rearrange("p t h -> p (t h)"), start=True, stop=True)
            mm(bank[6][:, 32:64], ones[:], dta[:].rearrange("p t h -> p (t h)"), start=True, stop=True)
            mm(bank[6][:, 64:80], upper[:], logf[:].rearrange("p t h -> p (t h)"), start=True, stop=False)
            mm(bank[6][:, 64:80], ones[:], logf_before[:].rearrange("p t h -> p (t h)"), start=False, stop=True
               ).then_inc(sums_done, 1)
            pe.wait_ge(silu_done, XM)
            n_tr = [0]

            def one_transpose(parts):
                n = n_tr[0]
                if n >= 2:
                    pe.wait_ge(tr_out, n - 1)
                for dst, src, rows in parts(bank[n % 2]):
                    last = tr(dst, src, ident[0:rows, 0:rows])
                last.then_inc(tr_done, 1)
                n_tr[0] += 1

            tile = [slice(t * P, (t + 1) * P) for t in range(NT)]
            for c in range(NT):
                one_transpose(lambda b: [(b[:, tile[m]], xcT[:, m, tile[c]], P) for m in range(4)])
            one_transpose(lambda b: [(b[:, tile[c]], xcT[:, 4, tile[c]], P) for c in range(NT)])
            pe.wait_ge(fox_ready, 1)
            for h in range(NF):
                for src in (qa, ka):
                    one_transpose(lambda b: [(b[0:66, tile[t]], src[:, t, h, :], P) for t in range(NT)])
            pe.wait_ge(nsa_ready, 1)
            for h in range(6):
                one_transpose(lambda b: [(b[0:HD, tile[t]], qn[:, t, h, :], P) for t in range(NT)])
            one_transpose(lambda b: [(b[:, tile[t]], proj[:, t, C_KV:C_KV + P], P) for t in range(NT)])

            for c in range(NT):
                pe.wait_ge(u_ready, c + 1)
                if c:
                    pe.wait_ge(ssd_m, c)
                for half in range(2):
                    mm(bank[2 + half][:], ones[:], u_dta[:, 4 * half:4 * half + 4, :], start=True, stop=False)
                    mm(bank[2 + half][:].rearrange("p (h l) -> p h l", h=4), ident_b[:],
                       bc(causal_tb[:].unsqueeze(1), 4, P), start=False, stop=True)
                for g in range(2):
                    gp = slice(g * HD, (g + 1) * HD)
                    last = mm(bank[4][:, g * P:(g + 1) * P], xcT[gp, 4, tile[c]], xcT[gp, 5, tile[c]],
                              start=True, stop=True)
                    if g == 0:
                        finish(last)
                last.then_inc(ssd_scores, 1)
                if c:
                    pe.wait_ge(state_ready, c)
                    for g in range(2):
                        gp = slice(g * HD, (g + 1) * HD)
                        last = mm(bank[5][:, g * 256:(g + 1) * 256], xcT[gp, 5, tile[c]], state[gp, :], start=True, stop=True)
                        if g == 0:
                            finish(last)
                pe.wait_ge(xdt_ready, c + 1)
                if c < NT - 1:
                    for g in range(2):
                        gp = slice(g * HD, (g + 1) * HD)
                        last = mm(bank[7][gp, 0:256], b_tok[:, c, gp], xdtd[:, g * 256:(g + 1) * 256],
                                  start=True, stop=True)
                    last.then_inc(ssd_new, 1)
                pe.wait_ge(ssd_m, c + 1)
                if c:
                    pe.wait_ge(y_gated, c)
                for h in range(NS):
                    last = mm(bank[6][:, h * HD:(h + 1) * HD], decay[:, h, :], xdt[:, h * HD:(h + 1) * HD],
                              start=True, stop=True)
                last.then_inc(ssd_y, 1)

            pe.wait_ge(y_gated, NT)
            pe.wait_ge(pe_added, 2)
            pe.wait_ge(wcmp_loaded, 32)
            for kv in range(2):
                rows = slice(kv * HD, (kv + 1) * HD)
                for j in range(CMP_BLK):
                    late = j // CMP_STRIDE
                    last = mm(bank[4][0:NC, kv * HD:(kv + 1) * HD],
                              kv_pe[rows, late, late:late + NC, j % CMP_STRIDE], wcT[rows, j, :],
                              start=j == 0, stop=j == CMP_BLK - 1)
                if kv == 0:
                    finish(last)
            last.then_inc(kc_done, 1)
            pe.wait_ge(kc_ready, 1)
            tr(bank[5][0:HD, 0:NC], kc_n[:], ident[0:NC, 0:NC]).then_inc(kcT_done, 1)

            pe.wait_ge(tr_out, 20)

            def scores(u):
                g, i, h, keys, _, _ = att[u]
                n = (i + 1) * P
                b = bank[u % 2]
                q_, k_ = (qT_f[:, h, tile[i]], kT_f[:, h, 0:n]) if keys is None else (
                    qT_n[:, h, tile[i]], qT_n[:, keys, 0:n])
                mm(b[:, 0:n], q_, k_, start=True, stop=False)
                mm(b[:, n - P:n], ident_b[:], causal_b[:], start=False, stop=True).then_inc(scores_done, 1)

            def turn(u):
                pe.wait_ge(exp_done, u + 1)
                for j in range(att[u][1] + 1):
                    last = tr(bank[2 + u % 2][:, tile[j]], prob[:, u % 2, tile[j]], ident[:])
                last.then_inc(pT_done, 1)

            def weigh(u):
                g, i, h, _, vcol, place_ = att[u]
                pe.wait_ge(pT_out_act if by_act[u] else pT_out_dve, nth_out[u])
                if u == first_of[g] and g >= 2:
                    pe.wait_ge(o_read, g - 1)
                for j in range(i + 1):
                    last = mm(bank[6 + g % 2][:, place_:place_ + HD], probT[:, u % 2, tile[j]],
                              proj[:, j, vcol:vcol + HD], start=j == 0, stop=j == i)
                last.then_inc(o_done, 1)

            def cmp_scores(i):
                if i == 0:
                    pe.wait_ge(kcT_out, 1)
                else:
                    pe.wait_ge(c_shift, i)
                for h in range(NQ):
                    o_ = bank[5][:, 32 * h:32 * h + NC]
                    mm(o_, qT_n[:, h, tile[i]], kcT[:], start=True, stop=False)
                    last = mm(o_, ident_b[:], cmp_b[:, i, 0:NC], start=False, stop=True)
                last.then_inc(c_scores, 1)

            def cmp_turn(i):
                pe.wait_ge(c_prob, i + 1)
                for h in range(NQ):
                    last = tr(bank[5][0:NC, tile[h]], p_cmp[:, h, 0:NC], ident[:])
                last.then_inc(cT_done, 1)

            def cmp_weigh(i):
                pe.wait_ge(cT_out, i + 1)
                if i:
                    pe.wait_ge(o_read, NT + i)
                for h in range(NQ):
                    last = mm(bank[4][:, h * HD:(h + 1) * HD], pT_cmp[:, h, :], vc[:], start=True, stop=True)
                last.then_inc(c_out, 1)

            for u in range(NU + 2):
                if u < NU:
                    scores(u)
                if 1 <= u <= NU:
                    turn(u - 1)
                if u >= 2:
                    weigh(u - 2)
                for i in range(NT):
                    at = u - first_of[NT + i]
                    if at == 0:
                        cmp_scores(i)
                    if at == 4:
                        cmp_turn(i)
                    if at == 6:
                        cmp_weigh(i)

            pe.wait_ge(mixed, 9)
            transpose_tokens(XH)
            pe.wait_ge(xt_lo, 2 * KT)
            for n in range(NW_OUT):
                j = NW_IN + n
                s = j % 2
                pe.wait_ge(w_lo_done, j + 1)
                for t in range(NT):
                    v = n * NT + t
                    if v >= 4:
                        pe.wait_ge(res_added, v - 3)
                    b = bank[2 + v % 4]
                    for k in range(KT):
                        last = three(b[:, 0:WO_N], hT_hi[:, k, tile[t]], hT_lo[:, k, tile[t]], w_hi[:, s, k, 0:WO_N],
                                     w_lo[:, s, k, 0:WO_N], k == 0, k == KT - 1)
                    last.then_inc(unit_done, 1)
            pe.wait_ge(h_ready, 2 * NT)
            transpose_tokens(XH, xt_hi)
            pe.wait_ge(xt_hi, 3 * KT)
            for t in range(NT):
                for k in range(KT):
                    last = mm(bank[2][:, t * NE:(t + 1) * NE], hT_f[:, k, tile[t]], router_sb[:, k, :],
                              start=k == 0, stop=k == KT - 1)
            last.then_inc(logits_done, 1)
            pe.wait_ge(routed, 1)
            flat = member[:].rearrange("p t e -> p (t e)")
            before = member_before[:].rearrange("p t e -> p (t e)")
            mm(bank[3][:, 0:32], supper[:], flat, start=True, stop=False)
            mm(bank[3][:, 0:32], ones[:], before[:, 0:32], start=False, stop=True)
            mm(bank[3][:, 32:40], ones[:], before[:, 32:40], start=True, stop=True).then_inc(ranks_done, 1)

            if do_ffn:
              pe.wait_ge(dest_ready, 1)
              with pe.Fori(0, layer * (NPASS - PASSES_E) + PASSES_E) as p:
                q = layer * PASSES_E + p
                n_left = pe.value_load(left_i[0:1, bass.ds(p, 1)], min_val=0, max_val=SEQ)
                with pe.If(n_left > 0):
                    pe.wait_ge(x_gathered, (layer * (PASSES_E + 1) + p + 1) * 32)
                    for kk in range(KT // 2):
                        if kk >= 2:
                            pe.wait_ge(x_lo, q * (KT // 2) + kk - 1)
                        for k in range(2):
                            for b in range(NB):
                                at = (k * NB + b) * P
                                last = tr(bank[6 + kk % 2][:, at:at + P], xblk[:, b, (2 * kk + k) * P:(2 * kk + k + 1) * P],
                                          ident[:])
                        last.then_inc(x_tr, 1)

                    def up(c, s, b, ks):
                        for k in ks:
                            last = three(bank[4 + b][:], xT_hi[:, k, b, :], xT_lo[:, k, b, :],
                                         f_w13_hi[:, s, k, :, :], f_w13_lo[:, s, k, :, :], k == 0, k == KT - 1)
                        return last

                    def down(s, first_, last_):
                        for b in range(NB):
                            for k in range(FK):
                                for half in range(2):
                                    o_ = bank[2 * b + half][:]
                                    cs = slice(half * 512, (half + 1) * 512)
                                    lst = three(o_, gT_hi[:, b, k, :], gT_lo[:, b, k, :], f_w2_hi[:, s, k, cs],
                                                f_w2_lo[:, s, k, cs], first_ and k == 0, last_ and k == FK - 1)
                        return lst

                    def turn_g(n):
                        for b in range(NB):
                            pe.wait_ge(gu_ready[b], n + 1)
                        for b in range(NB):
                            for k in range(FK):
                                at = (b * FK + k) * P
                                last = tr(bank[6][:, at:at + P], gate_up[:, b, k * P:(k + 1) * P], ident[:])
                        last.then_inc(gT_done, 1)

                    def chunk(c, s, first_=False, second=False, last_=False):
                        n = q * NCH + c
                        if first_:
                            pe.wait_ge(x_lo, (q + 1) * (KT // 2))
                        pe.wait_ge(f_lo, n * 3 + 1)
                        if not first_:
                            pe.wait_ge(gu_ready[0], n)
                        up(c, s, 0, range(0, KT // 2))
                        if not first_:
                            turn_g(n - 1)
                        pe.wait_ge(f_lo, n * 3 + 2)
                        up(c, s, 0, range(KT // 2, KT)).then_inc(h13_done[0], 1)
                        if not first_:
                            pe.wait_ge(gu_ready[1], n)
                        up(c, s, 1, range(KT)).then_inc(h13_done[1], 1)
                        if not first_:
                            pe.wait_ge(gT_lo_done, n)
                            if second:
                                for b in range(NB):
                                    pe.wait_ge(y_out[b], q)
                            pe.wait_ge(f_lo, n * 3)
                            down(1 - s, second, False).then_inc(f_used2, 1)

                    chunk(0, 0, first_=True)
                    chunk(1, 1, second=True)
                    with pe.Fori(1, NCH // 2) as half:
                        chunk(half * 2, 0)
                        chunk(half * 2 + 1, 1)
                    chunk(NCH - 1, 0)
                    n = q * NCH + NCH - 1
                    turn_g(n)
                    pe.wait_ge(gT_lo_done, n + 1)
                    pe.wait_ge(f_lo, n * 3 + 3)
                    down(0, False, True).then_inc(f_used2, 1)
                    pe.nop()
                with pe.Else():
                    pe.wait_ge(f_used2, q * NCH)
                    pe.sem_inc(f_used2, NCH)
                    for b in range(NB):
                        pe.sem_inc(h13_done[b], NCH)
                    pe.sem_inc(gT_done, NCH)
                    pe.sem_inc(x_tr, KT // 2)
                pe.nop()
            pe.sem_inc(layer_done, 1)
            pe.wait_ge(layer_go, layer + 1)
            pe.nop()

    @block.scalar
    def _(act):
        fn = nc.scalar.activation

        act.wait_ge(setup_done, 1)
        with act.Fori(0, depth) as layer:
            n_xt = [0]

            def heads(dst):
                for k in range(KT):
                    n = n_xt[0]
                    act.wait_ge(xt_done, n + 1)
                    fn(dst[:, k, :], bank[n % 2][:], ACT.Copy).then_inc(xt_hi, 1)
                    n_xt[0] += 1

            def split_hi(j):
                s = j % 2
                w = W_IN[j][1] if j < NW_IN else WO_N
                act.wait_ge(wraw_loaded[s], (j // 2 + 1) * 16)
                if NW_IN <= j < NW_IN + 2:
                    act.wait_ge(mixed, 9)
                elif j >= NW_IN + 2:
                    act.wait_ge(unit_done, len(units) + (j - NW_IN - 1) * NT)
                elif j >= 2:
                    act.wait_ge(unit_done, unit_of[j - 2][-1] + 1)
                fn(w_hi[:, s, :, 0:w], w_raw[:, s, :, 0:w], ACT.Copy).then_inc(w_hi_done, 1)

            def move_units(j):
                for u in unit_of[j]:
                    _, m, channels, off, w = units[u]
                    act.wait_ge(unit_done, u + 1)
                    if channels:
                        fn(xbcT[:, off + m, 3:3 + SEQ], bank[2 + u % 4][:], ACT.Copy).then_inc(proj_out, 1)
                    else:
                        fn(proj[:, m, off:off + w], bank[2 + u % 4][:, 0:w], ACT.Copy).then_inc(proj_out, 1)

            for t in range(NT):
                act.wait_ge(x_loaded[t], 16)
                fn(h_tok[:, t, :], XH[:, t, :], ACT.Square, accum_out=ss_x[:, t:t + 1]).then_inc(x_squared, 1)
            split_hi(0)
            split_hi(1)
            heads(hT_hi)
            move_units(0)
            split_hi(2)
            move_units(1)
            split_hi(3)
            for m in range(XM):
                act.wait_ge(conv_done, m + 1)
                fn(xcT[:, m, :], xcT[:, m, :], ACT.Silu).then_inc(silu_done, 1)
            move_units(2)
            split_hi(4)
            move_units(3)
            split_hi(5)
            act.wait_ge(params_loaded, 14 * 16)
            act.wait_ge(soft_in, 1)
            fn(neg_a[:], prow[:, 8:16], ACT.Exp).then_inc(soft_exp, 1)
            fn(e12[:], g12[:], ACT.Exp).then_inc(soft_exp, 1)
            act.wait_ge(soft_exp, 2)
            fn(e12[:], e12[:], ACT.Ln, bias=1.0).then_inc(soft_ln, 1)
            move_units(4)
            split_hi(6)
            move_units(5)
            move_units(6)
            act.wait_ge(proj_out, len(units))
            fn(proj[:, :, z_col], proj[:, :, z_col], ACT.Silu).then_inc(z_ready, 1)
            act.wait_ge(acs_ready, 1)
            fn(e_acs[:], acs[:], ACT.Exp)
            fn(e_end[:], to_end[:], ACT.Exp)
            act.wait_ge(fox_ready, 1)
            fn(e_tot[:].rearrange("p t h -> p (t h)"), bank[6][:, 32:64], ACT.Exp).then_inc(decays_ready, 1)
            fn(gate_e[:], proj[:, :, C_G:C_G + 12], ACT.Exp, scale=-1.0).then_inc(gate_exp, 1)

            n_tr = [0]

            def take(dst, rows, gain=None):
                n = n_tr[0]
                act.wait_ge(tr_done, n + 1)
                if gain is None:
                    fn(dst, bank[n % 2][0:rows, :], ACT.Copy).then_inc(tr_out, 1)
                else:
                    fn(dst, bank[n % 2][0:rows, :], ACT.Copy, scale=gain).then_inc(tr_out, 1)
                n_tr[0] += 1

            for c in range(NT):
                take(xs_tok[:, c, :], P)
            take(b_tok[:].rearrange("p t n -> p (t n)"), P)
            act.wait_ge(cols_ready, 1)
            for h in range(NF):
                take(qT_f[:, h, :], 66, qcol[:, 1:2])
                take(kT_f[:, h, :], 66, cols[0:66, R_KF:R_KF + 1])
            for h in range(6):
                take(qT_n[:, h, :], HD, qcol[0:HD, 0:1] if h < NQ else cols[0:HD, R_KN:R_KN + 1])
            take(kvT[:], P)

            def square_y(c):
                act.wait_ge(y_gated, c + 1)
                if c:
                    act.wait_ge(y_squared, c)
                fn(probT[:, 0, :], XH[:, c, 256:768], ACT.Square, accum_out=ss_y[:, c:c + 1]).then_inc(y_squared, 1)

            for c in range(NT):
                act.wait_ge(ssd_diff, c + 1)
                fn(decay[:], decay[:], ACT.Exp).then_inc(ssd_exp, 1)
                if c:
                    square_y(c - 1)
            square_y(NT - 1)
            act.wait_ge(y_squared, NT)
            act.wait_ge(kcT_done, 1)
            fn(kcT[:], bank[5][0:HD, 0:NC], ACT.Copy, scale=cols[0:HD, R_KN:R_KN + 1]).then_inc(kcT_out, 1)

            def exps(u):
                g, i, h, keys, _, _ = att[u]
                n = (i + 1) * P
                act.wait_ge(max_ready, u + 1)
                if u >= 2:
                    act.wait_ge(pT_done, u - 1)
                total = sum_f[:, i, h:h + 1] if keys is None else sum_n[:, i, h, keys - 3:keys - 2]
                fn(prob[:, u % 2, 0:n], bank[u % 2][:, 0:n], ACT.Exp, bias=neg_max[:, 0, u % 8:u % 8 + 1],
                   accum_out=total).then_inc(exp_done, 1)

            for u in range(NU + 1):
                if u < NU:
                    exps(u)
                if u and by_act[u - 1]:
                    v = u - 1
                    n = (att[v][1] + 1) * P
                    act.wait_ge(pT_done, v + 1)
                    if v >= 2:
                        act.wait_ge(o_done, v - 1)
                    fn(probT[:, v % 2, 0:n], bank[2 + v % 2][:, 0:n], ACT.Copy).then_inc(pT_out_act, 1)
                for i in range(NT):
                    at = u - first_of[NT + i]
                    if at == 2:
                        act.wait_ge(c_shift, i + 1)
                        fn(p_cmp[:, :, 0:NC], p_cmp[:, :, 0:NC], ACT.Exp).then_inc(c_exp, 1)
                    if at == 5:
                        act.wait_ge(cT_done, i + 1)
                        if i:
                            act.wait_ge(c_out, i)
                        fn(pT_cmp[:].rearrange("c h q -> c (h q)"), bank[5][0:NC, :], ACT.Copy).then_inc(cT_out, 1)

            split_hi(NW_IN)
            split_hi(NW_IN + 1)
            heads(hT_hi)
            split_hi(NW_IN + 2)
            split_hi(NW_IN + 3)
            for t in range(NT):
                act.wait_ge(res_added, (NW_OUT - 1) * NT + t + 1)
                fn(XH[:, t, :], x_new[:, t, :], ACT.Square, accum_out=ss_x[:, t:t + 1]).then_inc(x_squared, 1)
            heads(hT_f)
            act.wait_ge(gate_diff, 1)
            fn(gates[:, :, 1], gates[:, :, 0], ACT.Exp).then_inc(gate_e2, 1)

            if do_ffn:
              act.wait_ge(dest_ready, 1)
              with act.Fori(0, layer * (NPASS - PASSES_E) + PASSES_E) as p:
                q = layer * PASSES_E + p
                n_left = act.value_load(left_i[0:1, bass.ds(p, 1)], min_val=0, max_val=SEQ)
                with act.If(n_left > 0):
                    base_n = q * NCH

                    def split(half, s, used, parts):
                        act.wait_ge(f_loaded[s], (q * ((NCH + 1 - s) // 2) + half + 1) * 48)
                        for part in parts:
                            if part == 0:
                                act.wait_ge(h13_done[NB - 1], used)
                            if part == 2:
                                act.wait_ge(f_used2, used)
                                fn(f_w2_hi[:, s], f_w2[:, s], ACT.Copy).then_inc(f_hi, 1)
                            else:
                                ks = slice(part * KT // 2, (part + 1) * KT // 2)
                                fn(f_w13_hi[:, s, ks].rearrange("p k a n -> p (k a n)"),
                                   f_w13[:, s, ks].rearrange("p k a n -> p (k a n)"), ACT.Copy).then_inc(f_hi, 1)

                    def turned(n):
                        act.wait_ge(gT_done, n + 1)
                        act.wait_ge(f_used2, n)
                        fn(gT_hi[:].rearrange("p b k q -> p (b k q)"), bank[6][:], ACT.Copy).then_inc(gT_hi_done, 1)

                    def silu_of(n, b):
                        act.wait_ge(h13_done[b], n + 1)
                        act.wait_ge(gu_ready[b], n)
                        fn(silu[:, b, :], bank[4 + b][:, 0:FFC], ACT.Silu).then_inc(silu_out[b], 1)

                    def chunk(n, following, first_=False):
                        if not first_:
                            turned(n - 1)
                        if following:
                            split(*following, (0,))
                        silu_of(n, 0)
                        if following:
                            split(*following, (1,))
                        silu_of(n, 1)
                        if following:
                            split(*following, (2,))

                    split(0, 0, base_n, (0,))
                    for kk in range(KT // 2):
                        act.wait_ge(x_tr, q * (KT // 2) + kk + 1)
                        fn(xT_hi[:, 2 * kk:2 * kk + 2].rearrange("p k b q -> p (k b q)"), bank[6 + kk % 2][:],
                           ACT.Copy).then_inc(x_hi, 1)
                    split(0, 0, base_n, (1, 2))
                    chunk(base_n, (0, 1, base_n), True)
                    chunk(base_n + 1, (1, 0, base_n + 1))
                    with act.Fori(1, NCH // 2) as half:
                        chunk(base_n + half * 2, (half, 1, base_n + half * 2))
                        chunk(base_n + half * 2 + 1, (half + 1, 0, base_n + half * 2 + 1))
                    chunk(base_n + NCH - 1, None)
                    turned(base_n + NCH - 1)
                    act.wait_ge(f_used2, base_n + NCH)
                    act.wait_ge(y_added, q * 32)
                    act.wait_ge(slots_taken, q + 1)
                    for half in range(2):
                        last = fn(y_sb[:, 0, half * 512:(half + 1) * 512], bank[half][:], ACT.Copy,
                                  scale=slots[:].bitcast(F32)[:, 0, 1:2])
                    last.then_inc(y_out[0], 1)
                    act.nop()
                with act.Else():
                    act.wait_ge(y_out[0], q)
                    act.sem_inc(f_hi, 3 * NCH)
                    for b in range(NB):
                        act.sem_inc(silu_out[b], NCH)
                    act.sem_inc(gT_hi_done, NCH)
                    act.sem_inc(x_hi, KT // 2)
                    act.sem_inc(y_out[0], 1)
                act.nop()
            act.sem_inc(layer_done, 1)
            act.wait_ge(layer_go, layer + 1)
            act.nop()

    @block.vector
    def _(dve):
        tt, ts, stt = nc.vector.tensor_tensor, nc.vector.tensor_scalar, nc.vector.scalar_tensor_tensor
        copy, total = nc.vector.tensor_copy, nc.vector.tensor_reduce

        dve.wait_ge(setup_done, 1)
        with dve.Fori(0, depth) as layer:
            n_step, n_xt = [0], [0]

            def link(ins):
                n_step[0] += 1
                ins.then_inc(dve_step, 1)
                dve.wait_ge(dve_step, n_step[0])

            def mean(ss, n, done):
                ts(ss, ss, 1.0 / n, EPS, ALU.mult, ALU.add).then_inc(done, 1)

            def remainders():
                for k in range(KT):
                    n = n_xt[0]
                    dve.wait_ge(xt_hi, n + 1)
                    tt(hT_lo[:, k, :], bank[n % 2][:], hT_hi[:, k, :].bitcast(F32), ALU.subtract).then_inc(xt_lo, 1)
                    n_xt[0] += 1

            def split_lo(j):
                s = j % 2
                w = W_IN[j][1] if j < NW_IN else WO_N
                dve.wait_ge(w_hi_done, j + 1)
                tt(w_lo[:, s, :, 0:w], w_raw[:, s, :, 0:w], w_hi[:, s, :, 0:w].bitcast(F32), ALU.subtract
                   ).then_inc(w_lo_done, 1)

            def conv(m):
                dve.wait_ge(proj_out, m + 1)
                for tap in range(3, -1, -1):
                    w_ = cols[:, R_CW + tap * 6 + m:R_CW + tap * 6 + m + 1]
                    if tap == 3:
                        link(ts(xcT[:, m, :], xbcT[:, m, 3:3 + SEQ], w_, cols[:, R_CB + m:R_CB + m + 1], ALU.mult, ALU.add))
                    else:
                        ins = stt(xcT[:, m, :], xbcT[:, m, tap:tap + SEQ], w_, xcT[:, m, :], ALU.mult, ALU.add)
                        if tap:
                            link(ins)
                ins.then_inc(conv_done, 1)

            link(nc.vector.memset(xbcT[:, :, 0:3], 0.0))
            dve.wait_ge(x_squared, NT)
            mean(ss_x[:], DM, ms_ready)
            dve.wait_ge(rs_ready, 1)
            dve.wait_ge(grow_loaded, 16)
            for t in range(NT):
                dve.wait_ge(x_loaded[t], 16)
                stt(h_tok[:, t, :], XH[:, t, :], rs_x[:, t:t + 1], g_row[:], ALU.mult, ALU.mult).then_inc(h_ready, 1)
            split_lo(0)
            split_lo(1)
            remainders()
            dve.wait_ge(cols_t, 1)
            link(copy(cols[:], bank[7][:, 0:NR]))
            for n, row in enumerate((R_QN, R_QF)):
                ts(qcol[0:HD, n:n + 1], cols[0:HD, row:row + 1], HD ** -0.5, None, ALU.mult)
                last = copy(qcol[HD:66, n:n + 1], cols[HD:66, row:row + 1])
            last.then_inc(cols_ready, 1)
            split_lo(2)
            for m in range(3):
                conv(m)
            split_lo(3)
            for m in range(3, XM):
                conv(m)
            split_lo(4)
            dve.wait_ge(params_loaded, 14 * 16)
            dve.wait_ge(proj_out, unit_of[3][-1] + 1)
            tt(dt_t[:], proj[:, :, O_DT:O_DT + NS], bc(prow[:, 0:8].unsqueeze(1), NT, NS), ALU.add)
            link(tt(logf[:], proj[:, :, O_FF:O_FF + NF], bc(prow[:, 24:28].unsqueeze(1), NT, NF), ALU.add))
            stt(g12[:, :, 0:8], dt_t[:], -1.0, dt_t[:], ALU.mult, ALU.min)
            stt(g12[:, :, 8:12], logf[:], -1.0, logf[:], ALU.mult, ALU.min).then_inc(soft_in, 1)
            split_lo(5)
            dve.wait_ge(head_sq, 1)
            link(total(ss_f[:], sq_f.rearrange("p t (h d) -> p t h d", d=HD), AX.X, ALU.add))
            mean(ss_f[:], HD, head_ms)
            dve.wait_ge(soft_exp, 2)
            dve.wait_ge(soft_ln, 1)
            stt(dt_t[:], dt_t[:], 0.0, e12[:, :, 0:8], ALU.max, ALU.add)
            link(stt(logf[:], logf[:], 0.0, e12[:, :, 8:12], ALU.min, ALU.subtract))
            stt(dta[:], dt_t[:], -1.0, bc(neg_a[:].unsqueeze(1), NT, NS), ALU.mult, ALU.mult)
            link(copy(logf_before[:, 1, :], logf[:, 0, :]))
            link(tt(logf_before[:, 2, :], logf_before[:, 1, :], logf[:, 1, :], ALU.add))
            tt(logf_before[:, 3, :], logf_before[:, 2, :], logf[:, 2, :], ALU.add).then_inc(soft_done, 1)
            dve.wait_ge(head_rs, 1)
            for n, (dst, off) in enumerate(((qa, O_QF), (ka, O_KF))):
                for t in range(NT):
                    tt(dst[:, t, :, 0:HD], proj[:, t, off:off + 256].rearrange("p (h d) -> p h d", d=HD),
                       bc(rs_f[:, t, 4 * n:4 * n + 4].unsqueeze(2), NF, HD), ALU.mult)
            nc.vector.memset(qa[:, :, :, 65:66], 1.0)
            nc.vector.memset(ka[:, :, :, 64:65], 1.0)
            split_lo(6)
            dve.wait_ge(head_sq, 2)
            link(total(ss_n[:], sq_n.rearrange("p t (h d) -> p t h d", d=HD), AX.X, ALU.add))
            mean(ss_n[:], HD, head_ms)
            dve.wait_ge(sums_done, 1)
            link(copy(acs[:].rearrange("p t h -> p (t h)"), bank[6][:, 0:32]))
            tt(to_end[:].rearrange("p t h -> p (t h)"), bank[6][:, 32:64], acs[:].rearrange("p t h -> p (t h)"),
               ALU.subtract).then_inc(acs_ready, 1)
            c_log = bank[6][:, 64:80].rearrange("p (t h) -> p t h", h=NF)
            copy(qa[:, :, :, 64], c_log)
            ts(ka[:, :, :, 65], c_log, -1.0, None, ALU.mult).then_inc(fox_ready, 1)
            dve.wait_ge(head_rs, 2)
            for t in range(NT):
                tt(qn[:, t, 0:4, :], proj[:, t, 0:256].rearrange("p (h d) -> p h d", d=HD),
                   bc(rs_n[:, t, 0:4].unsqueeze(2), 4, HD), ALU.mult)
            for n in range(2):
                kv_ = C_KV + P * (n + 1)
                last = tt(qn[:, :, 4 + n, :], proj[:, :, kv_:kv_ + HD], bc(rs_n[:, :, 4 + n].unsqueeze(2), NT, HD), ALU.mult)
            last.then_inc(nsa_ready, 1)

            def by_head(ap):
                return ap.rearrange("p (h d) -> p h d", h=NS)

            for c in range(NT):
                dve.wait_ge(ssd_scores, c + 1)
                if c:
                    dve.wait_ge(ssd_y, c)
                for half in range(2):
                    hs = slice(4 * half, 4 * half + 4)
                    last = tt(decay[:, hs, :], bank[2 + half][:].rearrange("p (h l) -> p h l", h=4),
                              bc(acs[:, c, hs].unsqueeze(2), 4, P), ALU.subtract)
                last.then_inc(ssd_diff, 1)
                dve.wait_ge(ssd_exp, c + 1)
                for g in range(2):
                    hs = slice(4 * g, 4 * g + 4)
                    last = tt(decay[:, hs, :], decay[:, hs, :], bc(bank[4][:, g * P:(g + 1) * P].unsqueeze(1), 4, P),
                              ALU.mult)
                last.then_inc(ssd_m, 1)
                if c < NT - 1:
                    dve.wait_ge(ssd_new, c + 1)
                else:
                    dve.wait_ge(ssd_y, c + 1)
                if c:
                    link(tt(by_head(y_t[:]), by_head(bank[5][:]), bc(e_acs[:, c, :].unsqueeze(2), NS, HD), ALU.mult))
                if c < NT - 1:
                    if c == 0:
                        copy(state[:], bank[7][:, 0:256]).then_inc(state_ready, 1)
                    else:
                        for g in range(2):
                            gp = slice(g * HD, (g + 1) * HD)
                            e_ = e_tot[gp, c, 4 * g:4 * g + 4].unsqueeze(2).to_broadcast([HD, 4, HD])
                            last = tt(state[gp, :].rearrange("p (h d) -> p h d", h=4),
                                      state[gp, :].rearrange("p (h d) -> p h d", h=4), e_, ALU.mult)
                        link(last)
                        tt(state[:], state[:], bank[7][:, 0:256], ALU.add).then_inc(state_ready, 1)
                dve.wait_ge(xdt_ready, c + 1)
                dve.wait_ge(ssd_y, c + 1)
                if c:
                    link(tt(y_t[:], y_t[:], xs_d[:], ALU.add))
                    link(tt(y_t[:], bank[6][:], y_t[:], ALU.add))
                else:
                    link(tt(y_t[:], bank[6][:], xs_d[:], ALU.add))
                dve.wait_ge(z_ready, 1)
                tt(XH[:, c, 256:768], y_t[:], proj[:, c, z_col], ALU.mult).then_inc(y_gated, 1)
            dve.wait_ge(tr_out, 20)
            for v in range(2):
                at = R_PE + CMP_STRIDE * v
                tt(kv_pe[:, v], kvT[:].rearrange("p (b j) -> p b j", j=CMP_STRIDE),
                   bc(cols[:, at:at + CMP_STRIDE].unsqueeze(1), CMP_BLK, CMP_STRIDE), ALU.add).then_inc(pe_added, 1)
            dve.wait_ge(y_squared, NT)
            mean(ss_y[:], 512, y_ms)
            dve.wait_ge(kc_done, 1)
            copy(vc[:], bank[4][0:NC, HD:P])
            link(copy(kc_n[:], bank[4][0:NC, 0:HD]))
            link(tt(kc_sq[:], kc_n[:], kc_n[:], ALU.mult))
            link(total(ss_c[:], kc_sq[:], AX.X, ALU.add))
            mean(ss_c[:], HD, kc_ms)
            dve.wait_ge(y_rs, 1)
            for c in range(NT):
                last = stt(XH[:, c, 256:768], XH[:, c, 256:768], rs_y[:, c:c + 1], ssd_g[:], ALU.mult, ALU.mult)
            last.then_inc(mixed, 1)
            dve.wait_ge(kc_rs, 1)
            ts(kc_n[:], kc_n[:], rs_c[:], None, ALU.mult).then_inc(kc_ready, 1)
            dve.wait_ge(gate_exp, 1)
            link(ts(gate_e[:], gate_e[:], 1.0, None, ALU.add))
            link(nc.vector.reciprocal(gate_e[:], gate_e[:]))

            def finalize(g):
                i = g % NT
                dve.wait_ge(o_done, last_of[g] + 1)
                b = bank[6 + g % 2]

                def heads_of(ap):
                    return ap.rearrange("p (h d) -> p h d", h=NQ)
                if g < NT:
                    link(ts(coef[:, :, 0], sum_f[:, i, :], TINY, None, ALU.max))
                    link(nc.vector.reciprocal(coef[:, :, 0], coef[:, :, 0]))
                    last = tt(heads_of(XH[:, i, 768:1024]), heads_of(b[:, 0:256]), bc(coef[:, :, 0].unsqueeze(2), NF, HD),
                              ALU.mult)
                else:
                    dve.wait_ge(c_out, i + 1)
                    link(ts(coef[:], sum_n[:, i], TINY, None, ALU.max))
                    link(nc.vector.reciprocal(coef[:], coef[:]))
                    link(tt(coef[:], coef[:], gate_e[:, i, :].rearrange("p (h b) -> p h b", b=3), ALU.mult))
                    for dst, src, br in ((o_acc[:], bank[4][:, 0:256], 0), (o_part[:], b[:, 0:256], 1)):
                        ins = tt(heads_of(dst), heads_of(src), bc(coef[:, :, br].unsqueeze(2), NQ, HD), ALU.mult)
                    link(ins)
                    link(tt(o_acc[:], o_acc[:], o_part[:], ALU.add))
                    link(tt(heads_of(o_part[:]), heads_of(b[:, 256:512]), bc(coef[:, :, 2].unsqueeze(2), NQ, HD), ALU.mult))
                    last = tt(XH[:, i, 0:256], o_acc[:], o_part[:], ALU.add)
                last.then_inc(o_read, 1)
                dve.wait_ge(o_read, g + 1)
                dve.sem_inc(mixed, 1)

            for u in range(NU + 3):
                if u < NU:
                    n = (att[u][1] + 1) * P
                    dve.wait_ge(scores_done, u + 1)
                    total(neg_max[:, 0, u % 8:u % 8 + 1], bank[u % 2][:, 0:n], AX.X, ALU.max, negate=True
                          ).then_inc(max_ready, 1)
                if 1 <= u <= NU and not by_act[u - 1]:
                    v = u - 1
                    n = (att[v][1] + 1) * P
                    dve.wait_ge(pT_done, v + 1)
                    if v >= 2:
                        dve.wait_ge(o_done, v - 1)
                    copy(probT[:, v % 2, 0:n], bank[2 + v % 2][:, 0:n]).then_inc(pT_out_dve, 1)
                for i in range(NT):
                    at = u - first_of[NT + i]
                    s_c = bank[5][:, 0:P].rearrange("p (h c) -> p h c", h=NQ)[:, :, 0:NC]
                    pc = p_cmp[:, :, 0:NC]
                    if at == 1:
                        dve.wait_ge(c_scores, i + 1)
                        if i:
                            dve.wait_ge(cT_done, i)
                        link(total(neg_max_c[:], s_c, AX.X, ALU.max, negate=True))
                        tt(pc, s_c, bc(neg_max_c[:].unsqueeze(2), NQ, NC), ALU.add).then_inc(c_shift, 1)
                    if at == 3:
                        dve.wait_ge(c_exp, i + 1)
                        link(tt(pc, pc, bc(cmp_01[:, i, 0:NC].unsqueeze(1), NQ, NC), ALU.mult))
                        total(sum_n[:, i, :, 0], pc, AX.X, ALU.add).then_inc(c_prob, 1)
                for g in range(2 * NT):
                    if u == last_of[g] + 3:
                        finalize(g)

            split_lo(NW_IN)
            split_lo(NW_IN + 1)
            remainders()
            for n in range(NW_OUT):
                for t in range(NT):
                    v = n * NT + t
                    dve.wait_ge(unit_done, len(units) + v + 1)
                    if n == 0:
                        dve.wait_ge(x_again[t], 16)
                    cs = slice(n * WO_N, (n + 1) * WO_N)
                    tt(x_new[:, t, cs], x_new[:, t, cs], bank[2 + v % 4][:, 0:WO_N], ALU.add).then_inc(res_added, 1)
                if n < 2:
                    split_lo(NW_IN + 2 + n)
            dve.wait_ge(x_squared, 2 * NT)
            mean(ss_x[:], DM, ms_ready)
            dve.wait_ge(rs_ready, 2)
            dve.wait_ge(grow_loaded, 32)
            dve.wait_ge(xt_done, 2 * KT)
            for t in range(NT):
                stt(XH[:, t, :], x_new[:, t, :], rs_x[:, t:t + 1], g_row[:], ALU.mult, ALU.mult).then_inc(h_ready, 1)

            dve.wait_ge(logits_done, 1)
            copy(lg[:].rearrange("p t e -> p (t e)"), bank[2][:, 0:NT * NE])
            link(tt(e0_dense[:], e0[:], bc(is_dense[:], NE), ALU.mult))
            iota_b = bc(iota_m[:].unsqueeze(1), NT, NE)
            for c, oh in enumerate((oh1, oh2)):
                link(total(top_v[:, :, c], lg[:], AX.X, ALU.max))
                link(tt(eq[:], lg[:], bc(top_v[:, :, c].unsqueeze(2), NT, NE), ALU.is_equal))
                link(tt(eq[:], eq[:], iota_b, ALU.mult))
                link(total(first[:, :, c], eq[:], AX.X, ALU.min))
                link(tt(oh[:], iota_b, bc(first[:, :, c].unsqueeze(2), NT, NE), ALU.is_equal))
                if c == 0:
                    link(stt(lg[:], oh[:], -3e38, lg[:], ALU.mult, ALU.add))
            tt(gates[:, :, 0], top_v[:, :, 1], top_v[:, :, 0], ALU.subtract).then_inc(gate_diff, 1)
            link(ts(oh1[:], oh1[:], is_moe[:], None, ALU.mult))
            link(tt(oh1[:], oh1[:], bc(e0_dense[:].unsqueeze(1), NT, NE), ALU.add))
            link(ts(oh2[:], oh2[:], is_moe[:], None, ALU.mult))
            link(tt(member[:], oh1[:], oh2[:], ALU.add))
            for t in range(NT):
                link(tt(member_before[:, t + 1, :], member_before[:, t, :], member[:, t, :], ALU.add))
            dve.sem_inc(routed, 1)
            dve.wait_ge(gate_e2, 1)
            link(ts(gates[:, :, 0], gates[:, :, 1], 1.0, None, ALU.add))
            link(nc.vector.reciprocal(gates[:, :, 0], gates[:, :, 0]))
            link(tt(gates[:, :, 1], gates[:, :, 1], gates[:, :, 0], ALU.mult))
            link(ts(gates[:], gates[:], is_moe[:], None, ALU.mult))
            link(ts(gates[:, :, 0], gates[:, :, 0], is_dense[:], None, ALU.add))
            for c in range(2):
                copy(rows_i[:].bitcast(F32)[:, c, :, 1], gates[:, :, c])
            dve.wait_ge(ranks_done, 1)
            link(tt(place_e[:], bank[3][:, 0:NT * NE].rearrange("p (t e) -> p t e", e=NE),
                    bc(base_e[:].unsqueeze(1), NT, NE), ALU.add))
            for c, oh in enumerate((oh1, oh2)):
                link(tt(eq[:], place_e[:], oh[:], ALU.mult))
                link(total(dest[:, :, c], eq[:], AX.X, ALU.add))
            link(stt(dest[:, :, 1], bc(is_dense[:], NT), float(BIG_ID), dest[:, :, 1], ALU.mult, ALU.add))
            copy(dest_i[:].rearrange("p c t -> p t c"), dest[:])
            link(tt(left[:], bc(bank[3][:, 32:40].unsqueeze(2), NE, 2), base_p[:], ALU.subtract))
            link(ts(left[:], left[:], 0.0, None, ALU.max))
            copy(left_i[:], left[:].rearrange("p e h -> p (e h)")).then_inc(dest_ready, 1)

            if do_ffn:
              dve.wait_ge(dest_ready, 1)
              with dve.Fori(0, layer * (NPASS - PASSES_E) + PASSES_E) as p:
                q = layer * PASSES_E + p
                n_left = dve.value_load(left_i[0:1, bass.ds(p, 1)], min_val=0, max_val=SEQ)

                def take_slots():
                    dve.wait_ge(slots_loaded, (layer * (PASSES_E + 1) + p + 1) * 16)
                    dve.wait_ge(y_added, q * 32)
                    copy(slots[:], slots_next[:]).then_inc(slots_taken, 1)

                with dve.If(n_left > 0):
                    base_n = q * NCH

                    def split(n, s, parts):
                        for part in parts:
                            dve.wait_ge(f_hi, n * 3 + part + 1)
                            if part == 2:
                                tt(f_w2_lo[:, s], f_w2[:, s], f_w2_hi[:, s].bitcast(F32), ALU.subtract).then_inc(f_lo, 1)
                            else:
                                ks = slice(part * KT // 2, (part + 1) * KT // 2)
                                flat = "p k a n -> p (k a n)"
                                tt(f_w13_lo[:, s, ks].rearrange(flat), f_w13[:, s, ks].rearrange(flat),
                                   f_w13_hi[:, s, ks].bitcast(F32).rearrange(flat), ALU.subtract).then_inc(f_lo, 1)

                    def turned(n):
                        dve.wait_ge(gT_hi_done, n + 1)
                        tt(gT_lo[:].rearrange("p b k q -> p (b k q)"), bank[6][:],
                           gT_hi[:].bitcast(F32).rearrange("p b k q -> p (b k q)"), ALU.subtract).then_inc(gT_lo_done, 1)

                    def gate(n, b):
                        dve.wait_ge(silu_out[b], n + 1)
                        dve.wait_ge(gT_done, n)
                        tt(gate_up[:, b, :], silu[:, b, :], bank[4 + b][:, FFC:2 * FFC], ALU.mult).then_inc(gu_ready[b], 1)

                    def chunk(n, following, first_=False):
                        if not first_:
                            turned(n - 1)
                        if following is not None:
                            split(n + 1, following, (0,))
                        gate(n, 0)
                        if following is not None:
                            split(n + 1, following, (1,))
                        gate(n, 1)
                        if following is not None:
                            split(n + 1, following, (2,))

                    split(base_n, 0, (0,))
                    for kk in range(KT // 2):
                        dve.wait_ge(x_hi, q * (KT // 2) + kk + 1)
                        tt(xT_lo[:, 2 * kk:2 * kk + 2].rearrange("p k b q -> p (k b q)"), bank[6 + kk % 2][:],
                           xT_hi[:, 2 * kk:2 * kk + 2].bitcast(F32).rearrange("p k b q -> p (k b q)"), ALU.subtract
                           ).then_inc(x_lo, 1)
                    split(base_n, 0, (1, 2))
                    chunk(base_n, 1, True)
                    chunk(base_n + 1, 0)
                    take_slots()
                    with dve.Fori(1, NCH // 2) as half:
                        chunk(base_n + half * 2, 1)
                        chunk(base_n + half * 2 + 1, 0)
                    chunk(base_n + NCH - 1, None)
                    turned(base_n + NCH - 1)
                    dve.wait_ge(f_used2, base_n + NCH)
                    for half in range(2):
                        last = ts(y_sb[:, 1, half * 512:(half + 1) * 512], bank[2 + half][:],
                                  slots[:].bitcast(F32)[:, 1, 1:2], None, ALU.mult)
                    last.then_inc(y_out[1], 1)
                    dve.nop()
                with dve.Else():
                    take_slots()
                    dve.wait_ge(y_out[1], q)
                    dve.sem_inc(f_lo, 3 * NCH)
                    for b in range(NB):
                        dve.sem_inc(gu_ready[b], NCH)
                    dve.sem_inc(gT_lo_done, NCH)
                    dve.sem_inc(x_lo, KT // 2)
                    dve.sem_inc(y_out[1], 1)
                dve.nop()
            nc.vector.memset(is_moe[:], 1.0)
            link(nc.vector.memset(is_dense[:], 0.0))
            dve.sem_inc(layer_done, 1)
            dve.wait_ge(layer_go, layer + 1)
            dve.nop()

    block_cm.__exit__(None, None, None)


_INS = ['x', 'attn_norm', 'w_in', 'nsa_q_norm', 'nsa_k_norm', 'nsa_cmp_pe_k', 'nsa_cmp_pe_v', 'nsa_cmp_w_k',
        'nsa_cmp_w_v', 'ssd_conv_w', 'ssd_conv_b', 'ssd_dt_bias', 'ssd_a_log', 'ssd_d', 'ssd_norm', 'fox_q_norm',
        'fox_k_norm', 'fox_f_bias', 'w_out', 'ffn_norm', 'ffn_w1', 'ffn_w3', 'ffn_w2', 'moe_router', 'moe_w1',
        'moe_w3', 'moe_w2']


def kernel(**inputs):
    import numpy as _np
    import concourse.bacc as _bacc
    from concourse import mybir as _mybir
    from concourse.bass_utils import run_bass_kernel_spmd as _run

    nc = _bacc.Bacc("TRN2", target_bir_lowering=False, num_devices=1)
    arrays, args = {}, []
    for name in _INS:
        a = _np.ascontiguousarray(inputs[name])
        if name == 'x':
            a = a.reshape(SEQ, DM)
        arrays[f"in_{name}_dram"] = a
        args.append(nc.dram_tensor(f"in_{name}_dram", a.shape, _mybir.dt.from_np(a.dtype), kind="ExternalInput").ap())
    args.append(nc.dram_tensor("out_0_dram", (SEQ, DM), _mybir.dt.float32, kind="ExternalOutput").ap())
    build_program(nc, *args)
    r = _run(nc, [arrays], core_ids=[0])
    return r.results[0]["out_0_dram"].reshape(1, SEQ, DM)
```

```python
import concourse.bass as bass
from concourse import mybir
from concourse.alu_op_type import AluOpType as ALU

F32 = mybir.dt.float32
F32R = mybir.dt.float32r
BF16 = mybir.dt.bfloat16
I32 = mybir.dt.int32
ACT = mybir.ActivationFunctionType
AX = mybir.AxisListType

P = 128
DEPTH = 2
SEQ = 512
DM = 1024
NT = SEQ // P
KT = DM // P
HD = 64
NQ = 4
NF = 4
NS = 8
D_IN = 2712
D_FF = 2816
NE = 8
CMP_BLK, CMP_STRIDE = 32, 16
NC = (SEQ - CMP_BLK) // CMP_STRIDE + 1
EPS = 1e-6
TINY = 1.1754943508222875e-38
NEG = -1e30
BIG_ID = 1 << 20

C_Q, C_KV, C_G, C_Z, C_XBC, C_DT = 0, 256, 640, 652, 1164, 1932
N_XBC = 768
N_TOK = D_IN - N_XBC
O_DT = C_XBC
O_QF = O_DT + NS
O_KF = O_QF + 256
O_VF = O_KF + 256
O_FF = O_VF + 256
W_IN = [(C_XBC, 384, True, 0), (C_XBC + 384, 384, True, 3),
        (C_DT, 390, False, O_DT), (C_DT + 390, 390, False, O_DT + 390),
        (0, 388, False, 0), (388, 388, False, 388), (776, 388, False, 776)]
NW_IN = len(W_IN)
WO_N = 256
NW_OUT = DM // WO_N
WBUF = 392
XM = N_XBC // P

FFC = 256
NCH = D_FF // FFC
FK = FFC // P
NB = 2
HALVES = SEQ // (NB * P)
NSEG = NE * HALVES
DENSE_ITEMS = HALVES
MOE_ITEMS = 12
assert MOE_ITEMS >= 2 * SEQ // (NB * P) + NE - 1
PAIR = 2 * NCH
START = 1
SLOTS = NE * SEQ
R_CW, R_CB, R_QN, R_KN, R_QF, R_KF, R_PE = 0, 24, 30, 31, 32, 33, 34
NR = R_PE + CMP_BLK
N_PARAMS = 14
NCR = 2 * NF + 2


def build_program(nc, x, attn_norm, w_in, nsa_q_norm, nsa_k_norm, pe_k, pe_v, w_ck, w_cv,
                  conv_w, conv_b, dt_bias, a_log, ssd_d, ssd_norm, fox_q_norm, fox_k_norm,
                  fox_f_bias, w_out, ffn_norm, ffn_w1, ffn_w3, ffn_w2, router, moe_w1, moe_w3,
                  moe_w2, out, depth=DEPTH, do_ffn=True):
    top = [nc.sbuf_base + (-nc.sbuf_base) % 32]

    def place(name, shape, dtype=F32, at=None):
        size = mybir.dt.size(dtype)
        for n in shape[1:]:
            size *= n
        size += -size % 32
        start = top[0] if at is None else at
        if at is None:
            top[0] += size
        else:
            region_end[0] = max(region_end[0], start + size)
        return nc.alloc_sbuf_tensor_at("b_" + name, shape, dtype, offset=start), start + size

    region_end = [0]

    def fixed(name, shape, dtype=F32):
        return place(name, shape, dtype)[0]

    ident = fixed("ident", [P, P])
    upper = fixed("upper", [P, P])
    supper = fixed("supper", [P, P])
    ones = fixed("ones", [P, P])
    ident_b = fixed("ident_b", [P, P], BF16)
    causal_b = fixed("causal_b", [P, P], BF16)
    causal_tb = fixed("causal_tb", [P, P], BF16)
    cmp_b = fixed("cmp_b", [P, NT, 32], BF16)
    cmp_01 = fixed("cmp_01", [P, NT, 32])
    iota_e = fixed("iota_e", [P, NE])
    iota_i = fixed("iota_i", [P, NE], I32)
    iota_m = fixed("iota_m", [P, NE])
    e0_dense = fixed("e0_dense", [P, NE])
    base_e = fixed("base_e", [P, NE])
    e0 = fixed("e0", [P, NE])
    base_p = fixed("base_p", [P, NE, 2])
    seg = fixed("seg", [P, 3, NSEG])
    seg_i = fixed("seg_i", [P, 2, NSEG], I32)
    seg_before = fixed("seg_before", [P, NSEG, NSEG])
    minus_half = fixed("minus_half", [P, 32])
    is_moe = fixed("is_moe", [P, 1])
    is_dense = fixed("is_dense", [P, 1])
    empty_slot = fixed("empty_slot", [P, SLOTS // P + NB, 2], I32)
    g_row = fixed("g_row", [P, DM])
    ssd_g = fixed("ssd_g", [P, 512])
    prow = fixed("prow", [P, 28])
    stack = fixed("stack", [NR, P])
    cols = fixed("cols", [P, NR])
    qcol = fixed("qcol", [P, 2])
    ss_x = fixed("ss_x", [P, NT])
    rs_x = fixed("rs_x", [P, NT])
    ss_f = fixed("ss_f", [P, NT, 8])
    rs_f = fixed("rs_f", [P, NT, 8])
    ss_n = fixed("ss_n", [P, NT, 6])
    rs_n = fixed("rs_n", [P, NT, 6])
    g12 = fixed("g12", [P, NT, 12])
    e12 = fixed("e12", [P, NT, 12])
    dt_t = fixed("dt_t", [P, NT, NS])
    dta = fixed("dta", [P, NT, NS])
    logf = fixed("logf", [P, NT, NF])
    logf_before = fixed("logf_before", [P, NT, NF])
    neg_a = fixed("neg_a", [P, NS])
    acs = fixed("acs", [P, NT, NS])
    to_end = fixed("to_end", [P, NT, NS])
    e_acs = fixed("e_acs", [P, NT, NS])
    e_end = fixed("e_end", [P, NT, NS])
    e_tot = fixed("e_tot", [P, NT, NS])
    gate_e = fixed("gate_e", [P, NT, 12])
    neg_max = fixed("neg_max", [P, 8])
    c_t = fixed("c_t", [P, NT, NF])
    c_hi = fixed("c_hi", [P, NT, NF], F32R)
    sum_f = fixed("sum_f", [P, NT, NF])
    sum_n = fixed("sum_n", [P, NT, NQ, 3])
    neg_max_c = fixed("neg_max_c", [P, NQ])
    coef = fixed("coef", [P, NQ, 3])
    ss_y = fixed("ss_y", [P, NT])
    rs_y = fixed("rs_y", [P, NT])
    lg = fixed("lg", [P, NT, NE])
    eq = fixed("eq", [P, NT, NE])
    oh1 = fixed("oh1", [P, NT, NE])
    oh2 = fixed("oh2", [P, NT, NE])
    member = fixed("member", [P, NT, NE])
    member_before = fixed("member_before", [P, NT + 1, NE])
    place_e = fixed("place_e", [P, NT, NE])
    top_v = fixed("top_v", [P, NT, 2])
    gates = fixed("gates", [P, NT, 2])
    first = fixed("first", [P, NT, 2])
    dest = fixed("dest", [P, NT, 2])
    dest_i = fixed("dest_i", [P, 2, NT], I32)
    rows_i = fixed("rows_i", [P, 2, NT, 2], I32)
    left = fixed("left", [P, NE, 2])
    has = fixed("has", [P, NSEG])
    pos = fixed("pos", [P, NSEG])
    item_f = fixed("item_f", [P, 3, NSEG])
    count_f = fixed("count_f", [P, 1])
    item = fixed("item", [P, 3, NSEG], I32)
    n_items = fixed("n_items", [P, 1], I32)
    router_sb = fixed("router_sb", [P, KT, NE])
    base = top[0]

    XH, o = place("XH", [P, NT, DM], at=base)
    proj, o2 = place("proj", [P, NT, N_TOK], at=o)
    h_tok, _ = place("h_tok", [P, NT, DM], at=o)
    x_new, _ = place("x_new", [P, NT, DM], at=o)
    hT_hi, o3 = place("hT_hi", [P, KT, SEQ], F32R, at=o2)
    hT_lo, o4 = place("hT_lo", [P, KT, SEQ], F32R, at=o3)
    w_raw, o5 = place("w_raw", [P, 2, KT, WBUF], at=o4)
    w_hi, o6 = place("w_hi", [P, 2, KT, WBUF], F32R, at=o5)
    w_lo, o7 = place("w_lo", [P, 2, KT, WBUF], F32R, at=o6)
    xbcT, o8 = place("xbcT", [P, XM, SEQ + 4], at=o7)
    xcT, o9 = place("xcT", [P, XM, SEQ], at=o8)
    qa, o10 = place("qa", [P, NT, NF, HD], at=o9)
    ka, o11 = place("ka", [P, NT, NF, HD], at=o10)
    qn, o12 = place("qn", [P, NT, 6, HD], at=o11)
    assert o12 <= nc.sbuf_usable_end, (o12, nc.sbuf_usable_end)
    sq_f = XH[:, :, 0:512]
    sq_n = XH[:, :, 512:896]
    q_f, a1 = place("q_f", [P, NF, SEQ], F32R, at=o5)
    kh_f, a2 = place("kh_f", [P, NF, SEQ], F32R, at=a1)
    kl_f, a3 = place("kl_f", [P, NF, SEQ], F32R, at=a2)
    q_n, a4 = place("q_n", [P, NQ, SEQ], F32R, at=a3)
    kh_n, a5 = place("kh_n", [P, 2, SEQ], F32R, at=a4)
    kl_n, a6 = place("kl_n", [P, 2, SEQ], F32R, at=a5)
    wcT, a7 = place("wcT", [P, CMP_BLK, HD], at=a6)
    assert a7 <= o7, (a7, o7)
    wo_raw, d1 = place("wo_raw", [P, 2, KT, WO_N], at=o4)
    c_k, d2 = place("c_k", [P, NF, SEQ], F32R, at=d1)
    assert d2 <= o5, (d2, o5)
    xs_tok, b1 = place("xs_tok", [P, NT, 512], at=o2)
    b_tok, b2 = place("b_tok", [P, NT, P], at=b1)
    u_dta, b3 = place("u_dta", [P, NS, P], at=b2)
    decay, b4 = place("decay", [P, NS, P], at=b3)
    xdt, b5 = place("xdt", [P, 512], at=b4)
    xdtd, b6 = place("xdtd", [P, 512], at=b5)
    xs_d, b7 = place("xs_d", [P, 512], at=b6)
    state, b8 = place("state", [P, 256], at=b7)
    kvT, b9 = place("kvT", [P, SEQ], at=b8)
    y_sq, b10 = place("y_sq", [P, 512], at=b9)
    c_q, b11 = place("c_q", [P, SEQ], F32R, at=b10)
    c_src, b12 = place("c_src", [P, NT, 1 + NF, NCR], at=b11)
    assert b12 <= o4, (b12, o4)
    prob, e1 = place("prob", [P, 3, SEQ], at=o2)
    probT, e2 = place("probT", [P, 2, SEQ], at=e1)
    kv_pe, c1 = place("kv_pe", [P, 2, CMP_BLK, CMP_STRIDE], at=o7)
    kc_n, c2 = place("kc_n", [NC, HD], at=c1)
    kc_sq, c3 = place("kc_sq", [NC, HD], at=c2)
    vc, c4 = place("vc", [NC, HD], at=c3)
    kcT, c5 = place("kcT", [P, 2, NC + 1], F32R, at=c4)
    ss_c, c6 = place("ss_c", [NC, 1], at=c5)
    rs_c, c7 = place("rs_c", [NC, 1], at=c6)
    y_t, c8 = place("y_t", [P, 512], at=c7)
    p_cmp, c9 = place("p_cmp", [P, NQ, 32], at=c8)
    pT_cmp, c10 = place("pT_cmp", [NC, NQ, P], at=c9)
    o_acc, c11 = place("o_acc", [P, 256], at=c10)
    o_part, c12 = place("o_part", [P, 256], at=c11)
    assert c12 <= o8, (c12, o8)
    hT_f = place("hT_f", [P, KT, SEQ], at=o5)[0]
    sel, s1 = place("sel", [P, NSEG, NSEG], at=o5)
    sel_v = place("sel_v", [P, NSEG, NSEG], at=s1)[0]
    f_w13, f1 = place("f_w13", [P, 2, KT, 2, FFC], at=base)
    f_w2, f2 = place("f_w2", [P, 2, FK, DM], at=f1)
    f_w13_hi, f3 = place("f_w13_hi", [P, 2, KT, 2, FFC], F32R, at=f2)
    f_w13_lo, f4 = place("f_w13_lo", [P, 2, KT, 2, FFC], F32R, at=f3)
    f_w2_hi, f5 = place("f_w2_hi", [P, 2, FK, DM], F32R, at=f4)
    f_w2_lo, f6 = place("f_w2_lo", [P, 2, FK, DM], F32R, at=f5)
    xT_hi, f7 = place("xT_hi", [P, KT, NB, P], F32R, at=f6)
    xT_lo, f8 = place("xT_lo", [P, KT, NB, P], F32R, at=f7)
    xblk, f9 = place("xblk", [P, NB, DM], at=f8)
    silu, f10 = place("silu", [P, NB, FFC], at=f9)
    gate_up, f11 = place("gate_up", [P, NB, FFC], at=f10)
    gT_hi, f12 = place("gT_hi", [P, NB, FK, P], F32R, at=f11)
    gT_lo, f13 = place("gT_lo", [P, NB, FK, P], F32R, at=f12)
    y_sb, f14 = place("y_sb", [P, NB, DM], at=f13)
    slots_next, f15 = place("slots_next", [P, NB, 2], I32, at=f14)
    slots, f16 = place("slots", [P, NB, 2], I32, at=f15)
    assert f16 <= nc.sbuf_usable_end, (f16, nc.sbuf_usable_end)
    bank = [nc.alloc_psum_tensor(f"bank{n}", [P, 512], F32) for n in range(8)]

    h_rows = nc.dram_tensor("h_rows", (SEQ, DM), F32).ap()
    slot_rows = nc.dram_tensor("slot_rows", (SLOTS + NB * P, 2), I32).ap()

    mix_sems = []

    def sem(name):
        mix_sems.append(nc.alloc_semaphore(name))
        return mix_sems[-1]

    x_loaded = [sem(f"x_loaded{i}") for i in range(NT)]
    x_again = [sem(f"x_again{i}") for i in range(NT)]
    wraw_loaded = [sem(f"wraw_loaded{i}") for i in range(2)]
    (grow_loaded, params_loaded, wcmp_loaded, router_loaded, stored) = map(
        sem, ("grow_loaded", "params_loaded", "wcmp_loaded", "router_loaded", "stored"))
    (cols_t, cols_ready, x_squared, ms_ready, rs_ready, h_ready, xt_done, xt_hi, xt_lo, w_hi_done, w_lo_done,
     unit_done, proj_out, conv_done, silu_done) = map(sem, (
         "cols_t", "cols_ready", "x_squared", "ms_ready", "rs_ready", "h_ready", "xt_done", "xt_hi", "xt_lo",
         "w_hi_done", "w_lo_done", "unit_done", "proj_out", "conv_done", "silu_done"))
    (soft_in, soft_exp, soft_ln, soft_done, head_sq, head_ms, head_rs, fox_ready, nsa_ready, sums_done, acs_ready,
     decays_ready, z_ready, tr_done, tr_out) = map(sem, (
         "soft_in", "soft_exp", "soft_ln", "soft_done", "head_sq", "head_ms", "head_rs", "fox_ready", "nsa_ready",
         "sums_done", "acs_ready", "decays_ready", "z_ready", "tr_done", "tr_out"))
    (u_ready, xdt_ready, ssd_scores, ssd_diff, ssd_exp, ssd_m, ssd_y, ssd_new, state_ready, y_gated, y_squared, y_ms,
     y_rs) = map(sem, (
         "u_ready", "xdt_ready", "ssd_scores", "ssd_diff", "ssd_exp", "ssd_m", "ssd_y", "ssd_new", "state_ready",
         "y_gated", "y_squared", "y_ms", "y_rs"))
    (scores_done, max_ready, exp_done, pT_done, pT_out_act, pT_out_dve, o_done, o_read) = map(sem, (
        "scores_done", "max_ready", "exp_done", "pT_done", "pT_out_act", "pT_out_dve", "o_done", "o_read"))
    (pe_added, kc_done, kc_ms, kc_rs, kc_ready, kcT_done, kcT_out, c_scores, c_shift, c_exp, c_prob, cT_done, cT_out,
     c_out, gate_exp, mixed) = map(sem, (
         "pe_added", "kc_done", "kc_ms", "kc_rs", "kc_ready", "kcT_done", "kcT_out", "c_scores", "c_shift", "c_exp",
         "c_prob", "cT_done", "cT_out", "c_out", "gate_exp", "mixed"))
    (res_added, logits_done, routed, ranks_done, dest_ready, gate_diff, gate_e2, dve_step, pe_step,
     pool_step) = map(sem, (
         "res_added", "logits_done", "routed", "ranks_done", "dest_ready", "gate_diff", "gate_e2", "dve_step",
         "pe_step", "pool_step"))
    tr_lo, c_ready, c_set, kcT_lo = sem("tr_lo"), sem("c_ready"), sem("c_set"), sem("kcT_lo")
    f_loaded = [sem(f"f_loaded{s}") for s in range(2)]
    f_hi, f_lo, f_used2 = sem("f_hi"), sem("f_lo"), sem("f_used2")
    h13_done = [sem(f"h13_done{b}") for b in range(NB)]
    silu_out = [sem(f"silu_out{b}") for b in range(NB)]
    gu_ready = [sem(f"gu_ready{b}") for b in range(NB)]
    gT_done, gT_hi_done, gT_lo_done = sem("gT_done"), sem("gT_hi_done"), sem("gT_lo_done")
    y_out = [sem(f"y_out{b}") for b in range(2)]
    x_tr, x_hi, x_lo = sem("x_tr"), sem("x_hi"), sem("x_lo")
    slots_taken = sem("slots_taken")

    def keep(name):
        return nc.alloc_semaphore(name)

    clearing, pool_past = keep("clearing"), keep("pool_past")
    setup_done, setup_dve, layer_done, layer_go = keep("setup_done"), keep("setup_dve"), keep("layer_done"), keep("layer_go")
    scattered, slots_loaded, x_gathered, y_added = (keep("scattered"), keep("slots_loaded"), keep("x_gathered"),
                                                    keep("y_added"))

    units = []
    for j, (_, w, channels, off) in enumerate(W_IN):
        for m in range(w // P if channels else NT):
            units.append((j, m, channels, off, w))
    unit_of = [[u for u, x_ in enumerate(units) if x_[0] == j] for j in range(NW_IN)]
    att = [(i, i, h, None, O_VF + HD * h, HD * h) for i in range(NT) for h in range(NF)]
    att += [(NT + i, i, h, 4 + br, C_KV + HD * (3 + 2 * br), 256 * br + HD * h)
            for i in range(NT) for h in range(NQ) for br in range(2)]
    NU = len(att)
    by_act = [i in (1, 2) for _, i, *_ in att]
    nth_out = [sum(by_act[:u + 1]) if by_act[u] else u + 1 - sum(by_act[:u + 1]) for u in range(NU)]
    s_bank = (0, 1, 5)
    last_of = [max(u for u in range(NU) if att[u][0] == g) for g in range(2 * NT)]
    first_of = [min(u for u in range(NU) if att[u][0] == g) for g in range(2 * NT)]
    z_col = slice(C_Z, C_Z + 512)

    def x_rows(t, src):
        return src[t * P:(t + 1) * P, :]

    def bc(ap, *shape):
        return ap.to_broadcast([P, *shape])

    w_in_v = w_in.rearrange("l (k p) n -> p (l k) n", p=P)
    w_out_v = w_out.rearrange("l (k p) n -> p (l k) n", p=P)
    w_ck_v = w_ck.rearrange("l (j d) n -> d (l j) n", d=HD)
    w_cv_v = w_cv.rearrange("l (j d) n -> d (l j) n", d=HD)
    cw_v = conv_w.rearrange("l t (m c) -> (l t m) c", c=P)
    cb_v = conv_b.rearrange("l (m c) -> (l m) c", c=P)
    pk_v = pe_k.rearrange("l j d -> (l j) d")
    pv_v = pe_v.rearrange("l j d -> (l j) d")
    slot_v = slot_rows.rearrange("(b p) c -> p b c", p=P)
    dense13 = [w.rearrange("l (k p) n -> p (l k) n", p=P) for w in (ffn_w1, ffn_w3)]
    moe13 = [w.rearrange("l e (k p) n -> p (l e k) n", p=P) for w in (moe_w1, moe_w3)]
    dense2 = ffn_w2.rearrange("l (k p) n -> p (l k) n", p=P)
    moe2 = moe_w2.rearrange("l e (k p) n -> p (l e k) n", p=P)

    block_cm = nc.Block()
    block = block_cm.__enter__()

    @block.sync
    def _(sp):
        def load_x(layer, dst, sems):
            with sp.If(layer < 1):
                for t in range(NT):
                    sp.dma_start(dst[:, t, :], x_rows(t, x)).then_inc(sems[t], 16)
                sp.nop()
            with sp.Else():
                for t in range(NT):
                    sp.dma_start(dst[:, t, :], x_rows(t, out)).then_inc(sems[t], 16)
                sp.nop()

        def load_ffn(w13, w2, n, c, s, krow, frow):
            if n is not None:
                sp.wait_ge(f_lo, n * 3 - 3 + START)
            for i in range(2):
                sp.dma_start(f_w13[:, s, :, i, :], w13[i][:, krow, bass.ds(c * FFC, FFC)]).then_inc(f_loaded[s], 16)
            sp.dma_start(f_w2[:, s], w2[:, bass.ds(frow + c * FK, FK), :]).then_inc(f_loaded[s], 16)

        def for_layer(layer, expert, body):
            with sp.If(layer < 1):
                body(dense13, dense2, slice(0, KT), 0)
                sp.nop()
            with sp.Else():
                body(moe13, moe2, bass.ds(expert * KT, KT), expert * (NCH * FK))
                sp.nop()

        with sp.Fori(0, depth) as layer:
            load_x(layer, XH, x_loaded)
            sp.dma_start(g_row[:], attn_norm[bass.ds(layer, 1), :].partition_broadcast(P)).then_inc(grow_loaded, 16)
            for j, (col, w, _, _) in enumerate(W_IN):
                if j >= 2:
                    sp.wait_ge(w_lo_done, j - 1)
                sp.dma_start(w_raw[:, j % 2, :, 0:w], w_in_v[:, bass.ds(layer * KT, KT), col:col + w]).then_inc(
                    wraw_loaded[j % 2], 16)
                if j == 0:
                    small = [
                        (stack[R_CW:R_CB, :], cw_v[bass.ds(layer * 24, 24), :]),
                        (stack[R_CB:R_QN, :], cb_v[bass.ds(layer * 6, 6), :]),
                        (stack[R_QN:R_KN, 0:HD], nsa_q_norm[bass.ds(layer, 1), :]),
                        (stack[R_KN:R_QF, 0:HD], nsa_k_norm[bass.ds(layer, 1), :]),
                        (stack[R_QF:R_KF, 0:HD], fox_q_norm[bass.ds(layer, 1), :]),
                        (stack[R_KF:R_PE, 0:HD], fox_k_norm[bass.ds(layer, 1), :]),
                        (stack[R_PE:NR, 0:HD], pk_v[bass.ds(layer * CMP_BLK, CMP_BLK), :]),
                        (stack[R_PE:NR, HD:P], pv_v[bass.ds(layer * CMP_BLK, CMP_BLK), :]),
                        (prow[:, 0:8], dt_bias[bass.ds(layer, 1), :].partition_broadcast(P)),
                        (prow[:, 8:16], a_log[bass.ds(layer, 1), :].partition_broadcast(P)),
                        (prow[:, 16:24], ssd_d[bass.ds(layer, 1), :].partition_broadcast(P)),
                        (prow[:, 24:28], fox_f_bias[bass.ds(layer, 1), :].partition_broadcast(P)),
                        (ssd_g[:], ssd_norm[bass.ds(layer, 1), :].partition_broadcast(P)),
                        (router_sb[:], router.rearrange("l (k p) n -> p (l k) n", p=P)),
                    ]
                    assert len(small) == N_PARAMS
                    sp.wait_ge(setup_done, 1)
                    for dst, src in small:
                        sp.dma_start(dst, src).then_inc(params_loaded, 16)
                    sp.dma_start(slot_v, empty_slot[:]).then_inc(router_loaded, 16)
            sp.wait_ge(unit_done, len(units))
            sp.dma_start(wcT[0:HD], w_ck_v[:, bass.ds(layer * CMP_BLK, CMP_BLK), :]).then_inc(wcmp_loaded, 16)
            sp.dma_start(wcT[HD:P], w_cv_v[:, bass.ds(layer * CMP_BLK, CMP_BLK), :]).then_inc(wcmp_loaded, 16)
            sp.wait_ge(h_ready, NT)
            sp.dma_start(g_row[:], ffn_norm[bass.ds(layer, 1), :].partition_broadcast(P)).then_inc(grow_loaded, 16)
            for n in range(NW_OUT):
                j = NW_IN + n
                sp.wait_ge(w_lo_done, max(j - 1, NW_IN))
                sp.dma_start(wo_raw[:, j % 2], w_out_v[:, bass.ds(layer * KT, KT), n * WO_N:(n + 1) * WO_N]
                             ).then_inc(wraw_loaded[j % 2], 16)
                if n == 1:
                    sp.wait_ge(mixed, 9)
                    load_x(layer, x_new, x_again)
            sp.wait_ge(res_added, NW_OUT * NT)
            for t in range(NT):
                sp.dma_start(x_rows(t, out), x_new[:, t, :]).then_inc(stored, 16)
            sp.wait_ge(h_ready, 2 * NT)
            for t in range(NT):
                sp.dma_start(x_rows(t, h_rows), XH[:, t, :]).then_inc(stored, 16)
            sp.wait_ge(stored, 2 * NT * 16)
            sp.wait_ge(dest_ready, 1)
            if do_ffn:
              def expert_of(i):
                  return sp.value_load(item[0:1, 1, bass.ds(i, 1)], min_val=0, max_val=NE - 1)

              for_layer(layer, expert_of(0), lambda w13, w2, krow, frow: load_ffn(w13, w2, None, 0, 0, krow, frow))
              with sp.Fori(0, (layer * (MOE_ITEMS - DENSE_ITEMS) + DENSE_ITEMS) // 2) as pair:
                for odd in range(2):
                  tokens = sp.value_load(item[0:1, 2, bass.ds(pair * 2 + odd, 1)], min_val=0, max_val=SEQ)
                  with sp.If(tokens > 0):
                    def chunks(w13, w2, krow, frow):
                        n = pair * PAIR + odd * NCH
                        load_ffn(w13, w2, n + 1, 1, (odd + 1) % 2, krow, frow)
                        with sp.Fori(1, NCH // 2) as two:
                            load_ffn(w13, w2, n + two * 2, two * 2, odd, krow, frow)
                            load_ffn(w13, w2, n + two * 2 + 1, two * 2 + 1, 1 - odd, krow, frow)
                        load_ffn(w13, w2, n + NCH - 1, NCH - 1, odd, krow, frow)

                    def chunk_0(w13, w2, krow, frow):
                        load_ffn(w13, w2, pair * PAIR + (odd + 1) * NCH, 0, 1 - odd, krow, frow)

                    for_layer(layer, expert_of(pair * 2 + odd), chunks)
                    for_layer(layer, expert_of(pair * 2 + odd + 1), chunk_0)
                    sp.nop()
                  sp.nop()
            sp.wait_ge(layer_done, (layer + 1) * 4)
            sp.sem_inc(clearing, 1)
            sp.sem_clear(range(mix_sems[0].num, mix_sems[-1].num + 1))
            sp.sem_inc(layer_go, 1)

    @block.gpsimd
    def _(pool):
        def step(ins, count=[0]):
            count[0] += 1
            ins.then_inc(setup_dve, 1)
            pool.wait_ge(setup_dve, count[0])

        step(nc.gpsimd.memset(ones[:], 1.0))
        nc.gpsimd.affine_select(upper[:], ones[:], [[1, P]], ALU.is_ge, 0.0, base=0, channel_multiplier=-1)
        nc.gpsimd.affine_select(supper[:], ones[:], [[1, P]], ALU.is_gt, 0.0, base=0, channel_multiplier=-1)
        step(nc.gpsimd.affine_select(ident[:], ones[:], [[-1, P]], ALU.is_equal, 0.0, base=0, channel_multiplier=1))
        nc.gpsimd.tensor_copy(ident_b[:], ident[:])
        nc.gpsimd.memset(cmp_01[:], 1.0)
        step(nc.gpsimd.memset(causal_b[:], 0.0))
        step(nc.gpsimd.memset(causal_tb[:], 0.0))
        step(nc.gpsimd.memset(cmp_b[:], 0.0))
        nc.gpsimd.affine_select(causal_b[:], causal_b[:], [[-1, P]], ALU.is_ge, NEG, base=0, channel_multiplier=1)
        nc.gpsimd.affine_select(causal_tb[:], causal_tb[:], [[1, P]], ALU.is_ge, NEG, base=0, channel_multiplier=-1)
        for dst, fill in ((cmp_b, NEG), (cmp_01, 0.0)):
            nc.gpsimd.affine_select(dst[:], dst[:], [[P, NT], [-CMP_STRIDE, 32]], ALU.is_ge, fill,
                                    base=1 - CMP_BLK, channel_multiplier=1)
        nc.gpsimd.memset(minus_half[:], -0.5)
        nc.gpsimd.memset(stack[:], 1.0)
        nc.gpsimd.memset(is_moe[:], 0.0)
        nc.gpsimd.memset(is_dense[:], 1.0)
        nc.gpsimd.memset(empty_slot[:].bitcast(F32), 0.0)
        nc.gpsimd.memset(member_before[:], 0.0)
        nc.gpsimd.memset(logf_before[:], 0.0)
        nc.gpsimd.iota(iota_i[:], [[1, NE]], base=0, channel_multiplier=0)
        nc.gpsimd.iota(seg_i[:, 0, :], [[1, NSEG]], base=0, channel_multiplier=0)
        nc.gpsimd.iota(seg_i[:, 1, :], [[1, NE], [0, HALVES]], base=0, channel_multiplier=0)
        step(nc.gpsimd.memset(seg_before[:], 1.0))
        nc.gpsimd.affine_select(seg_before[:], seg_before[:], [[1, NSEG], [-1, NSEG]], ALU.is_gt, 0.0, base=0,
                                channel_multiplier=0)
        for c in range(2):
            last = nc.gpsimd.iota(rows_i[:, c, :, 0], [[P, NT]], base=0, channel_multiplier=1)
        step(last)
        nc.gpsimd.iota(empty_slot[:, :, 0], [[0, SLOTS // P + NB]], base=BIG_ID, channel_multiplier=0)
        nc.gpsimd.tensor_copy(seg[:, 0:2, :], seg_i[:])
        step(nc.gpsimd.tensor_copy(iota_e[:], iota_i[:]))
        nc.gpsimd.tensor_scalar(seg[:, 2, :], seg[:, 0, :], float(NB), -float(SLOTS // P), ALU.mult, ALU.add)
        nc.gpsimd.tensor_scalar(iota_m[:], iota_e[:], -float(NE), None, ALU.add)
        nc.gpsimd.tensor_scalar(base_e[:], iota_e[:], float(SEQ), None, ALU.mult)
        for half in range(HALVES):
            nc.gpsimd.memset(base_p[:, :, half], float(half * NB * P))
        step(nc.gpsimd.tensor_scalar(e0[:], iota_e[:], 0.0, None, ALU.is_equal))
        nc.gpsimd.nop().then_inc(setup_done, 1)
        pool.dma_start(h_rows[0:P, 0:32], minus_half[:]).then_inc(y_added, 16)
        pool.wait_ge(y_added, 16)

        with pool.Fori(0, depth) as layer:
            n_step = [0]

            def link(ins):
                n_step[0] += 1
                ins.then_inc(pool_step, 1)
                pool.wait_ge(pool_step, n_step[0])

            def power(dst, src, n, wait, count, done, rows=P):
                pool.wait_ge(wait, count)
                nc.gpsimd.tensor_tensor(dst, src, minus_half[0:rows, 0:n], ALU.pow).then_inc(done, 1)

            power(rs_x[:], ss_x[:], NT, ms_ready, 1, rs_ready)
            pool.wait_ge(h_ready, NT)
            pool.wait_ge(proj_out, unit_of[3][-1] + 1)
            nc.gpsimd.tensor_tensor(sq_f, proj[:, :, O_QF:O_QF + 512], proj[:, :, O_QF:O_QF + 512],
                                    ALU.mult).then_inc(head_sq, 1)
            power(rs_f[:].rearrange("p t h -> p (t h)"), ss_f[:].rearrange("p t h -> p (t h)"), 32, head_ms, 1, head_rs)
            pool.wait_ge(proj_out, unit_of[5][-1] + 1)
            nc.gpsimd.tensor_tensor(sq_n[:, :, 0:256], proj[:, :, 0:256], proj[:, :, 0:256], ALU.mult)
            kvw = proj[:, :, C_KV + 128:C_KV + 384].rearrange("p t (a b) -> p t a b", a=2)[:, :, :, 0:HD]
            nc.gpsimd.tensor_tensor(sq_n[:, :, 256:384].rearrange("p t (a b) -> p t a b", a=2), kvw, kvw,
                                    ALU.mult).then_inc(head_sq, 1)
            power(rs_n[:].rearrange("p t h -> p (t h)"), ss_n[:].rearrange("p t h -> p (t h)"), 24, head_ms, 2, head_rs)
            pool.wait_ge(unit_done, len(units))
            nc.gpsimd.memset(c_src[:, :, 0, 2 * NF:NCR], 1.0)
            link(nc.gpsimd.memset(c_src[:, :, 1:1 + NF, 0:2 * NF], 0.0))
            for h in range(NF):
                for at in (h, NF + h):
                    nc.gpsimd.memset(c_src[:, :, 1 + h, at:at + 1], 1.0)
            nc.gpsimd.memset(c_q[:].bitcast(F32), 0.0)
            pool.wait_ge(w_lo_done, NW_IN)
            nc.gpsimd.memset(c_k[:].bitcast(F32), 0.0)
            nc.gpsimd.memset(kcT[:, :, NC:NC + 1].bitcast(F32), 0.0).then_inc(c_set, 1)
            for c in range(NT):
                xs_c = xs_tok[:, c, :].rearrange("p (h d) -> p h d", h=NS)

                def v(t):
                    return t[:].rearrange("p (h d) -> p h d", h=NS)
                if c == 0:
                    pool.wait_ge(soft_done, 1)
                    pool.wait_ge(decays_ready, 1)
                    pool.wait_ge(tr_out, NT + 1)
                else:
                    pool.wait_ge(ssd_scores, c)
                nc.gpsimd.tensor_tensor(u_dta[:], bc(upper[:].unsqueeze(1), NS, P), bc(dta[:, c, :].unsqueeze(2), NS, P),
                                        ALU.mult).then_inc(u_ready, 1)
                if c:
                    pool.wait_ge(ssd_y, c)
                    pool.wait_ge(y_gated, c)
                link(nc.gpsimd.tensor_tensor(v(xdt), xs_c, bc(dt_t[:, c, :].unsqueeze(2), NS, HD), ALU.mult))
                nc.gpsimd.tensor_tensor(v(xdtd), v(xdt), bc(e_end[:, c, :].unsqueeze(2), NS, HD), ALU.mult)
                nc.gpsimd.tensor_tensor(v(xs_d), xs_c, bc(prow[:, 16:24].unsqueeze(2), NS, HD), ALU.mult
                                        ).then_inc(xdt_ready, 1)
            power(rs_c[:], ss_c[:], 1, kc_ms, 1, kc_rs, NC)
            power(rs_y[:], ss_y[:], NT, y_ms, 1, y_rs)
            power(rs_x[:], ss_x[:], NT, ms_ready, 2, rs_ready)
            pool.wait_ge(router_loaded, 16)
            pool.wait_ge(dest_ready, 1)
            for c in range(2):
                for t in range(NT):
                    pool.indirect_dma_start(slot_rows, bass.IndirectOffsetOnAxis(dest_i[:, c, t:t + 1], 0),
                                            rows_i[:, c, t, :], None, bounds_check=SLOTS - 1, oob_is_err=False
                                            ).then_inc(scattered, 16)
            pool.wait_ge(stored, 2 * NT * 16)
            pool.wait_ge(scattered, (layer + 1) * (2 * NT * 16))
            pool.sem_inc(pool_past, 1)

            def fetch(i):
                n = layer * (DENSE_ITEMS + 1) + i + 1
                blk = pool.value_load(item[0:1, 0, bass.ds(i, 1)], min_val=0, max_val=SLOTS // P)
                pool.dma_start(slots_next[:], slot_v[:, bass.ds(blk, NB), :]).then_inc(slots_loaded, 16)
                pool.wait_ge(slots_loaded, n * 16)
                pool.sem_inc(pool_past, 1)
                for b in range(NB):
                    pool.indirect_dma_start(xblk[:, b, :], None, h_rows,
                                            bass.IndirectOffsetOnAxis(slots_next[:, b, 0:1], 0),
                                            bounds_check=SEQ - 1, oob_is_err=False).then_inc(x_gathered, 16)

            if do_ffn:
              link(nc.gpsimd.memset(xblk[:], 0.0))
              link(nc.gpsimd.memset(y_sb[:], 0.0))
              fetch(0)
              with pool.Fori(0, layer * (MOE_ITEMS - DENSE_ITEMS) + DENSE_ITEMS) as i:
                tokens = pool.value_load(item[0:1, 2, bass.ds(i, 1)], min_val=0, max_val=SEQ)
                with pool.If(tokens > 0):
                    pool.wait_ge(x_tr, (i + 1) * (KT // 2))
                    pool.wait_ge(slots_taken, i + 1)
                    pool.sem_inc(pool_past, 1)
                    fetch(i + 1)
                    for b in range(2):
                        pool.wait_ge(y_out[b], i + 1 + START)
                    pool.sem_inc(pool_past, 1)
                    for b in range(NB):
                        pool.indirect_dma_start(out, bass.IndirectOffsetOnAxis(slots[:, b, 0:1], 0), y_sb[:, b, :], None,
                                                bounds_check=SEQ - 1, oob_is_err=False, compute_op=ALU.add
                                                ).then_inc(y_added, 16)
                    pool.nop()
                pool.nop()
              items = pool.value_load(n_items[0:1, 0:1], min_val=1, max_val=MOE_ITEMS)
              pool.wait_ge(y_added, (layer * DENSE_ITEMS + items) * 32 + 16)
              pool.wait_ge(x_gathered, (layer * (DENSE_ITEMS + 1) + items + 1) * 32)
            pool.sem_inc(layer_done, 1)
            pool.wait_ge(layer_go, layer + 1)
            pool.nop()

    @block.tensor
    def _(pe):
        mm, tr = nc.tensor.matmul, nc.tensor.transpose

        def three(dst, ah, al, bh, bl, start, stop):
            mm(dst, ah, bh, start=start, stop=False)
            mm(dst, ah, bl, start=False, stop=False)
            return mm(dst, al, bh, start=False, stop=stop)

        pe.wait_ge(setup_done, 1)
        with pe.Fori(0, depth) as layer:
            n_xt, n_step = [0], [0]

            def finish(ins):
                n_step[0] += 1
                ins.then_inc(pe_step, 1)
                pe.wait_ge(pe_step, n_step[0])

            def transpose_tokens(src, read=xt_lo):
                for k in range(KT):
                    n = n_xt[0]
                    if n >= 2:
                        pe.wait_ge(read, n - 1)
                    for t in range(NT):
                        last = tr(bank[n % 2][:, t * P:(t + 1) * P], src[:, t, k * P:(k + 1) * P], ident[:])
                    last.then_inc(xt_done, 1)
                    n_xt[0] += 1

            pe.wait_ge(h_ready, NT)
            transpose_tokens(h_tok)
            pe.wait_ge(params_loaded, N_PARAMS * 16)
            tr(bank[7][:, 0:NR], stack[:], ident[0:NR, 0:NR]).then_inc(cols_t, 1)
            pe.wait_ge(xt_lo, KT)
            for u, (j, m, channels, off, w) in enumerate(units):
                s = j % 2
                if u == unit_of[j][0]:
                    pe.wait_ge(w_lo_done, j + 1)
                if u >= 4:
                    pe.wait_ge(proj_out, u - 3)
                b = bank[2 + u % 4]
                ms = slice(m * P, (m + 1) * P)
                for k in range(KT):
                    if channels:
                        last = three(b[:], w_hi[:, s, k, ms], w_lo[:, s, k, ms], hT_hi[:, k, :], hT_lo[:, k, :],
                                     k == 0, k == KT - 1)
                    else:
                        last = three(b[:, 0:w], hT_hi[:, k, ms], hT_lo[:, k, ms], w_hi[:, s, k, 0:w],
                                     w_lo[:, s, k, 0:w], k == 0, k == KT - 1)
                last.then_inc(unit_done, 1)
            pe.wait_ge(soft_done, 1)
            mm(bank[6][:, 0:32], upper[:], dta[:].rearrange("p t h -> p (t h)"), start=True, stop=True)
            mm(bank[6][:, 32:64], ones[:], dta[:].rearrange("p t h -> p (t h)"), start=True, stop=True)
            mm(bank[6][:, 64:80], upper[:], logf[:].rearrange("p t h -> p (t h)"), start=True, stop=False)
            mm(bank[6][:, 64:80], ones[:], logf_before[:].rearrange("p t h -> p (t h)"), start=False, stop=True
               ).then_inc(sums_done, 1)
            n_tr, n_lo = [0], [0]
            read_by = []

            def one_transpose(parts, with_lo=False):
                n = n_tr[0]
                if n >= 4:
                    pe.wait_ge(*read_by[n - 4])
                elif n == 2:
                    pe.wait_ge(proj_out, len(units))
                for dst, src, rows in parts(bank[n % 4]):
                    last = tr(dst, src, ident[0:rows, 0:rows])
                last.then_inc(tr_done, 1)
                n_tr[0] += 1
                n_lo[0] += with_lo
                read_by.append((tr_lo, n_lo[0]) if with_lo else (tr_out, n_tr[0]))

            tile = [slice(t * P, (t + 1) * P) for t in range(NT)]
            pe.wait_ge(silu_done, XM)
            for c in range(NT):
                one_transpose(lambda b: [(b[:, tile[m]], xcT[:, m, tile[c]], P) for m in range(4)])
            one_transpose(lambda b: [(b[:, tile[c]], xcT[:, 4, tile[c]], P) for c in range(NT)])
            pe.wait_ge(fox_ready, 1)
            for h in range(NF):
                for src in (qa, ka):
                    one_transpose(lambda b: [(b[0:HD, tile[t]], src[:, t, h, :], P) for t in range(NT)], True)
            pe.wait_ge(nsa_ready, 1)
            for h in range(6):
                one_transpose(lambda b: [(b[0:HD, tile[t]], qn[:, t, h, :], P) for t in range(NT)], True)
            one_transpose(lambda b: [(b[:, tile[t]], proj[:, t, C_KV:C_KV + P], P) for t in range(NT)])
            pe.wait_ge(c_ready, 1)
            for n in range(1 + NF):
                one_transpose(lambda b: [(b[0:NCR, tile[t]], c_src[:, t, n, :], P) for t in range(NT)])
            for sem_, count in read_by[-4:]:
                pe.wait_ge(sem_, count)

            for c in range(NT):
                pe.wait_ge(u_ready, c + 1)
                if c:
                    pe.wait_ge(ssd_m, c)
                for half in range(2):
                    mm(bank[2 + half][:], ones[:], u_dta[:, 4 * half:4 * half + 4, :], start=True, stop=False)
                    mm(bank[2 + half][:].rearrange("p (h l) -> p h l", h=4), ident_b[:],
                       bc(causal_tb[:].unsqueeze(1), 4, P), start=False, stop=True)
                for g in range(2):
                    gp = slice(g * HD, (g + 1) * HD)
                    last = mm(bank[4][:, g * P:(g + 1) * P], xcT[gp, 4, tile[c]], xcT[gp, 5, tile[c]],
                              start=True, stop=True)
                    if g == 0:
                        finish(last)
                last.then_inc(ssd_scores, 1)
                if c:
                    pe.wait_ge(state_ready, c)
                    for g in range(2):
                        gp = slice(g * HD, (g + 1) * HD)
                        last = mm(bank[5][:, g * 256:(g + 1) * 256], xcT[gp, 5, tile[c]], state[gp, :], start=True, stop=True)
                        if g == 0:
                            finish(last)
                pe.wait_ge(xdt_ready, c + 1)
                if c < NT - 1:
                    for g in range(2):
                        gp = slice(g * HD, (g + 1) * HD)
                        last = mm(bank[7][gp, 0:256], b_tok[:, c, gp], xdtd[:, g * 256:(g + 1) * 256],
                                  start=True, stop=True)
                    last.then_inc(ssd_new, 1)
                if c == 0:
                    pe.wait_ge(pe_added, 2)
                    pe.wait_ge(wcmp_loaded, 32)
                    pe.wait_ge(tr_out, len(read_by))
                for j in range(c * CMP_BLK // NT, (c + 1) * CMP_BLK // NT):
                    for kv in range(2):
                        rows = slice(kv * HD, (kv + 1) * HD)
                        late = j // CMP_STRIDE
                        last = mm(bank[kv][0:NC, 0:HD], kv_pe[rows, late, late:late + NC, j % CMP_STRIDE],
                                  wcT[rows, j, :], start=j == 0, stop=j == CMP_BLK - 1)
                if c == NT - 1:
                    last.then_inc(kc_done, 1)
                pe.wait_ge(ssd_m, c + 1)
                if c:
                    pe.wait_ge(y_gated, c)
                for h in range(NS):
                    last = mm(bank[6][:, h * HD:(h + 1) * HD], decay[:, h, :], xdt[:, h * HD:(h + 1) * HD],
                              start=True, stop=True)
                last.then_inc(ssd_y, 1)


            pe.wait_ge(tr_out, len(read_by))
            pe.wait_ge(tr_lo, 14)
            pe.wait_ge(kc_ms, 1)
            pe.wait_ge(y_gated, NT)

            def scores(u):
                g, i, h, keys, _, _ = att[u]
                n = (i + 1) * P
                b = bank[s_bank[u % 3]]
                q_, kh, kl = (q_f[:, h], kh_f[:, h], kl_f[:, h]) if keys is None else (
                    q_n[:, h], kh_n[:, keys - 4], kl_n[:, keys - 4])
                mm(b[:, 0:n], q_[:, tile[i]], kh[:, 0:n], start=True, stop=False)
                mm(b[:, 0:n], q_[:, tile[i]], kl[:, 0:n], start=False, stop=False)
                if keys is None:
                    mm(b[:, 0:n], c_q[:, tile[i]], c_k[:, h, 0:n], start=False, stop=False)
                mm(b[:, n - P:n], ident_b[:], causal_b[:], start=False, stop=True).then_inc(scores_done, 1)

            def turn(u):
                pe.wait_ge(exp_done, u + 1)
                for j in range(att[u][1] + 1):
                    last = tr(bank[2 + u % 2][:, tile[j]], prob[:, u % 3, tile[j]], ident[:])
                last.then_inc(pT_done, 1)

            def weigh(u):
                g, i, h, _, vcol, place_ = att[u]
                pe.wait_ge(pT_out_act if by_act[u] else pT_out_dve, nth_out[u])
                if u == first_of[g] and g >= 2:
                    pe.wait_ge(o_read, g - 1)
                for j in range(i + 1):
                    last = mm(bank[6 + g % 2][:, place_:place_ + HD], probT[:, u % 2, tile[j]],
                              proj[:, j, vcol:vcol + HD], start=j == 0, stop=j == i)
                last.then_inc(o_done, 1)

            def cmp_scores(i):
                if i == 0:
                    pe.wait_ge(kcT_lo, 1)
                else:
                    pe.wait_ge(o_read, NT + i)
                for h in range(NQ):
                    o_ = bank[4][:, 256 + 32 * h:256 + 32 * (h + 1)]
                    mm(o_, q_n[:, h, tile[i]], kcT[:, 0, :], start=True, stop=False)
                    mm(o_, q_n[:, h, tile[i]], kcT[:, 1, :], start=False, stop=False)
                    last = mm(o_, ident_b[:], cmp_b[:, i, :], start=False, stop=True)
                last.then_inc(c_scores, 1)

            def cmp_turn(i):
                pe.wait_ge(c_prob, i + 1)
                for h in range(NQ):
                    last = tr(bank[4][0:NC, tile[h]], p_cmp[:, h, 0:NC], ident[:])
                last.then_inc(cT_done, 1)

            def cmp_weigh(i):
                pe.wait_ge(cT_out, i + 1)
                for h in range(NQ):
                    last = mm(bank[4][:, h * HD:(h + 1) * HD], pT_cmp[:, h, :], vc[:], start=True, stop=True)
                last.then_inc(c_out, 1)

            for u in range(NU + 4):
                if u < NU:
                    scores(u)
                if 2 <= u < NU + 2:
                    turn(u - 2)
                if u == 6:
                    pe.wait_ge(kc_ready, 1)
                    tr(bank[4][0:HD, 0:NC], kc_n[:], ident[0:NC, 0:NC]).then_inc(kcT_done, 1)
                if 3 <= u < NU + 3:
                    weigh(u - 3)
                for i in range(NT):
                    at = u - first_of[NT + i]
                    if at == 4:
                        cmp_scores(i)
                    if at == 8:
                        cmp_turn(i)
                    if at == 10:
                        cmp_weigh(i)

            pe.wait_ge(mixed, 9)
            transpose_tokens(XH)
            pe.wait_ge(xt_lo, 2 * KT)
            for n in range(NW_OUT):
                j = NW_IN + n
                s = j % 2
                pe.wait_ge(w_lo_done, j + 1)
                for t in range(NT):
                    v = n * NT + t
                    if v >= 4:
                        pe.wait_ge(res_added, v - 3)
                    b = bank[2 + v % 4]
                    for k in range(KT):
                        last = three(b[:, 0:WO_N], hT_hi[:, k, tile[t]], hT_lo[:, k, tile[t]], w_hi[:, s, k, 0:WO_N],
                                     w_lo[:, s, k, 0:WO_N], k == 0, k == KT - 1)
                    last.then_inc(unit_done, 1)
            pe.wait_ge(h_ready, 2 * NT)
            transpose_tokens(XH, xt_hi)
            pe.wait_ge(xt_hi, 3 * KT)
            for t in range(NT):
                for k in range(KT):
                    last = mm(bank[2][:, t * NE:(t + 1) * NE], hT_f[:, k, tile[t]], router_sb[:, k, :],
                              start=k == 0, stop=k == KT - 1)
            last.then_inc(logits_done, 1)
            pe.wait_ge(routed, 1)
            flat = member[:].rearrange("p t e -> p (t e)")
            before = member_before[:].rearrange("p t e -> p (t e)")
            mm(bank[3][:, 0:32], supper[:], flat, start=True, stop=False)
            mm(bank[3][:, 0:32], ones[:], before[:, 0:32], start=False, stop=True)
            mm(bank[3][:, 32:40], ones[:], before[:, 32:40], start=True, stop=True).then_inc(ranks_done, 1)

            if do_ffn:
              pe.wait_ge(dest_ready, 1)
              for s_ in (f_used2, gT_done, *h13_done):
                  pe.sem_inc(s_, START)

              def turn_x(i, kk):
                  if kk == 0:
                      pe.wait_ge(x_gathered, (layer * (DENSE_ITEMS + 1) + i + 1) * 32)
                  if kk or not isinstance(i, int):
                      pe.wait_ge(x_lo, i * (KT // 2) + kk)
                  for k in range(2):
                      for b in range(NB):
                          at = (k * NB + b) * P
                          last = tr(bank[7][:, at:at + P], xblk[:, b, (2 * kk + k) * P:(2 * kk + k + 1) * P], ident[:])
                  last.then_inc(x_tr, 1)

              def work(pair, odd, nb):
                  i = pair * 2 + odd
                  base_n = pair * PAIR + odd * NCH

                  def up(s, b, ks):
                      for k in ks:
                          last = three(bank[4 + b][:], xT_hi[:, k, b, :], xT_lo[:, k, b, :],
                                       f_w13_hi[:, s, k, :, :], f_w13_lo[:, s, k, :, :], k == 0, k == KT - 1)
                      return last

                  def down(s, k, first_, last_):
                      for b in range(nb):
                          for half in range(2):
                              cs = slice(half * 512, (half + 1) * 512)
                              lst = three(bank[2 * b + half][:], gT_hi[:, b, k, :], gT_lo[:, b, k, :], f_w2_hi[:, s, k, cs],
                                          f_w2_lo[:, s, k, cs], first_ and k == 0, last_ and k == FK - 1)
                      return lst

                  def turn_g(n):
                      for b in range(nb):
                          pe.wait_ge(gu_ready[b], n + 1 + START)
                      for b in range(nb):
                          for k in range(FK):
                              at = (b * FK + k) * P
                              last = tr(bank[6][:, at:at + P], gate_up[:, b, k * P:(k + 1) * P], ident[:])
                      last.then_inc(gT_done, 1)

                  def chunk(c, s, first_=False, second=False, final=False):
                      n = base_n + c
                      if first_:
                          pe.wait_ge(x_lo, (i + 1) * (KT // 2))
                      pe.wait_ge(f_lo, n * 3 + 1 + START)
                      if not first_:
                          pe.wait_ge(gu_ready[0], n + START)
                      up(s, 0, range(0, KT // 2))
                      if not first_:
                          turn_g(n - 1)
                      pe.wait_ge(f_lo, n * 3 + 2 + START)
                      last = up(s, 0, range(KT // 2, KT))
                      last.then_inc(h13_done[0], 1)
                      if nb == 2:
                          if not first_:
                              pe.wait_ge(gu_ready[1], n + START)
                          up(s, 1, range(KT)).then_inc(h13_done[1], 1)
                      if final:
                          turn_x(i + 1, 0)
                      if not first_:
                          pe.wait_ge(gT_lo_done, n)
                          if second:
                              for b in range(2):
                                  pe.wait_ge(y_out[b], i + START)
                          pe.wait_ge(f_lo, n * 3 + START)
                          down(1 - s, 0, second, False)
                          down(1 - s, 1, second, False).then_inc(f_used2, 1)

                  chunk(0, odd, first_=True)
                  chunk(1, 1 - odd, second=True)
                  with pe.Fori(1, NCH // 2) as two:
                      chunk(two * 2, odd)
                      chunk(two * 2 + 1, 1 - odd)
                  chunk(NCH - 1, odd, final=True)
                  n = base_n + NCH - 1
                  turn_x(i + 1, 1)
                  turn_g(n)
                  turn_x(i + 1, 2)
                  pe.wait_ge(gT_lo_done, n + 1)
                  pe.wait_ge(f_lo, n * 3 + 3 + START)
                  down(odd, 0, False, True)
                  turn_x(i + 1, 3)
                  down(odd, 1, False, True).then_inc(f_used2, 1)
                  if nb == 1:
                      pe.sem_inc(h13_done[1], NCH)
                  pe.nop()

              for kk in range(KT // 2):
                  turn_x(0, kk)
              with pe.Fori(0, (layer * (MOE_ITEMS - DENSE_ITEMS) + DENSE_ITEMS) // 2) as pair:
                for odd in range(2):
                  tokens = pe.value_load(item[0:1, 2, bass.ds(pair * 2 + odd, 1)], min_val=0, max_val=SEQ)
                  with pe.If(tokens > P):
                      work(pair, odd, 2)
                  with pe.Else():
                      with pe.If(tokens > 0):
                          work(pair, odd, 1)
                      pe.nop()
                  pe.nop()
            pe.sem_inc(layer_done, 1)
            pe.wait_ge(layer_go, layer + 1)
            pe.nop()

    @block.scalar
    def _(act):
        fn = nc.scalar.activation

        act.wait_ge(setup_done, 1)
        with act.Fori(0, depth) as layer:
            n_xt = [0]

            def heads(dst):
                for k in range(KT):
                    n = n_xt[0]
                    act.wait_ge(xt_done, n + 1)
                    fn(dst[:, k, :], bank[n % 2][:], ACT.Copy).then_inc(xt_hi, 1)
                    n_xt[0] += 1

            def split_hi(j):
                s = j % 2
                w = W_IN[j][1] if j < NW_IN else WO_N
                act.wait_ge(wraw_loaded[s], (j // 2 + 1) * 16)
                if NW_IN <= j < NW_IN + 2:
                    act.wait_ge(mixed, 9)
                elif j >= NW_IN + 2:
                    act.wait_ge(unit_done, len(units) + (j - NW_IN - 1) * NT)
                elif j >= 2:
                    act.wait_ge(unit_done, unit_of[j - 2][-1] + 1)
                src = w_raw[:, s, :, 0:w] if j < NW_IN else wo_raw[:, s]
                fn(w_hi[:, s, :, 0:w], src, ACT.Copy).then_inc(w_hi_done, 1)

            def move_units(j):
                for u in unit_of[j]:
                    _, m, channels, off, w = units[u]
                    act.wait_ge(unit_done, u + 1)
                    if channels:
                        fn(xbcT[:, off + m, 3:3 + SEQ], bank[2 + u % 4][:], ACT.Copy).then_inc(proj_out, 1)
                    else:
                        fn(proj[:, m, off:off + w], bank[2 + u % 4][:, 0:w], ACT.Copy).then_inc(proj_out, 1)

            for t in range(NT):
                act.wait_ge(x_loaded[t], 16)
                fn(h_tok[:, t, :], XH[:, t, :], ACT.Square, accum_out=ss_x[:, t:t + 1]).then_inc(x_squared, 1)
            split_hi(0)
            split_hi(1)
            heads(hT_hi)
            move_units(0)
            split_hi(2)
            move_units(1)
            split_hi(3)
            for m in range(XM):
                act.wait_ge(conv_done, m + 1)
                fn(xcT[:, m, :], xcT[:, m, :], ACT.Silu).then_inc(silu_done, 1)
            move_units(2)
            split_hi(4)
            move_units(3)
            split_hi(5)
            act.wait_ge(params_loaded, N_PARAMS * 16)
            act.wait_ge(soft_in, 1)
            fn(neg_a[:], prow[:, 8:16], ACT.Exp).then_inc(soft_exp, 1)
            fn(e12[:], g12[:], ACT.Exp).then_inc(soft_exp, 1)
            act.wait_ge(soft_exp, 2)
            fn(e12[:], e12[:], ACT.Ln, bias=1.0).then_inc(soft_ln, 1)
            move_units(4)
            split_hi(6)
            move_units(5)
            move_units(6)
            n_tr = [0]

            def take(dst, rows):
                n = n_tr[0]
                act.wait_ge(tr_done, n + 1)
                fn(dst, bank[n % 4][0:rows, :], ACT.Copy).then_inc(tr_out, 1)
                n_tr[0] += 1

            def take_head(dst, gain, both):
                n = n_tr[0]
                act.wait_ge(tr_done, n + 1)
                if both:
                    fn(dst[HD:P], bank[n % 4][0:HD, :], ACT.Copy, scale=gain[0:HD])
                fn(dst[0:HD], bank[n % 4][0:HD, :], ACT.Copy, scale=gain[0:HD]).then_inc(tr_out, 1)
                n_tr[0] += 1

            for c in range(NT):
                take(xs_tok[:, c, :], P)
            take(b_tok[:].rearrange("p t n -> p (t n)"), P)
            act.wait_ge(acs_ready, 1)
            fn(c_hi[:], c_t[:], ACT.Copy)
            fn(e_acs[:], acs[:], ACT.Exp)
            fn(e_end[:], to_end[:], ACT.Exp)
            fn(e_tot[:].rearrange("p t h -> p (t h)"), bank[6][:, 32:64], ACT.Exp).then_inc(decays_ready, 1)
            act.wait_ge(cols_ready, 1)
            for h in range(NF):
                take_head(q_f[:, h, :], qcol[:, 1:2], False)
                take_head(kh_f[:, h, :], cols[:, R_KF:R_KF + 1], True)
            for h in range(6):
                if h < NQ:
                    take_head(q_n[:, h, :], qcol[:, 0:1], False)
                else:
                    take_head(kh_n[:, h - NQ, :], cols[:, R_KN:R_KN + 1], True)
            take(kvT[:], P)
            act.wait_ge(c_set, 1)
            take(c_q[0:NCR], NCR)
            for h in range(NF):
                take(c_k[0:NCR, h, :], NCR)
            act.wait_ge(proj_out, len(units))
            fn(proj[:, :, z_col], proj[:, :, z_col], ACT.Silu).then_inc(z_ready, 1)

            def square_y(c):
                act.wait_ge(y_gated, c + 1)
                if c:
                    act.wait_ge(y_squared, c)
                fn(y_sq[:], XH[:, c, 256:768], ACT.Square, accum_out=ss_y[:, c:c + 1]).then_inc(y_squared, 1)

            for c in range(NT):
                act.wait_ge(ssd_diff, c + 1)
                fn(decay[:], decay[:], ACT.Exp).then_inc(ssd_exp, 1)
                if c:
                    square_y(c - 1)
            square_y(NT - 1)
            act.wait_ge(y_squared, NT)
            fn(gate_e[:], proj[:, :, C_G:C_G + 12], ACT.Exp, scale=-1.0).then_inc(gate_exp, 1)
            def exps(u):
                g, i, h, keys, _, _ = att[u]
                n = (i + 1) * P
                act.wait_ge(max_ready, u + 1)
                if u >= 3:
                    act.wait_ge(pT_done, u - 2)
                total = sum_f[:, i, h:h + 1] if keys is None else sum_n[:, i, h, keys - 3:keys - 2]
                fn(prob[:, u % 3, 0:n], bank[s_bank[u % 3]][:, 0:n], ACT.Exp, bias=neg_max[:, u % 8:u % 8 + 1],
                   accum_out=total).then_inc(exp_done, 1)

            for u in range(NU + 4):
                if u < NU:
                    exps(u)
                if u == 8:
                    act.wait_ge(kcT_done, 1)
                    for rows in (slice(HD, P), slice(0, HD)):
                        last = fn(kcT[rows, 0, 0:NC], bank[4][0:HD, 0:NC], ACT.Copy, scale=cols[0:HD, R_KN:R_KN + 1])
                    last.then_inc(kcT_out, 1)
                v = u - 2
                if 0 <= v < NU and by_act[v]:
                    n = (att[v][1] + 1) * P
                    act.wait_ge(pT_done, v + 1)
                    if v >= 2:
                        act.wait_ge(o_done, v - 1)
                    fn(probT[:, v % 2, 0:n], bank[2 + v % 2][:, 0:n], ACT.Copy).then_inc(pT_out_act, 1)
                for i in range(NT):
                    at = u - first_of[NT + i]
                    if at == 6:
                        act.wait_ge(c_shift, i + 1)
                        fn(p_cmp[:, :, 0:NC], p_cmp[:, :, 0:NC], ACT.Exp).then_inc(c_exp, 1)
                    if at == 9:
                        act.wait_ge(cT_done, i + 1)
                        if i:
                            act.wait_ge(c_out, i)
                        fn(pT_cmp[:].rearrange("c h q -> c (h q)"), bank[4][0:NC, :], ACT.Copy).then_inc(cT_out, 1)

            split_hi(NW_IN)
            heads(hT_hi)
            split_hi(NW_IN + 1)
            split_hi(NW_IN + 2)
            split_hi(NW_IN + 3)
            for t in range(NT):
                act.wait_ge(res_added, (NW_OUT - 1) * NT + t + 1)
                fn(XH[:, t, :], x_new[:, t, :], ACT.Square, accum_out=ss_x[:, t:t + 1]).then_inc(x_squared, 1)
            heads(hT_f)
            act.wait_ge(gate_diff, 1)
            fn(gates[:, :, 1], gates[:, :, 0], ACT.Exp).then_inc(gate_e2, 1)

            if do_ffn:
              act.wait_ge(dest_ready, 1)
              act.sem_inc(y_out[0], START)

              def split(n, which, s, parts, nb=0):
                  for part in parts:
                      if part == 0:
                          act.wait_ge(f_loaded[s], (which + 1) * 48)
                          if not isinstance(n, int):
                              act.wait_ge(h13_done[nb - 1], n - 1 + START)
                      if part == 2:
                          if not isinstance(n, int):
                              act.wait_ge(f_used2, n - 1 + START)
                          fn(f_w2_hi[:, s], f_w2[:, s], ACT.Copy).then_inc(f_hi, 1)
                      else:
                          ks = slice(part * KT // 2, (part + 1) * KT // 2)
                          fn(f_w13_hi[:, s, ks].rearrange("p k a n -> p (k a n)"),
                             f_w13[:, s, ks].rearrange("p k a n -> p (k a n)"), ACT.Copy).then_inc(f_hi, 1)

              def heads_x(i, kk):
                  act.wait_ge(x_tr, i * (KT // 2) + kk + 1)
                  fn(xT_hi[:, 2 * kk:2 * kk + 2].rearrange("p k b q -> p (k b q)"), bank[7][:], ACT.Copy
                     ).then_inc(x_hi, 1)

              def work(pair, odd, nb):
                  i = pair * 2 + odd
                  base_n = pair * PAIR + odd * NCH

                  def turned(n):
                      act.wait_ge(gT_done, n + 1 + START)
                      act.wait_ge(f_used2, n + START)
                      fn(gT_hi[:, 0:nb].rearrange("p b k q -> p (b k q)"), bank[6][:, 0:nb * FFC], ACT.Copy
                         ).then_inc(gT_hi_done, 1)

                  def silu_of(n, b):
                      act.wait_ge(h13_done[b], n + 1 + START)
                      act.wait_ge(gu_ready[b], n + START)
                      fn(silu[:, b, :], bank[4 + b][:, 0:FFC], ACT.Silu).then_inc(silu_out[b], 1)

                  def chunk(c, s, which, final=False):
                      n = base_n + c
                      if not isinstance(c, int) or c:
                          turned(n - 1)
                      split(n + 1, which, 1 - s, (0,), nb)
                      silu_of(n, 0)
                      split(n + 1, which, 1 - s, (1,))
                      if nb == 2:
                          silu_of(n, 1)
                      if not final:
                          split(n + 1, which, 1 - s, (2,))

                  def slot_count(c):
                      return pair * NCH + (odd * NCH + c) // 2

                  chunk(0, odd, slot_count(1))
                  chunk(1, 1 - odd, slot_count(2))
                  with act.Fori(1, NCH // 2) as two:
                      chunk(two * 2, odd, slot_count(1) + two)
                      chunk(two * 2 + 1, 1 - odd, slot_count(2) + two)
                  chunk(NCH - 1, odd, slot_count(NCH), final=True)
                  n = base_n + NCH - 1
                  heads_x(i + 1, 0)
                  heads_x(i + 1, 1)
                  turned(n)
                  heads_x(i + 1, 2)
                  heads_x(i + 1, 3)
                  split(n + 1, slot_count(NCH), 1 - odd, (2,))
                  act.wait_ge(f_used2, n + 1 + START)
                  act.wait_ge(y_added, (layer * DENSE_ITEMS + i) * 32 + 16)
                  act.wait_ge(slots_taken, i + 1)
                  for b in range(nb):
                      last = fn(y_sb[:, b, 0:512], bank[2 * b][:], ACT.Copy, scale=slots[:].bitcast(F32)[:, b, 1:2])
                  last.then_inc(y_out[0], 1)
                  if nb == 1:
                      act.sem_inc(silu_out[1], NCH)
                  act.nop()

              split(0, 0, 0, (0,))
              for kk in range(KT // 2):
                  heads_x(0, kk)
              split(0, 0, 0, (1, 2))
              with act.Fori(0, (layer * (MOE_ITEMS - DENSE_ITEMS) + DENSE_ITEMS) // 2) as pair:
                for odd in range(2):
                  tokens = act.value_load(item[0:1, 2, bass.ds(pair * 2 + odd, 1)], min_val=0, max_val=SEQ)
                  with act.If(tokens > P):
                      work(pair, odd, 2)
                  with act.Else():
                      with act.If(tokens > 0):
                          work(pair, odd, 1)
                      act.nop()
                  act.nop()
            act.sem_inc(layer_done, 1)
            act.wait_ge(layer_go, layer + 1)
            act.nop()

    @block.vector
    def _(dve):
        tt, ts, stt = nc.vector.tensor_tensor, nc.vector.tensor_scalar, nc.vector.scalar_tensor_tensor
        copy, total = nc.vector.tensor_copy, nc.vector.tensor_reduce

        dve.wait_ge(setup_done, 1)
        with dve.Fori(0, depth) as layer:
            n_step, n_xt = [0], [0]

            def link(ins):
                n_step[0] += 1
                ins.then_inc(dve_step, 1)
                dve.wait_ge(dve_step, n_step[0])

            def mean(ss, n, done):
                ts(ss, ss, 1.0 / n, EPS, ALU.mult, ALU.add).then_inc(done, 1)

            def remainders():
                for k in range(KT):
                    n = n_xt[0]
                    dve.wait_ge(xt_hi, n + 1)
                    tt(hT_lo[:, k, :], bank[n % 2][:], hT_hi[:, k, :].bitcast(F32), ALU.subtract).then_inc(xt_lo, 1)
                    n_xt[0] += 1

            def split_lo(j):
                s = j % 2
                w = W_IN[j][1] if j < NW_IN else WO_N
                dve.wait_ge(w_hi_done, j + 1)
                src = w_raw[:, s, :, 0:w] if j < NW_IN else wo_raw[:, s]
                tt(w_lo[:, s, :, 0:w], src, w_hi[:, s, :, 0:w].bitcast(F32), ALU.subtract
                   ).then_inc(w_lo_done, 1)

            def conv(m):
                dve.wait_ge(proj_out, m + 1)
                for tap in range(3, -1, -1):
                    w_ = cols[:, R_CW + tap * 6 + m:R_CW + tap * 6 + m + 1]
                    if tap == 3:
                        link(ts(xcT[:, m, :], xbcT[:, m, 3:3 + SEQ], w_, cols[:, R_CB + m:R_CB + m + 1], ALU.mult, ALU.add))
                    else:
                        ins = stt(xcT[:, m, :], xbcT[:, m, tap:tap + SEQ], w_, xcT[:, m, :], ALU.mult, ALU.add)
                        if tap:
                            link(ins)
                ins.then_inc(conv_done, 1)

            link(nc.vector.memset(xbcT[:, :, 0:3], 0.0))
            dve.wait_ge(x_squared, NT)
            mean(ss_x[:], DM, ms_ready)
            dve.wait_ge(rs_ready, 1)
            dve.wait_ge(grow_loaded, 16)
            for t in range(NT):
                dve.wait_ge(x_loaded[t], 16)
                stt(h_tok[:, t, :], XH[:, t, :], rs_x[:, t:t + 1], g_row[:], ALU.mult, ALU.mult).then_inc(h_ready, 1)
            split_lo(0)
            split_lo(1)
            remainders()
            dve.wait_ge(cols_t, 1)
            link(copy(cols[:], bank[7][:, 0:NR]))
            for n, row in enumerate((R_QN, R_QF)):
                last = ts(qcol[:, n:n + 1], cols[:, row:row + 1], HD ** -0.5, None, ALU.mult)
            last.then_inc(cols_ready, 1)
            split_lo(2)
            for m in range(3):
                conv(m)
            split_lo(3)
            for m in range(3, XM):
                conv(m)
            split_lo(4)
            dve.wait_ge(params_loaded, N_PARAMS * 16)
            dve.wait_ge(proj_out, unit_of[3][-1] + 1)
            tt(dt_t[:], proj[:, :, O_DT:O_DT + NS], bc(prow[:, 0:8].unsqueeze(1), NT, NS), ALU.add)
            link(tt(logf[:], proj[:, :, O_FF:O_FF + NF], bc(prow[:, 24:28].unsqueeze(1), NT, NF), ALU.add))
            stt(g12[:, :, 0:8], dt_t[:], -1.0, dt_t[:], ALU.mult, ALU.min)
            stt(g12[:, :, 8:12], logf[:], -1.0, logf[:], ALU.mult, ALU.min).then_inc(soft_in, 1)
            split_lo(5)
            dve.wait_ge(head_sq, 1)
            link(total(ss_f[:], sq_f.rearrange("p t (h d) -> p t h d", d=HD), AX.X, ALU.add))
            mean(ss_f[:], HD, head_ms)
            dve.wait_ge(soft_exp, 2)
            dve.wait_ge(soft_ln, 1)
            stt(dt_t[:], dt_t[:], 0.0, e12[:, :, 0:8], ALU.max, ALU.add)
            link(stt(logf[:], logf[:], 0.0, e12[:, :, 8:12], ALU.min, ALU.subtract))
            stt(dta[:], dt_t[:], -1.0, bc(neg_a[:].unsqueeze(1), NT, NS), ALU.mult, ALU.mult)
            link(copy(logf_before[:, 1, :], logf[:, 0, :]))
            link(tt(logf_before[:, 2, :], logf_before[:, 1, :], logf[:, 1, :], ALU.add))
            tt(logf_before[:, 3, :], logf_before[:, 2, :], logf[:, 2, :], ALU.add).then_inc(soft_done, 1)
            dve.wait_ge(head_rs, 1)
            for n, (dst, off) in enumerate(((qa, O_QF), (ka, O_KF))):
                for t in range(NT):
                    last = tt(dst[:, t], proj[:, t, off:off + 256].rearrange("p (h d) -> p h d", d=HD),
                              bc(rs_f[:, t, 4 * n:4 * n + 4].unsqueeze(2), NF, HD), ALU.mult)
            last.then_inc(fox_ready, 1)
            split_lo(6)
            dve.wait_ge(head_sq, 2)
            link(total(ss_n[:], sq_n.rearrange("p t (h d) -> p t h d", d=HD), AX.X, ALU.add))
            mean(ss_n[:], HD, head_ms)
            dve.wait_ge(sums_done, 1)
            flat_th = "p t h -> p (t h)"
            link(copy(acs[:].rearrange(flat_th), bank[6][:, 0:32]))
            copy(c_t[:].rearrange(flat_th), bank[6][:, 64:80])
            tt(to_end[:].rearrange(flat_th), bank[6][:, 32:64], acs[:].rearrange(flat_th), ALU.subtract
               ).then_inc(acs_ready, 1)
            dve.wait_ge(head_rs, 2)
            for t in range(NT):
                tt(qn[:, t, 0:4, :], proj[:, t, 0:256].rearrange("p (h d) -> p h d", d=HD),
                   bc(rs_n[:, t, 0:4].unsqueeze(2), 4, HD), ALU.mult)
            for n in range(2):
                kv_ = C_KV + P * (n + 1)
                last = tt(qn[:, :, 4 + n, :], proj[:, :, kv_:kv_ + HD], bc(rs_n[:, :, 4 + n].unsqueeze(2), NT, HD), ALU.mult)
            last.then_inc(nsa_ready, 1)
            dve.wait_ge(decays_ready, 1)
            dve.wait_ge(c_set, 1)
            c_h = c_hi[:].bitcast(F32)
            copy(c_src[:, :, 0, 0:NF], c_h)
            tt(c_src[:, :, 0, NF:2 * NF], c_t[:], c_h, ALU.subtract)
            ts(c_src[:, :, 1:1 + NF, 2 * NF], c_h, -1.0, None, ALU.mult)
            tt(c_src[:, :, 1:1 + NF, 2 * NF + 1], c_h, c_t[:], ALU.subtract).then_inc(c_ready, 1)

            n_take = [NT + 1]

            def take_lo(dst, src, gain, both):
                dve.wait_ge(tr_out, n_take[0] + 1)
                b = bank[n_take[0] % 4]
                if both:
                    link(stt(dst[0:HD], b[0:HD, :], gain[0:HD], src[0:HD].bitcast(F32), ALU.mult, ALU.subtract))
                    copy(dst[HD:P], dst[0:HD].bitcast(F32)).then_inc(tr_lo, 1)
                else:
                    stt(dst[HD:P], b[0:HD, :], gain[0:HD], src[0:HD].bitcast(F32), ALU.mult, ALU.subtract
                        ).then_inc(tr_lo, 1)
                n_take[0] += 1

            for h in range(NF):
                take_lo(q_f[:, h, :], q_f[:, h, :], qcol[:, 1:2], False)
                take_lo(kl_f[:, h, :], kh_f[:, h, :], cols[:, R_KF:R_KF + 1], True)
            for h in range(6):
                if h < NQ:
                    take_lo(q_n[:, h, :], q_n[:, h, :], qcol[:, 0:1], False)
                else:
                    take_lo(kl_n[:, h - NQ, :], kh_n[:, h - NQ, :], cols[:, R_KN:R_KN + 1], True)

            def by_head(ap):
                return ap.rearrange("p (h d) -> p h d", h=NS)

            dve.wait_ge(tr_out, 20)
            for v in range(2):
                at = R_PE + CMP_STRIDE * v
                tt(kv_pe[:, v], kvT[:].rearrange("p (b j) -> p b j", j=CMP_STRIDE),
                   bc(cols[:, at:at + CMP_STRIDE].unsqueeze(1), CMP_BLK, CMP_STRIDE), ALU.add).then_inc(pe_added, 1)
            for c in range(NT):
                dve.wait_ge(ssd_scores, c + 1)
                if c:
                    dve.wait_ge(ssd_y, c)
                for half in range(2):
                    hs = slice(4 * half, 4 * half + 4)
                    last = tt(decay[:, hs, :], bank[2 + half][:].rearrange("p (h l) -> p h l", h=4),
                              bc(acs[:, c, hs].unsqueeze(2), 4, P), ALU.subtract)
                last.then_inc(ssd_diff, 1)
                dve.wait_ge(ssd_exp, c + 1)
                for g in range(2):
                    hs = slice(4 * g, 4 * g + 4)
                    last = tt(decay[:, hs, :], decay[:, hs, :], bc(bank[4][:, g * P:(g + 1) * P].unsqueeze(1), 4, P),
                              ALU.mult)
                last.then_inc(ssd_m, 1)
                if c < NT - 1:
                    dve.wait_ge(ssd_new, c + 1)
                else:
                    dve.wait_ge(ssd_y, c + 1)
                if c:
                    link(tt(by_head(y_t[:]), by_head(bank[5][:]), bc(e_acs[:, c, :].unsqueeze(2), NS, HD), ALU.mult))
                if c < NT - 1:
                    if c == 0:
                        copy(state[:], bank[7][:, 0:256]).then_inc(state_ready, 1)
                    else:
                        for g in range(2):
                            gp = slice(g * HD, (g + 1) * HD)
                            e_ = e_tot[gp, c, 4 * g:4 * g + 4].unsqueeze(2).to_broadcast([HD, 4, HD])
                            last = tt(state[gp, :].rearrange("p (h d) -> p h d", h=4),
                                      state[gp, :].rearrange("p (h d) -> p h d", h=4), e_, ALU.mult)
                        link(last)
                        tt(state[:], state[:], bank[7][:, 0:256], ALU.add).then_inc(state_ready, 1)
                dve.wait_ge(xdt_ready, c + 1)
                dve.wait_ge(ssd_y, c + 1)
                if c:
                    link(tt(y_t[:], y_t[:], xs_d[:], ALU.add))
                    link(tt(y_t[:], bank[6][:], y_t[:], ALU.add))
                else:
                    link(tt(y_t[:], bank[6][:], xs_d[:], ALU.add))
                dve.wait_ge(z_ready, 1)
                tt(XH[:, c, 256:768], y_t[:], proj[:, c, z_col], ALU.mult).then_inc(y_gated, 1)
            dve.wait_ge(kc_done, 1)
            copy(vc[:], bank[1][0:NC, 0:HD])
            link(copy(kc_n[:], bank[0][0:NC, 0:HD]))
            link(tt(kc_sq[:], kc_n[:], kc_n[:], ALU.mult))
            link(total(ss_c[:], kc_sq[:], AX.X, ALU.add))
            mean(ss_c[:], HD, kc_ms)
            dve.wait_ge(y_squared, NT)
            mean(ss_y[:], 512, y_ms)
            def finalize(g):
                i = g % NT
                dve.wait_ge(o_done, last_of[g] + 1)
                b = bank[6 + g % 2]

                def heads_of(ap):
                    return ap.rearrange("p (h d) -> p h d", h=NQ)
                if g < NT:
                    link(ts(coef[:, :, 0], sum_f[:, i, :], TINY, None, ALU.max))
                    link(nc.vector.reciprocal(coef[:, :, 0], coef[:, :, 0]))
                    last = tt(heads_of(XH[:, i, 768:1024]), heads_of(b[:, 0:256]), bc(coef[:, :, 0].unsqueeze(2), NF, HD),
                              ALU.mult)
                else:
                    dve.wait_ge(c_out, i + 1)
                    link(ts(coef[:], sum_n[:, i], TINY, None, ALU.max))
                    link(nc.vector.reciprocal(coef[:], coef[:]))
                    link(tt(coef[:], coef[:], gate_e[:, i, :].rearrange("p (h b) -> p h b", b=3), ALU.mult))
                    for dst, src, br in ((o_acc[:], bank[4][:, 0:256], 0), (o_part[:], b[:, 0:256], 1)):
                        ins = tt(heads_of(dst), heads_of(src), bc(coef[:, :, br].unsqueeze(2), NQ, HD), ALU.mult)
                    link(ins)
                    link(tt(o_acc[:], o_acc[:], o_part[:], ALU.add))
                    link(tt(heads_of(o_part[:]), heads_of(b[:, 256:512]), bc(coef[:, :, 2].unsqueeze(2), NQ, HD), ALU.mult))
                    last = tt(XH[:, i, 0:256], o_acc[:], o_part[:], ALU.add)
                last.then_inc(o_read, 1)
                dve.wait_ge(o_read, g + 1)
                dve.sem_inc(mixed, 1)

            for u in range(NU + 5):
                if u < NU:
                    n = (att[u][1] + 1) * P
                    dve.wait_ge(scores_done, u + 1)
                    total(neg_max[:, u % 8:u % 8 + 1], bank[s_bank[u % 3]][:, 0:n], AX.X, ALU.max, negate=True
                          ).then_inc(max_ready, 1)
                if u == 4:
                    dve.wait_ge(kc_rs, 1)
                    ts(kc_n[:], kc_n[:], rs_c[:], None, ALU.mult).then_inc(kc_ready, 1)
                if u == 5:
                    dve.wait_ge(gate_exp, 1)
                    link(ts(gate_e[:], gate_e[:], 1.0, None, ALU.add))
                    link(nc.vector.reciprocal(gate_e[:], gate_e[:]))
                if u == 6:
                    dve.wait_ge(y_rs, 1)
                    for c in range(NT):
                        last = stt(XH[:, c, 256:768], XH[:, c, 256:768], rs_y[:, c:c + 1], ssd_g[:], ALU.mult, ALU.mult)
                    last.then_inc(mixed, 1)
                if u == 9:
                    dve.wait_ge(kcT_out, 1)
                    link(stt(kcT[0:HD, 1, 0:NC], bank[4][0:HD, 0:NC], cols[0:HD, R_KN:R_KN + 1],
                             kcT[0:HD, 0, 0:NC].bitcast(F32), ALU.mult, ALU.subtract))
                    copy(kcT[HD:P, 1, 0:NC], kcT[0:HD, 1, 0:NC].bitcast(F32)).then_inc(kcT_lo, 1)
                v = u - 2
                if 0 <= v < NU and not by_act[v]:
                    n = (att[v][1] + 1) * P
                    dve.wait_ge(pT_done, v + 1)
                    if v >= 2:
                        dve.wait_ge(o_done, v - 1)
                    copy(probT[:, v % 2, 0:n], bank[2 + v % 2][:, 0:n]).then_inc(pT_out_dve, 1)
                for i in range(NT):
                    at = u - first_of[NT + i]
                    s_c = bank[4][:, 256:384].rearrange("p (h c) -> p h c", h=NQ)[:, :, 0:NC]
                    pc = p_cmp[:, :, 0:NC]
                    if at == 5:
                        dve.wait_ge(c_scores, i + 1)
                        if i:
                            dve.wait_ge(cT_done, i)
                        link(total(neg_max_c[:], s_c, AX.X, ALU.max, negate=True))
                        tt(pc, s_c, bc(neg_max_c[:].unsqueeze(2), NQ, NC), ALU.add).then_inc(c_shift, 1)
                    if at == 7:
                        dve.wait_ge(c_exp, i + 1)
                        link(tt(pc, pc, bc(cmp_01[:, i, 0:NC].unsqueeze(1), NQ, NC), ALU.mult))
                        total(sum_n[:, i, :, 0], pc, AX.X, ALU.add).then_inc(c_prob, 1)
                for g in range(2 * NT):
                    if u == last_of[g] + 4:
                        finalize(g)

            split_lo(NW_IN)
            remainders()
            split_lo(NW_IN + 1)
            for n in range(NW_OUT):
                for t in range(NT):
                    v = n * NT + t
                    dve.wait_ge(unit_done, len(units) + v + 1)
                    if n == 0:
                        dve.wait_ge(x_again[t], 16)
                    cs = slice(n * WO_N, (n + 1) * WO_N)
                    tt(x_new[:, t, cs], x_new[:, t, cs], bank[2 + v % 4][:, 0:WO_N], ALU.add).then_inc(res_added, 1)
                if n < 2:
                    split_lo(NW_IN + 2 + n)
            dve.wait_ge(x_squared, 2 * NT)
            mean(ss_x[:], DM, ms_ready)
            dve.wait_ge(rs_ready, 2)
            dve.wait_ge(grow_loaded, 32)
            dve.wait_ge(xt_done, 2 * KT)
            for t in range(NT):
                stt(XH[:, t, :], x_new[:, t, :], rs_x[:, t:t + 1], g_row[:], ALU.mult, ALU.mult).then_inc(h_ready, 1)

            dve.wait_ge(logits_done, 1)
            copy(lg[:].rearrange("p t e -> p (t e)"), bank[2][:, 0:NT * NE])
            link(tt(e0_dense[:], e0[:], bc(is_dense[:], NE), ALU.mult))
            iota_b = bc(iota_m[:].unsqueeze(1), NT, NE)
            for c, oh in enumerate((oh1, oh2)):
                link(total(top_v[:, :, c], lg[:], AX.X, ALU.max))
                link(tt(eq[:], lg[:], bc(top_v[:, :, c].unsqueeze(2), NT, NE), ALU.is_equal))
                link(tt(eq[:], eq[:], iota_b, ALU.mult))
                link(total(first[:, :, c], eq[:], AX.X, ALU.min))
                link(tt(oh[:], iota_b, bc(first[:, :, c].unsqueeze(2), NT, NE), ALU.is_equal))
                if c == 0:
                    link(stt(lg[:], oh[:], -3e38, lg[:], ALU.mult, ALU.add))
            tt(gates[:, :, 0], top_v[:, :, 1], top_v[:, :, 0], ALU.subtract).then_inc(gate_diff, 1)
            link(ts(oh1[:], oh1[:], is_moe[:], None, ALU.mult))
            link(tt(oh1[:], oh1[:], bc(e0_dense[:].unsqueeze(1), NT, NE), ALU.add))
            link(ts(oh2[:], oh2[:], is_moe[:], None, ALU.mult))
            link(tt(member[:], oh1[:], oh2[:], ALU.add))
            for t in range(NT):
                link(tt(member_before[:, t + 1, :], member_before[:, t, :], member[:, t, :], ALU.add))
            dve.sem_inc(routed, 1)
            dve.wait_ge(gate_e2, 1)
            link(ts(gates[:, :, 0], gates[:, :, 1], 1.0, None, ALU.add))
            link(nc.vector.reciprocal(gates[:, :, 0], gates[:, :, 0]))
            link(tt(gates[:, :, 1], gates[:, :, 1], gates[:, :, 0], ALU.mult))
            link(ts(gates[:], gates[:], is_moe[:], None, ALU.mult))
            link(ts(gates[:, :, 0], gates[:, :, 0], is_dense[:], None, ALU.add))
            for c in range(2):
                copy(rows_i[:].bitcast(F32)[:, c, :, 1], gates[:, :, c])
            dve.wait_ge(ranks_done, 1)
            link(tt(place_e[:], bank[3][:, 0:NT * NE].rearrange("p (t e) -> p t e", e=NE),
                    bc(base_e[:].unsqueeze(1), NT, NE), ALU.add))
            for c, oh in enumerate((oh1, oh2)):
                link(tt(eq[:], place_e[:], oh[:], ALU.mult))
                link(total(dest[:, :, c], eq[:], AX.X, ALU.add))
            link(stt(dest[:, :, 1], bc(is_dense[:], NT), float(BIG_ID), dest[:, :, 1], ALU.mult, ALU.add))
            copy(dest_i[:].rearrange("p c t -> p t c"), dest[:])
            link(tt(left[:], bc(bank[3][:, 32:40].unsqueeze(2), NE, 2), base_p[:], ALU.subtract))
            link(ts(left[:], left[:], 0.0, None, ALU.max))
            left_s = left[:].rearrange("p e h -> p (e h)")

            def along_items(ap):
                return bc(ap.unsqueeze(1), NSEG, NSEG)

            link(ts(has[:], left_s, 0.0, None, ALU.is_gt))
            link(total(count_f[:], has[:], AX.X, ALU.add))
            copy(n_items[:], count_f[:])
            link(tt(sel_v[:], seg_before[:], along_items(has[:]), ALU.mult))
            link(total(pos[:], sel_v[:], AX.X, ALU.add))
            link(tt(sel[:], along_items(pos[:]), bc(seg[:, 0, :].unsqueeze(2), NSEG, NSEG), ALU.is_equal))
            link(tt(sel[:], sel[:], along_items(has[:]), ALU.mult))
            for n, value in enumerate((seg[:, 2, :], seg[:, 1, :], left_s)):
                link(tt(sel_v[:], sel[:], along_items(value), ALU.mult))
                link(total(item_f[:, n, :], sel_v[:], AX.X, ALU.add))
            link(ts(item_f[:, 0, :], item_f[:, 0, :], float(SLOTS // P), None, ALU.add))
            copy(item[:], item_f[:]).then_inc(dest_ready, 1)

            if do_ffn:
              dve.wait_ge(dest_ready, 1)
              for s_ in (f_lo, *gu_ready, y_out[1]):
                  dve.sem_inc(s_, START)

              def split(n, s, parts):
                  for part in parts:
                      dve.wait_ge(f_hi, n * 3 + part + 1)
                      if part == 2:
                          tt(f_w2_lo[:, s], f_w2[:, s], f_w2_hi[:, s].bitcast(F32), ALU.subtract).then_inc(f_lo, 1)
                      else:
                          ks = slice(part * KT // 2, (part + 1) * KT // 2)
                          flat = "p k a n -> p (k a n)"
                          tt(f_w13_lo[:, s, ks].rearrange(flat), f_w13[:, s, ks].rearrange(flat),
                             f_w13_hi[:, s, ks].bitcast(F32).rearrange(flat), ALU.subtract).then_inc(f_lo, 1)

              def remainders_x(i, kk):
                  dve.wait_ge(x_hi, i * (KT // 2) + kk + 1)
                  tt(xT_lo[:, 2 * kk:2 * kk + 2].rearrange("p k b q -> p (k b q)"), bank[7][:],
                     xT_hi[:, 2 * kk:2 * kk + 2].bitcast(F32).rearrange("p k b q -> p (k b q)"), ALU.subtract
                     ).then_inc(x_lo, 1)

              def work(pair, odd, nb):
                  i = pair * 2 + odd
                  base_n = pair * PAIR + odd * NCH

                  def turned(n):
                      dve.wait_ge(gT_hi_done, n + 1)
                      tt(gT_lo[:, 0:nb].rearrange("p b k q -> p (b k q)"), bank[6][:, 0:nb * FFC],
                         gT_hi[:, 0:nb].bitcast(F32).rearrange("p b k q -> p (b k q)"), ALU.subtract
                         ).then_inc(gT_lo_done, 1)

                  def gate(n, b):
                      dve.wait_ge(silu_out[b], n + 1)
                      dve.wait_ge(gT_done, n + START)
                      tt(gate_up[:, b, :], silu[:, b, :], bank[4 + b][:, FFC:2 * FFC], ALU.mult).then_inc(gu_ready[b], 1)

                  def chunk(c, s, final=False):
                      n = base_n + c
                      if not isinstance(c, int) or c:
                          turned(n - 1)
                      split(n + 1, 1 - s, (0,))
                      gate(n, 0)
                      split(n + 1, 1 - s, (1,))
                      if nb == 2:
                          gate(n, 1)
                      if not final:
                          split(n + 1, 1 - s, (2,))

                  chunk(0, odd)
                  chunk(1, 1 - odd)
                  dve.wait_ge(slots_loaded, (layer * (DENSE_ITEMS + 1) + i + 1) * 16)
                  dve.wait_ge(y_added, (layer * DENSE_ITEMS + i) * 32 + 16)
                  copy(slots[:], slots_next[:]).then_inc(slots_taken, 1)
                  with dve.Fori(1, NCH // 2) as two:
                      chunk(two * 2, odd)
                      chunk(two * 2 + 1, 1 - odd)
                  chunk(NCH - 1, odd, final=True)
                  n = base_n + NCH - 1
                  remainders_x(i + 1, 0)
                  remainders_x(i + 1, 1)
                  turned(n)
                  remainders_x(i + 1, 2)
                  remainders_x(i + 1, 3)
                  split(n + 1, 1 - odd, (2,))
                  dve.wait_ge(f_used2, n + 1 + START)
                  for b in range(nb):
                      last = ts(y_sb[:, b, 512:DM], bank[2 * b + 1][:], slots[:].bitcast(F32)[:, b, 1:2], None, ALU.mult)
                  last.then_inc(y_out[1], 1)
                  if nb == 1:
                      dve.sem_inc(gu_ready[1], NCH)
                  dve.nop()

              split(0, 0, (0,))
              for kk in range(KT // 2):
                  remainders_x(0, kk)
              split(0, 0, (1, 2))
              with dve.Fori(0, (layer * (MOE_ITEMS - DENSE_ITEMS) + DENSE_ITEMS) // 2) as pair:
                for odd in range(2):
                  tokens = dve.value_load(item[0:1, 2, bass.ds(pair * 2 + odd, 1)], min_val=0, max_val=SEQ)
                  with dve.If(tokens > P):
                      work(pair, odd, 2)
                  with dve.Else():
                      with dve.If(tokens > 0):
                          work(pair, odd, 1)
                      dve.nop()
                  dve.nop()
            nc.vector.memset(is_moe[:], 1.0)
            link(nc.vector.memset(is_dense[:], 0.0))
            dve.sem_inc(layer_done, 1)
            dve.wait_ge(layer_go, layer + 1)
            dve.nop()

    block_cm.__exit__(None, None, None)


_INS = ['x', 'attn_norm', 'w_in', 'nsa_q_norm', 'nsa_k_norm', 'nsa_cmp_pe_k', 'nsa_cmp_pe_v', 'nsa_cmp_w_k',
        'nsa_cmp_w_v', 'ssd_conv_w', 'ssd_conv_b', 'ssd_dt_bias', 'ssd_a_log', 'ssd_d', 'ssd_norm', 'fox_q_norm',
        'fox_k_norm', 'fox_f_bias', 'w_out', 'ffn_norm', 'ffn_w1', 'ffn_w3', 'ffn_w2', 'moe_router', 'moe_w1',
        'moe_w3', 'moe_w2']


def kernel(**inputs):
    import numpy as _np
    import concourse.bacc as _bacc
    from concourse import mybir as _mybir
    from concourse.bass_utils import run_bass_kernel_spmd as _run

    nc = _bacc.Bacc("TRN2", target_bir_lowering=False, num_devices=1)
    arrays, args = {}, []
    for name in _INS:
        a = _np.ascontiguousarray(inputs[name])
        if name == 'x':
            a = a.reshape(SEQ, DM)
        arrays[f"in_{name}_dram"] = a
        args.append(nc.dram_tensor(f"in_{name}_dram", a.shape, _mybir.dt.from_np(a.dtype), kind="ExternalInput").ap())
    args.append(nc.dram_tensor("out_0_dram", (SEQ, DM), _mybir.dt.float32, kind="ExternalOutput").ap())
    build_program(nc, *args)
    r = _run(nc, [arrays], core_ids=[0])
    return r.results[0]["out_0_dram"].reshape(1, SEQ, DM)
```

```python
import concourse.bass as bass
from concourse import mybir
from concourse.alu_op_type import AluOpType as ALU

F32 = mybir.dt.float32
F32R = mybir.dt.float32r
BF16 = mybir.dt.bfloat16
I32 = mybir.dt.int32
ACT = mybir.ActivationFunctionType
AX = mybir.AxisListType

P = 128
DEPTH = 2
SEQ = 512
DM = 1024
NT = SEQ // P
KT = DM // P
HD = 64
NQ = 4
NF = 4
NS = 8
D_IN = 2712
D_FF = 2816
NE = 8
CMP_BLK, CMP_STRIDE = 32, 16
NC = (SEQ - CMP_BLK) // CMP_STRIDE + 1
EPS = 1e-6
TINY = 1.1754943508222875e-38
NEG = -1e30
BIG_ID = 1 << 20

C_Q, C_KV, C_G, C_Z, C_XBC, C_DT = 0, 256, 640, 652, 1164, 1932
N_XBC = 768
N_TOK = D_IN - N_XBC
O_DT = C_XBC
O_QF = O_DT + NS
O_KF = O_QF + 256
O_VF = O_KF + 256
O_FF = O_VF + 256
W_IN = [(C_XBC, 384, True, 0), (C_XBC + 384, 384, True, 3),
        (C_DT, 390, False, O_DT), (C_DT + 390, 390, False, O_DT + 390),
        (0, 388, False, 0), (388, 388, False, 388), (776, 388, False, 776)]
NW_IN = len(W_IN)
WO_N = 256
NW_OUT = DM // WO_N
WBUF = 392
XM = N_XBC // P
W0_POOL = KT // 2
TURNS = [(t, half) for t in range(NT) for half in range(2)]

FFC = 256
NCH = D_FF // FFC
FK = FFC // P
NB = 2
HALVES = SEQ // (NB * P)
NSEG = NE * HALVES
DENSE_ITEMS = HALVES
MOE_ITEMS = 12
assert MOE_ITEMS >= 2 * SEQ // (NB * P) + NE - 1
PAIR = 2 * NCH
START = 4
SLOTS = NE * SEQ
R_CW, R_CB, R_QN, R_KN, R_QF, R_KF, R_PE = 0, 24, 30, 31, 32, 33, 34
NR = R_PE + CMP_BLK
N_PARAMS = 14
NCR = 2 * NF + 2


def build_program(nc, x, attn_norm, w_in, nsa_q_norm, nsa_k_norm, pe_k, pe_v, w_ck, w_cv,
                  conv_w, conv_b, dt_bias, a_log, ssd_d, ssd_norm, fox_q_norm, fox_k_norm,
                  fox_f_bias, w_out, ffn_norm, ffn_w1, ffn_w3, ffn_w2, router, moe_w1, moe_w3,
                  moe_w2, out, depth=DEPTH, do_ffn=True):
    top = [nc.sbuf_base + (-nc.sbuf_base) % 32]

    def place(name, shape, dtype=F32, at=None):
        size = mybir.dt.size(dtype)
        for n in shape[1:]:
            size *= n
        size += -size % 32
        start = top[0] if at is None else at
        if at is None:
            top[0] += size
        else:
            region_end[0] = max(region_end[0], start + size)
        return nc.alloc_sbuf_tensor_at("b_" + name, shape, dtype, offset=start), start + size

    region_end = [0]

    def fixed(name, shape, dtype=F32):
        return place(name, shape, dtype)[0]

    ident = fixed("ident", [P, P])
    upper = fixed("upper", [P, P])
    supper = fixed("supper", [P, P])
    ones = fixed("ones", [P, P])
    ident_b = fixed("ident_b", [P, P], BF16)
    causal_b = fixed("causal_b", [P, P], BF16)
    causal_tb = fixed("causal_tb", [P, P], BF16)
    cmp_b = fixed("cmp_b", [P, NT, 32], BF16)
    cmp_01 = fixed("cmp_01", [P, NT, 32])
    iota_e = fixed("iota_e", [P, NE])
    iota_i = fixed("iota_i", [P, NE], I32)
    iota_m = fixed("iota_m", [P, NE])
    base_e = fixed("base_e", [P, NE])
    base_p = fixed("base_p", [P, NE, 2])
    seg = fixed("seg", [P, 3, NSEG])
    seg_i = fixed("seg_i", [P, 2, NSEG], I32)
    seg_before = fixed("seg_before", [P, NSEG, NSEG])
    minus_half = fixed("minus_half", [P, 32])
    first_slots = fixed("first_slots", [P, SLOTS // P + NB, 2], I32)
    g_row = fixed("g_row", [P, DM])
    ssd_g = fixed("ssd_g", [P, 512])
    prow = fixed("prow", [P, 28])
    stack = fixed("stack", [NR, P])
    cols = fixed("cols", [P, NR])
    qcol = fixed("qcol", [P, 2])
    ss_x = fixed("ss_x", [P, NT])
    rs_x = fixed("rs_x", [P, NT])
    ss_f = fixed("ss_f", [P, NT, 8])
    rs_f = fixed("rs_f", [P, NT, 8])
    ss_n = fixed("ss_n", [P, NT, 6])
    rs_n = fixed("rs_n", [P, NT, 6])
    g12 = fixed("g12", [P, NT, 12])
    e12 = fixed("e12", [P, NT, 12])
    dt_t = fixed("dt_t", [P, NT, NS])
    dta = fixed("dta", [P, NT, NS])
    logf = fixed("logf", [P, NT, NF])
    logf_before = fixed("logf_before", [P, NT, NF])
    neg_a = fixed("neg_a", [P, NS])
    acs = fixed("acs", [P, NT, NS])
    to_end = fixed("to_end", [P, NT, NS])
    e_acs = fixed("e_acs", [P, NT, NS])
    e_end = fixed("e_end", [P, NT, NS])
    e_tot = fixed("e_tot", [P, NT, NS])
    gate_e = fixed("gate_e", [P, NT, 12])
    neg_max = fixed("neg_max", [P, 8])
    c_t = fixed("c_t", [P, NT, NF])
    c_hi = fixed("c_hi", [P, NT, NF], F32R)
    sum_f = fixed("sum_f", [P, NT, NF])
    sum_n = fixed("sum_n", [P, NT, NQ, 3])
    neg_max_c = fixed("neg_max_c", [P, NQ])
    coef = fixed("coef", [P, NQ, 3])
    ss_y = fixed("ss_y", [P, NT])
    rs_y = fixed("rs_y", [P, NT])
    lg = fixed("lg", [P, NT, NE])
    eq = fixed("eq", [P, NT, NE])
    oh1 = fixed("oh1", [P, NT, NE])
    oh2 = fixed("oh2", [P, NT, NE])
    member = fixed("member", [P, NT, NE])
    member_before = fixed("member_before", [P, NT + 1, NE])
    place_e = fixed("place_e", [P, NT, NE])
    top_v = fixed("top_v", [P, NT, 2])
    gates = fixed("gates", [P, NT, 2])
    first = fixed("first", [P, NT, 2])
    dest = fixed("dest", [P, NT, 2])
    dest_i = fixed("dest_i", [P, 2, NT], I32)
    rows_i = fixed("rows_i", [P, 2, NT, 2], I32)
    left = fixed("left", [P, NE, 2])
    has = fixed("has", [P, NSEG])
    pos = fixed("pos", [P, NSEG])
    item_f = fixed("item_f", [P, 3, NSEG])
    count_f = fixed("count_f", [P, 1])
    item = fixed("item", [P, 3, NSEG], I32)
    n_items = fixed("n_items", [P, 1], I32)
    router_sb = fixed("router_sb", [P, KT, NE])
    base = top[0]

    XH, o = place("XH", [P, NT, DM], at=base)
    proj, o2 = place("proj", [P, NT, N_TOK], at=o)
    h_tok, _ = place("h_tok", [P, NT, DM], at=o)
    x_new, _ = place("x_new", [P, NT, DM], at=o)
    hT_hi, o3 = place("hT_hi", [P, KT, SEQ], F32R, at=o2)
    hT_lo, o4 = place("hT_lo", [P, KT, SEQ], F32R, at=o3)
    w_raw, o5 = place("w_raw", [P, 2, KT, WBUF], at=o4)
    w_hi, o6 = place("w_hi", [P, 2, KT, WBUF], F32R, at=o5)
    w_lo, o7 = place("w_lo", [P, 2, KT, WBUF], F32R, at=o6)
    xbcT, o8 = place("xbcT", [P, XM, SEQ + 4], at=o7)
    xcT, o9 = place("xcT", [P, XM, SEQ], at=o8)
    qa, o10 = place("qa", [P, NT, NF, HD], at=o9)
    ka, o11 = place("ka", [P, NT, NF, HD], at=o10)
    qn, o12 = place("qn", [P, NT, 6, HD], at=o11)
    assert o12 <= nc.sbuf_usable_end, (o12, nc.sbuf_usable_end)
    sq_f = XH[:, :, 0:512]
    sq_n = XH[:, :, 512:896]
    q_f, a1 = place("q_f", [P, NF, SEQ], F32R, at=o5)
    kh_f, a2 = place("kh_f", [P, NF, SEQ], F32R, at=a1)
    kl_f, a3 = place("kl_f", [P, NF, SEQ], F32R, at=a2)
    q_n, a4 = place("q_n", [P, NQ, SEQ], F32R, at=a3)
    kh_n, a5 = place("kh_n", [P, 2, SEQ], F32R, at=a4)
    kl_n, a6 = place("kl_n", [P, 2, SEQ], F32R, at=a5)
    wcT, a7 = place("wcT", [P, CMP_BLK, HD], at=a6)
    assert a7 <= o7, (a7, o7)
    wo_raw, d1 = place("wo_raw", [P, 2, KT, WO_N], at=o4)
    c_k, d2 = place("c_k", [P, NF, SEQ], F32R, at=d1)
    assert d2 <= o5, (d2, o5)
    xs_tok, b1 = place("xs_tok", [P, NT, 512], at=o2)
    b_tok, b2 = place("b_tok", [P, NT, P], at=b1)
    u_dta, b3 = place("u_dta", [P, NS, P], at=b2)
    decay, b4 = place("decay", [P, NS, P], at=b3)
    xdt0, b5 = place("xdt0", [P, 512], at=b4)
    xdtd0, b6 = place("xdtd0", [P, 512], at=b5)
    xs_d0, b7 = place("xs_d0", [P, 512], at=b6)
    xdt1, g1 = place("xdt1", [P, 512], at=o9)
    xdtd1, g2 = place("xdtd1", [P, 512], at=g1)
    xs_d1, g3 = place("xs_d1", [P, 512], at=g2)
    assert g3 <= o11, (g3, o11)
    xdt, xdtd, xs_d = (xdt0, xdt1), (xdtd0, xdtd1), (xs_d0, xs_d1)
    state, b8 = place("state", [P, 256], at=b7)
    kvT, b9 = place("kvT", [P, SEQ], at=b8)
    y_sq, b10 = place("y_sq", [P, 512], at=b9)
    c_q, b11 = place("c_q", [P, SEQ], F32R, at=b10)
    c_src, b12 = place("c_src", [P, NT, 1 + NF, NCR], at=b11)
    assert b12 <= o4, (b12, o4)
    prob, e1 = place("prob", [P, 3, SEQ], at=o2)
    probT, e2 = place("probT", [P, 2, SEQ], at=e1)
    kv_pe, c1 = place("kv_pe", [P, 2, CMP_BLK, CMP_STRIDE], at=o7)
    kc_n, c2 = place("kc_n", [NC, HD], at=c1)
    kc_sq, c3 = place("kc_sq", [NC, HD], at=c2)
    vc, c4 = place("vc", [NC, HD], at=c3)
    kcT, c5 = place("kcT", [P, 2, NC + 1], F32R, at=c4)
    ss_c, c6 = place("ss_c", [NC, 1], at=c5)
    rs_c, c7 = place("rs_c", [NC, 1], at=c6)
    y_t, c8 = place("y_t", [P, 512], at=c7)
    p_cmp, c9 = place("p_cmp", [P, NQ, 32], at=c8)
    pT_cmp, c10 = place("pT_cmp", [NC, NQ, P], at=c9)
    o_acc, c11 = place("o_acc", [P, 256], at=c10)
    o_part, c12 = place("o_part", [P, 256], at=c11)
    assert c12 <= o8, (c12, o8)
    hT_f = place("hT_f", [P, KT, SEQ], at=o5)[0]
    sel, s1 = place("sel", [P, NSEG, NSEG], at=o5)
    sel_v = place("sel_v", [P, NSEG, NSEG], at=s1)[0]
    f_w2_hi, f1 = place("f_w2_hi", [P, 2, FK, DM], F32R, at=base)
    f_w2_lo, f2 = place("f_w2_lo", [P, 2, FK, DM], F32R, at=f1)
    f_w2, f3 = place("f_w2", [P, 2, FK, DM], at=f2)
    f_w13_hi, f4 = place("f_w13_hi", [P, 2, KT, 2, FFC], F32R, at=f3)
    f_w13, f5 = place("f_w13", [P, 2, KT, 2, FFC], at=f4)
    f_w13_lo, f6 = place("f_w13_lo", [P, 2, KT, 2, FFC], F32R, at=f5)
    assert f2 >= o + NT * DM * 4 and f3 >= o2 and f4 >= o4 and f4 + KT * 2 * FFC * 4 <= o5
    xT_hi, f7 = place("xT_hi", [P, KT, NB, P], F32R, at=f6)
    xT_lo, f8 = place("xT_lo", [P, KT, NB, P], F32R, at=f7)
    xblk, f9 = place("xblk", [P, NB, DM], at=f8)
    silu, f10 = place("silu", [P, NB, FFC], at=f9)
    gate_up, f11 = place("gate_up", [P, NB, FFC], at=f10)
    gT_hi, f12 = place("gT_hi", [P, NB, FK, P], F32R, at=f11)
    gT_lo, f13 = place("gT_lo", [P, NB, FK, P], F32R, at=f12)
    y_sb, f14 = place("y_sb", [P, NB, DM], at=f13)
    slots_next, f15 = place("slots_next", [P, NB, 2], I32, at=f14)
    slots, f16 = place("slots", [P, NB, 2], I32, at=f15)
    part_up, f17 = place("part_up", [HD, 2 * FFC], at=f16)
    assert f17 <= nc.sbuf_usable_end
    bank = [nc.alloc_psum_tensor(f"bank{n}", [P, 512], F32) for n in range(8)]

    h_rows = nc.dram_tensor("h_rows", (SEQ, DM), F32).ap()
    slot_rows = nc.dram_tensor("slot_rows", (SLOTS + NB * P, 2), I32).ap()

    mix_sems = []

    def sem(name):
        mix_sems.append(nc.alloc_semaphore(name))
        return mix_sems[-1]

    x_loaded = [sem(f"x_loaded{i}") for i in range(NT)]
    x_again = [sem(f"x_again{i}") for i in range(NT)]
    wraw_loaded = [sem(f"wraw_loaded{i}") for i in range(2)]
    (grow_loaded, params_loaded, wcmp_loaded, router_loaded, stored) = map(
        sem, ("grow_loaded", "params_loaded", "wcmp_loaded", "router_loaded", "stored"))
    (cols_t, cols_ready, x_squared, ms_ready, rs_ready, h_ready, xt_done, xt_hi, xt_lo, w_hi_done, w_lo_done,
     unit_done, proj_out, conv_done, silu_done) = map(sem, (
         "cols_t", "cols_ready", "x_squared", "ms_ready", "rs_ready", "h_ready", "xt_done", "xt_hi", "xt_lo",
         "w_hi_done", "w_lo_done", "unit_done", "proj_out", "conv_done", "silu_done"))
    (soft_in, soft_exp, soft_ln, soft_done, head_sq, head_ms, head_rs, fox_ready, nsa_ready, sums_done, acs_ready,
     decays_ready, z_ready, tr_done, tr_out) = map(sem, (
         "soft_in", "soft_exp", "soft_ln", "soft_done", "head_sq", "head_ms", "head_rs", "fox_ready", "nsa_ready",
         "sums_done", "acs_ready", "decays_ready", "z_ready", "tr_done", "tr_out"))
    (u_ready, xdt_ready, ssd_scores, ssd_diff, ssd_exp, ssd_m, ssd_y, ssd_new, state_ready, y_gated, y_squared, y_ms,
     y_rs) = map(sem, (
         "u_ready", "xdt_ready", "ssd_scores", "ssd_diff", "ssd_exp", "ssd_m", "ssd_y", "ssd_new", "state_ready",
         "y_gated", "y_squared", "y_ms", "y_rs"))
    (scores_done, max_ready, exp_done, pT_done, pT_out_act, pT_out_dve, o_done, o_read) = map(sem, (
        "scores_done", "max_ready", "exp_done", "pT_done", "pT_out_act", "pT_out_dve", "o_done", "o_read"))
    (pe_added, kc_done, kc_ms, kc_rs, kc_ready, kcT_done, kcT_out, c_scores, c_shift, c_exp, c_prob, cT_done, cT_out,
     c_out, gate_exp, mixed) = map(sem, (
         "pe_added", "kc_done", "kc_ms", "kc_rs", "kc_ready", "kcT_done", "kcT_out", "c_scores", "c_shift", "c_exp",
         "c_prob", "cT_done", "cT_out", "c_out", "gate_exp", "mixed"))
    (res_added, logits_done, routed, ranks_done, dest_ready, gate_diff, gate_e2, dve_step, pe_step,
     pool_step) = map(sem, (
         "res_added", "logits_done", "routed", "ranks_done", "dest_ready", "gate_diff", "gate_e2", "dve_step",
         "pe_step", "pool_step"))
    tr_lo, c_ready, c_set, kcT_lo = sem("tr_lo"), sem("c_ready"), sem("c_set"), sem("kcT_lo")
    slots_known, route_step = sem("slots_known"), sem("route_step")
    f_loaded = [[sem(f"f_loaded{s}_{part}") for part in range(3)] for s in range(2)]
    f_hi, f_lo, f_used2 = sem("f_hi"), sem("f_lo"), sem("f_used2")
    h13_done = [sem(f"h13_done{b}") for b in range(NB)]
    silu_out = [sem(f"silu_out{b}") for b in range(NB)]
    gu_ready = [sem(f"gu_ready{b}") for b in range(NB)]
    gT_done, gT_hi_done, gT_lo_done = sem("gT_done"), sem("gT_hi_done"), sem("gT_lo_done")
    y_out = [sem(f"y_out{b}") for b in range(2)]
    x_tr, x_hi, x_lo = sem("x_tr"), sem("x_hi"), sem("x_lo")
    slots_taken = sem("slots_taken")
    x_stacked, part_out, part_sum, y_step = sem("x_stacked"), sem("part_out"), sem("part_sum"), sem("y_step")

    w0_rest = sem("w0_rest")

    def keep(name):
        return nc.alloc_semaphore(name)

    clearing, pool_past = keep("clearing"), keep("pool_past")
    setup_done, setup_dve, layer_done, layer_go = keep("setup_done"), keep("setup_dve"), keep("layer_done"), keep("layer_go")
    pool_done, w0_loaded, g0_loaded = keep("pool_done"), keep("w0_loaded"), keep("g0_loaded")
    rows_sent = keep("rows_sent")
    scattered, slots_loaded, x_gathered, y_added = (keep("scattered"), keep("slots_loaded"), keep("x_gathered"),
                                                    keep("y_added"))

    units = []
    for j, (_, w, channels, off) in enumerate(W_IN):
        for m in range(w // P if channels else NT):
            units.append((j, m, channels, off, w))
    unit_of = [[u for u, x_ in enumerate(units) if x_[0] == j] for j in range(NW_IN)]
    att = [(i, i, h, None, O_VF + HD * h, HD * h) for i in range(NT) for h in range(NF)]
    att += [(NT + i, i, h, 4 + br, C_KV + HD * (3 + 2 * br), 256 * br + HD * h)
            for i in range(NT) for h in range(NQ) for br in range(2)]
    NU = len(att)
    by_act = [i in (1, 2) for _, i, *_ in att]
    nth_out = [sum(by_act[:u + 1]) if by_act[u] else u + 1 - sum(by_act[:u + 1]) for u in range(NU)]

    xt_bank = (0, 1, 6, 7)

    def x_bank(i, kk):
        return 6 + kk % 2 if isinstance(i, int) else 7

    s_bank = (0, 1, 5)
    last_of = [max(u for u in range(NU) if att[u][0] == g) for g in range(2 * NT)]
    first_of = [min(u for u in range(NU) if att[u][0] == g) for g in range(2 * NT)]
    z_col = slice(C_Z, C_Z + 512)

    def x_rows(t, src):
        return src[t * P:(t + 1) * P, :]

    def bc(ap, *shape):
        return ap.to_broadcast([P, *shape])

    w_in_v = w_in.rearrange("l (k p) n -> p (l k) n", p=P)
    w_out_v = w_out.rearrange("l (k p) n -> p (l k) n", p=P)
    w_ck_v = w_ck.rearrange("l (j d) n -> d (l j) n", d=HD)
    w_cv_v = w_cv.rearrange("l (j d) n -> d (l j) n", d=HD)
    cw_v = conv_w.rearrange("l t (m c) -> (l t m) c", c=P)
    cb_v = conv_b.rearrange("l (m c) -> (l m) c", c=P)
    pk_v = pe_k.rearrange("l j d -> (l j) d")
    pv_v = pe_v.rearrange("l j d -> (l j) d")
    slot_v = slot_rows.rearrange("(b p) c -> p b c", p=P)
    dense13 = [w.rearrange("l (k p) n -> p (l k) n", p=P) for w in (ffn_w1, ffn_w3)]
    moe13 = [w.rearrange("l e (k p) n -> p (l e k) n", p=P) for w in (moe_w1, moe_w3)]
    dense2 = ffn_w2.rearrange("l (k p) n -> p (l k) n", p=P)
    moe2 = moe_w2.rearrange("l e (k p) n -> p (l e k) n", p=P)

    block_cm = nc.Block()
    block = block_cm.__enter__()

    @block.sync
    def _(sp):
        def load_x(layer, dst, sems, with_gains=False):
            with sp.If(layer < 1):
                for t in range(NT):
                    sp.dma_start(dst[:, t, :], x_rows(t, x)).then_inc(sems[t], 16)
                    if t == 0 and with_gains:
                        load_g0(0)
                sp.nop()
            with sp.Else():
                for t in range(NT):
                    sp.dma_start(dst[:, t, :], x_rows(t, out)).then_inc(sems[t], 16)
                sp.nop()

        def load_ffn(w13, w2, n, c, s, krow, frow, parts=(0, 1, 2)):
            for part in parts:
                if n is not None:
                    sp.wait_ge(f_lo, n * 3 + (part - 5 + START))
                if part == 2:
                    sp.dma_start(f_w2[:, s], w2[:, bass.ds(frow + c * FK, FK), :]).then_inc(f_loaded[s][2], 16)
                else:
                    ks, rows = slice(part * KT // 2, (part + 1) * KT // 2), krow(part)
                    for i in range(2):
                        sp.dma_start(f_w13[:, s, ks, i, :], w13[i][:, rows, bass.ds(c * FFC, FFC)]).then_inc(
                            f_loaded[s][part], 16)

        def for_layer(layer, expert, body):
            with sp.If(layer < 1):
                body(dense13, dense2, lambda part: slice(part * KT // 2, (part + 1) * KT // 2), 0)
                sp.nop()
            with sp.Else():
                body(moe13, moe2, lambda part: bass.ds(expert * KT + part * KT // 2, KT // 2), expert * (NCH * FK))
                sp.nop()

        def load_w0(layer):
            col, w = W_IN[0][:2]
            sp.dma_start(w_raw[:, 0, :, 0:w], w_in_v[:, layer * KT:(layer + 1) * KT, col:col + w]
                         ).then_inc(w0_loaded, 16)

        def load_g0(layer):
            sp.dma_start(g_row[:], attn_norm[layer:layer + 1, :].partition_broadcast(P)).then_inc(g0_loaded, 16)

        with sp.Fori(0, depth) as layer:
            load_x(layer, XH, x_loaded, True)
            for j, (col, w, _, _) in enumerate(W_IN):
                if j >= 2:
                    sp.wait_ge(w_lo_done, j - 1)
                    sp.wait_ge(w0_rest, 1)
                if j == 0:
                    with sp.If(layer < 1):
                        load_w0(0)
                        sp.nop()
                else:
                    sp.dma_start(w_raw[:, j % 2, :, 0:w], w_in_v[:, bass.ds(layer * KT, KT), col:col + w]).then_inc(
                        wraw_loaded[j % 2], 16)
                if j == 0:
                    small = [
                        (stack[R_CW:R_CB, :], cw_v[bass.ds(layer * 24, 24), :]),
                        (stack[R_CB:R_QN, :], cb_v[bass.ds(layer * 6, 6), :]),
                        (stack[R_QN:R_KN, 0:HD], nsa_q_norm[bass.ds(layer, 1), :]),
                        (stack[R_KN:R_QF, 0:HD], nsa_k_norm[bass.ds(layer, 1), :]),
                        (stack[R_QF:R_KF, 0:HD], fox_q_norm[bass.ds(layer, 1), :]),
                        (stack[R_KF:R_PE, 0:HD], fox_k_norm[bass.ds(layer, 1), :]),
                        (stack[R_PE:NR, 0:HD], pk_v[bass.ds(layer * CMP_BLK, CMP_BLK), :]),
                        (stack[R_PE:NR, HD:P], pv_v[bass.ds(layer * CMP_BLK, CMP_BLK), :]),
                        (prow[:, 0:8], dt_bias[bass.ds(layer, 1), :].partition_broadcast(P)),
                        (prow[:, 8:16], a_log[bass.ds(layer, 1), :].partition_broadcast(P)),
                        (prow[:, 16:24], ssd_d[bass.ds(layer, 1), :].partition_broadcast(P)),
                        (prow[:, 24:28], fox_f_bias[bass.ds(layer, 1), :].partition_broadcast(P)),
                        (ssd_g[:], ssd_norm[bass.ds(layer, 1), :].partition_broadcast(P)),
                        (router_sb[:], router.rearrange("l (k p) n -> p (l k) n", p=P)),
                    ]
                    assert len(small) == N_PARAMS
                    sp.wait_ge(setup_done, 1)
                    for dst, src in small:
                        sp.dma_start(dst, src).then_inc(params_loaded, 16)
                    sp.dma_start(slot_v, first_slots[:]).then_inc(router_loaded, 16)
            sp.wait_ge(unit_done, len(units))
            sp.dma_start(wcT[0:HD], w_ck_v[:, bass.ds(layer * CMP_BLK, CMP_BLK), :]).then_inc(wcmp_loaded, 16)
            sp.dma_start(wcT[HD:P], w_cv_v[:, bass.ds(layer * CMP_BLK, CMP_BLK), :]).then_inc(wcmp_loaded, 16)
            sp.wait_ge(h_ready, NT)
            sp.dma_start(g_row[:], ffn_norm[bass.ds(layer, 1), :].partition_broadcast(P)).then_inc(grow_loaded, 16)
            for n in range(NW_OUT):
                j = NW_IN + n
                sp.wait_ge(w_lo_done, max(j - 1, NW_IN))
                sp.dma_start(wo_raw[:, j % 2], w_out_v[:, bass.ds(layer * KT, KT), n * WO_N:(n + 1) * WO_N]
                             ).then_inc(wraw_loaded[j % 2], 16)
                if n == 1:
                    sp.wait_ge(mixed, 9)
                    load_x(layer, x_new, x_again)
            if do_ffn:
              with sp.If(layer < 1):
                sp.wait_ge(w_lo_done, NW_IN + NW_OUT)
                load_ffn(dense13, dense2, None, 0, 0, lambda part: slice(part * KT // 2, (part + 1) * KT // 2), 0)
                sp.nop()
            for t in range(NT):
                sp.wait_ge(res_added, (NW_OUT - 1) * NT + t + 1)
                sp.dma_start(x_rows(t, out), x_new[:, t, :]).then_inc(stored, 16)
            for t in range(NT):
                sp.wait_ge(h_ready, NT + t + 1)
                sp.dma_start(x_rows(t, h_rows), XH[:, t, :]).then_inc(stored, 16)
            sp.wait_ge(stored, 2 * NT * 16)
            sp.wait_ge(unit_done, len(units) + NW_OUT * NT)
            sp.wait_ge(dest_ready, 1)
            if do_ffn:
              def expert_of(i):
                  return sp.value_load(item[0:1, 1, bass.ds(i, 1)], min_val=0, max_val=NE - 1)

              def first_chunk(w13, w2, krow, frow):
                  load_ffn(w13, w2, None, 0, 0, krow, frow, (0, 1))
                  sp.wait_ge(x_gathered, layer * ((DENSE_ITEMS + 1) * 32) + 32)
                  load_ffn(w13, w2, None, 0, 0, krow, frow, (2,))

              with sp.If(layer > 0):
                  expert = expert_of(0)
                  first_chunk(moe13, moe2, lambda part: bass.ds(expert * KT + part * KT // 2, KT // 2),
                              expert * (NCH * FK))
                  sp.nop()
              with sp.Fori(0, (layer * (MOE_ITEMS - DENSE_ITEMS) + DENSE_ITEMS) // 2) as pair:
                for odd in range(2):
                  tokens = sp.value_load(item[0:1, 2, bass.ds(pair * 2 + odd, 1)], min_val=0, max_val=SEQ)
                  with sp.If(tokens > 0):
                    def chunks(w13, w2, krow, frow):
                        n = pair * PAIR + odd * NCH
                        load_ffn(w13, w2, n + 1, 1, (odd + 1) % 2, krow, frow)
                        with sp.Fori(1, NCH // 2) as two:
                            load_ffn(w13, w2, n + two * 2, two * 2, odd, krow, frow)
                            load_ffn(w13, w2, n + two * 2 + 1, two * 2 + 1, 1 - odd, krow, frow)
                        load_ffn(w13, w2, n + NCH - 1, NCH - 1, odd, krow, frow)

                    def chunk_0(w13, w2, krow, frow):
                        load_ffn(w13, w2, pair * PAIR + (odd + 1) * NCH, 0, 1 - odd, krow, frow)

                    for_layer(layer, expert_of(pair * 2 + odd), chunks)
                    for_layer(layer, expert_of(pair * 2 + odd + 1), chunk_0)
                    sp.nop()
                  sp.nop()
            sp.wait_ge(layer_done, (layer + 1) * 3)
            sp.wait_ge(rows_sent, layer + 1)
            sp.sem_inc(clearing, 1)
            if depth == 2:
                with sp.If(layer < 1):
                    load_w0(1)
                    sp.nop()
            sp.wait_ge(pool_done, layer + 1)
            sp.sem_inc(clearing, 1)
            if depth == 2:
                with sp.If(layer < 1):
                    load_g0(1)
                    sp.nop()
            sp.sem_inc(clearing, 1)
            sp.sem_clear(range(mix_sems[0].num, mix_sems[-1].num + 1))
            sp.sem_inc(layer_go, 1)

    @block.gpsimd
    def _(pool):
        def step(ins, count=[0]):
            count[0] += 1
            ins.then_inc(setup_dve, 1)
            pool.wait_ge(setup_dve, count[0])

        step(nc.gpsimd.memset(ones[:], 1.0))
        nc.gpsimd.affine_select(upper[:], ones[:], [[1, P]], ALU.is_ge, 0.0, base=0, channel_multiplier=-1)
        nc.gpsimd.affine_select(supper[:], ones[:], [[1, P]], ALU.is_gt, 0.0, base=0, channel_multiplier=-1)
        step(nc.gpsimd.affine_select(ident[:], ones[:], [[-1, P]], ALU.is_equal, 0.0, base=0, channel_multiplier=1))
        nc.gpsimd.tensor_copy(ident_b[:], ident[:])
        nc.gpsimd.memset(cmp_01[:], 1.0)
        step(nc.gpsimd.memset(causal_b[:], 0.0))
        step(nc.gpsimd.memset(causal_tb[:], 0.0))
        step(nc.gpsimd.memset(cmp_b[:], 0.0))
        nc.gpsimd.affine_select(causal_b[:], causal_b[:], [[-1, P]], ALU.is_ge, NEG, base=0, channel_multiplier=1)
        nc.gpsimd.affine_select(causal_tb[:], causal_tb[:], [[1, P]], ALU.is_ge, NEG, base=0, channel_multiplier=-1)
        for dst, fill in ((cmp_b, NEG), (cmp_01, 0.0)):
            nc.gpsimd.affine_select(dst[:], dst[:], [[P, NT], [-CMP_STRIDE, 32]], ALU.is_ge, fill,
                                    base=1 - CMP_BLK, channel_multiplier=1)
        nc.gpsimd.memset(minus_half[:], -0.5)
        nc.gpsimd.memset(stack[:], 1.0)
        nc.gpsimd.memset(first_slots[:].bitcast(F32), 0.0)
        nc.gpsimd.memset(member_before[:], 0.0)
        nc.gpsimd.memset(logf_before[:], 0.0)
        nc.gpsimd.iota(iota_i[:], [[1, NE]], base=0, channel_multiplier=0)
        nc.gpsimd.iota(seg_i[:, 0, :], [[1, NSEG]], base=0, channel_multiplier=0)
        nc.gpsimd.iota(seg_i[:, 1, :], [[1, NE], [0, HALVES]], base=0, channel_multiplier=0)
        step(nc.gpsimd.memset(seg_before[:], 1.0))
        nc.gpsimd.affine_select(seg_before[:], seg_before[:], [[1, NSEG], [-1, NSEG]], ALU.is_gt, 0.0, base=0,
                                channel_multiplier=0)
        for c in range(2):
            last = nc.gpsimd.iota(rows_i[:, c, :, 0], [[P, NT]], base=0, channel_multiplier=1)
        step(last)
        nc.gpsimd.iota(first_slots[:, :, 0], [[0, SLOTS // P + NB]], base=BIG_ID, channel_multiplier=0)
        nc.gpsimd.tensor_copy(seg[:, 0:2, :], seg_i[:])
        step(nc.gpsimd.tensor_copy(iota_e[:], iota_i[:]))
        nc.gpsimd.tensor_scalar(seg[:, 2, :], seg[:, 0, :], float(NB), -float(SLOTS // P), ALU.mult, ALU.add)
        nc.gpsimd.tensor_scalar(iota_m[:], iota_e[:], -float(NE), None, ALU.add)
        nc.gpsimd.tensor_scalar(base_e[:], iota_e[:], float(SEQ), None, ALU.mult)
        for half in range(HALVES):
            nc.gpsimd.memset(base_p[:, :, half], float(half * NB * P))
        nc.gpsimd.iota(first_slots[:, 0:NT, 0], [[P, NT]], base=0, channel_multiplier=1)
        nc.gpsimd.memset(first_slots[:, 0:NT, 1].bitcast(F32), 1.0)
        nc.gpsimd.iota(item[:, 0, :], [[0, NSEG]], base=SLOTS // P, channel_multiplier=0)
        nc.gpsimd.memset(item[:, 1:3, :].bitcast(F32), 0.0)
        step(nc.gpsimd.iota(n_items[:], [[0, 1]], base=DENSE_ITEMS, channel_multiplier=0))
        nc.gpsimd.iota(item[:, 0, 0:DENSE_ITEMS], [[NB, DENSE_ITEMS]], base=0, channel_multiplier=0)
        step(nc.gpsimd.iota(item[:, 2, 0:DENSE_ITEMS], [[0, DENSE_ITEMS]], base=NB * P, channel_multiplier=0))
        nc.gpsimd.nop().then_inc(setup_done, 1)
        pool.dma_start(h_rows[0:P, 0:32], minus_half[:]).then_inc(y_added, 16)

        with pool.Fori(0, depth) as layer:
            n_step = [0]

            def link(ins):
                n_step[0] += 1
                ins.then_inc(pool_step, 1)
                pool.wait_ge(pool_step, n_step[0])

            def power(dst, src, n, wait, count, done, rows=P):
                pool.wait_ge(wait, count)
                nc.gpsimd.tensor_tensor(dst, src, minus_half[0:rows, 0:n], ALU.pow).then_inc(done, 1)

            for t in range(NT):
                power(rs_x[:, t:t + 1], ss_x[:, t:t + 1], 1, ms_ready, t + 1, rs_ready)
            pool.wait_ge(y_added, 16)
            pool.wait_ge(w_hi_done, 1)
            w0 = W_IN[0][1]
            part = slice(0, W0_POOL)
            nc.gpsimd.tensor_tensor(w_lo[:, 0, part, 0:w0], w_raw[:, 0, part, 0:w0], w_hi[:, 0, part, 0:w0].bitcast(F32),
                                    ALU.subtract).then_inc(w_lo_done, 1)
            pool.wait_ge(h_ready, NT)
            pool.wait_ge(proj_out, unit_of[3][-1] + 1)
            nc.gpsimd.tensor_tensor(sq_f, proj[:, :, O_QF:O_QF + 512], proj[:, :, O_QF:O_QF + 512],
                                    ALU.mult).then_inc(head_sq, 1)
            power(rs_f[:].rearrange("p t h -> p (t h)"), ss_f[:].rearrange("p t h -> p (t h)"), 32, head_ms, 1, head_rs)
            pool.wait_ge(proj_out, unit_of[5][-1] + 1)
            nc.gpsimd.tensor_tensor(sq_n[:, :, 0:256], proj[:, :, 0:256], proj[:, :, 0:256], ALU.mult)
            kvw = proj[:, :, C_KV + 128:C_KV + 384].rearrange("p t (a b) -> p t a b", a=2)[:, :, :, 0:HD]
            nc.gpsimd.tensor_tensor(sq_n[:, :, 256:384].rearrange("p t (a b) -> p t a b", a=2), kvw, kvw,
                                    ALU.mult).then_inc(head_sq, 1)
            power(rs_n[:].rearrange("p t h -> p (t h)"), ss_n[:].rearrange("p t h -> p (t h)"), 24, head_ms, 2, head_rs)
            pool.wait_ge(unit_done, len(units))
            nc.gpsimd.memset(c_src[:, :, 0, 2 * NF:NCR], 1.0)
            link(nc.gpsimd.memset(c_src[:, :, 1:1 + NF, 0:2 * NF], 0.0))
            for h in range(NF):
                for at in (h, NF + h):
                    nc.gpsimd.memset(c_src[:, :, 1 + h, at:at + 1], 1.0)
            nc.gpsimd.memset(c_q[:].bitcast(F32), 0.0)
            pool.wait_ge(w_lo_done, NW_IN)
            nc.gpsimd.memset(c_k[:].bitcast(F32), 0.0)
            nc.gpsimd.memset(kcT[:, :, NC:NC + 1].bitcast(F32), 0.0).then_inc(c_set, 1)
            for c in range(NT):
                xs_c = xs_tok[:, c, :].rearrange("p (h d) -> p h d", h=NS)

                def v(t):
                    return t[:].rearrange("p (h d) -> p h d", h=NS)
                if c == 0:
                    pool.wait_ge(soft_done, 1)
                    pool.wait_ge(decays_ready, 1)
                    pool.wait_ge(tr_out, NT + 1)
                else:
                    pool.wait_ge(ssd_scores, c)
                nc.gpsimd.tensor_tensor(u_dta[:], bc(upper[:].unsqueeze(1), NS, P), bc(dta[:, c, :].unsqueeze(2), NS, P),
                                        ALU.mult).then_inc(u_ready, 1)
                a = c % 2
                if c >= 2:
                    pool.wait_ge(ssd_y, c - 1)
                    pool.wait_ge(y_gated, c - 1)
                link(nc.gpsimd.tensor_tensor(v(xdt[a]), xs_c, bc(dt_t[:, c, :].unsqueeze(2), NS, HD), ALU.mult))
                nc.gpsimd.tensor_tensor(v(xdtd[a]), v(xdt[a]), bc(e_end[:, c, :].unsqueeze(2), NS, HD), ALU.mult)
                nc.gpsimd.tensor_tensor(v(xs_d[a]), xs_c, bc(prow[:, 16:24].unsqueeze(2), NS, HD), ALU.mult
                                        ).then_inc(xdt_ready, 1)
            power(rs_c[:], ss_c[:], 1, kc_ms, 1, kc_rs, NC)
            power(rs_y[:], ss_y[:], NT, y_ms, 1, y_rs)
            pool.wait_ge(mixed, 9)
            nc.gpsimd.memset(xblk[:], 0.0)
            link(nc.gpsimd.memset(y_sb[:], 0.0))
            for t in range(NT):
                power(rs_x[:, t:t + 1], ss_x[:, t:t + 1], 1, ms_ready, NT + t + 1, rs_ready)
            pool.wait_ge(router_loaded, 16)
            with pool.If(layer > 0):
                pool.wait_ge(slots_known, 1)
                for c in range(2):
                    for t in range(NT):
                        pool.indirect_dma_start(slot_rows, bass.IndirectOffsetOnAxis(dest_i[:, c, t:t + 1], 0),
                                                rows_i[:, c, t, :], None, bounds_check=SLOTS - 1, oob_is_err=False
                                                ).then_inc(scattered, 16)
                pool.wait_ge(scattered, layer * (2 * NT * 16))
                pool.sem_inc(pool_past, 1)
                pool.nop()
            pool.wait_ge(dest_ready, 1)

            def fetch_slots(i):
                n = layer * (DENSE_ITEMS + 1) + i + 1
                blk = pool.value_load(item[0:1, 0, bass.ds(i, 1)], min_val=0, max_val=SLOTS // P)
                pool.dma_start(slots_next[:], slot_v[:, bass.ds(blk, NB), :]).then_inc(slots_loaded, 16)
                pool.wait_ge(slots_loaded, n * 16)
                pool.sem_inc(pool_past, 1)

            def gather():
                for b in range(NB):
                    pool.indirect_dma_start(xblk[:, b, :], None, h_rows,
                                            bass.IndirectOffsetOnAxis(slots_next[:, b, 0:1], 0),
                                            bounds_check=SEQ - 1, oob_is_err=False).then_inc(x_gathered, 16)

            if do_ffn:
              fetch_slots(0)
              pool.wait_ge(stored, 2 * NT * 16)
              gather()
              with pool.Fori(0, layer * (MOE_ITEMS - DENSE_ITEMS) + DENSE_ITEMS) as i:
                tokens = pool.value_load(item[0:1, 2, bass.ds(i, 1)], min_val=0, max_val=SEQ)
                with pool.If(tokens > 0):
                    pool.wait_ge(x_tr, (i + 1) * (KT // 2))
                    pool.wait_ge(slots_taken, i + 1)
                    pool.sem_inc(pool_past, 1)
                    fetch_slots(i + 1)
                    gather()
                    for b in range(2):
                        pool.wait_ge(y_out[b], i + 1 + START)
                    pool.sem_inc(pool_past, 1)
                    for b in range(NB):
                        pool.indirect_dma_start(out, bass.IndirectOffsetOnAxis(slots[:, b, 0:1], 0), y_sb[:, b, :], None,
                                                bounds_check=SEQ - 1, oob_is_err=False, compute_op=ALU.add
                                                ).then_inc(y_added, 16)
                    pool.nop()
                pool.nop()
              pool.sem_inc(rows_sent, 1)
              items = pool.value_load(n_items[0:1, 0:1], min_val=1, max_val=MOE_ITEMS)
              pool.wait_ge(y_added, (layer * DENSE_ITEMS + items) * 32 + 16)
              pool.wait_ge(x_gathered, (layer * (DENSE_ITEMS + 1) + items + 1) * 32)
              pool.wait_ge(f_lo, items * (3 * NCH) + 3 + START)
              pool.sem_inc(pool_past, 1)
            nc.gpsimd.iota(first_slots[:, 0:NT, 0], [[0, NT]], base=BIG_ID, channel_multiplier=0)
            link(nc.gpsimd.memset(first_slots[:, 0:NT, 1].bitcast(F32), 0.0))
            pool.sem_inc(pool_done, 1)
            pool.wait_ge(layer_go, layer + 1)
            pool.nop()

    @block.tensor
    def _(pe):
        mm, tr = nc.tensor.matmul, nc.tensor.transpose

        def three(dst, ah, al, bh, bl, start, stop):
            mm(dst, ah, bh, start=start, stop=False)
            mm(dst, ah, bl, start=False, stop=False)
            return mm(dst, al, bh, start=False, stop=stop)

        pe.wait_ge(setup_done, 1)
        with pe.Fori(0, depth) as layer:
            n_xt, n_step = [0], [0]

            def finish(ins):
                n_step[0] += 1
                ins.then_inc(pe_step, 1)
                pe.wait_ge(pe_step, n_step[0])

            def transpose_tokens(src, ready, read=xt_lo):
                for t, half in TURNS:
                    n = n_xt[0]
                    if half == 0:
                        pe.wait_ge(h_ready, ready + t + 1)
                    if n >= 4:
                        pe.wait_ge(read, n - 3)
                    for j in range(4):
                        k = 4 * half + j
                        last = tr(bank[xt_bank[n % 4]][:, j * P:(j + 1) * P], src[:, t, k * P:(k + 1) * P], ident[:])
                    last.then_inc(xt_done, 1)
                    n_xt[0] += 1

            transpose_tokens(h_tok, 0)
            pe.wait_ge(params_loaded, N_PARAMS * 16)
            tr(bank[5][:, 0:NR], stack[:], ident[0:NR, 0:NR]).then_inc(cols_t, 1)
            pe.wait_ge(xt_lo, KT)
            for u, (j, m, channels, off, w) in enumerate(units):
                s = j % 2
                if u == unit_of[j][0]:
                    pe.wait_ge(w_lo_done, j + 1)
                    if j == 0:
                        pe.wait_ge(w0_rest, 1)
                if u >= 4:
                    pe.wait_ge(proj_out, u - 3)
                elif u == 3:
                    pe.wait_ge(cols_ready, 1)
                b = bank[2 + u % 4]
                ms = slice(m * P, (m + 1) * P)
                for k in range(KT):
                    if channels:
                        last = three(b[:], w_hi[:, s, k, ms], w_lo[:, s, k, ms], hT_hi[:, k, :], hT_lo[:, k, :],
                                     k == 0, k == KT - 1)
                    else:
                        last = three(b[:, 0:w], hT_hi[:, k, ms], hT_lo[:, k, ms], w_hi[:, s, k, 0:w],
                                     w_lo[:, s, k, 0:w], k == 0, k == KT - 1)
                last.then_inc(unit_done, 1)
            pe.wait_ge(soft_done, 1)
            mm(bank[6][:, 0:32], upper[:], dta[:].rearrange("p t h -> p (t h)"), start=True, stop=True)
            mm(bank[6][:, 32:64], ones[:], dta[:].rearrange("p t h -> p (t h)"), start=True, stop=True)
            mm(bank[6][:, 64:80], upper[:], logf[:].rearrange("p t h -> p (t h)"), start=True, stop=False)
            mm(bank[6][:, 64:80], ones[:], logf_before[:].rearrange("p t h -> p (t h)"), start=False, stop=True
               ).then_inc(sums_done, 1)
            n_tr, n_lo = [0], [0]
            read_by = []

            def one_transpose(parts, with_lo=False):
                n = n_tr[0]
                if n >= 4:
                    pe.wait_ge(*read_by[n - 4])
                elif n == 2:
                    pe.wait_ge(proj_out, len(units))
                for dst, src, rows in parts(bank[n % 4]):
                    last = tr(dst, src, ident[0:rows, 0:rows])
                last.then_inc(tr_done, 1)
                n_tr[0] += 1
                n_lo[0] += with_lo
                read_by.append((tr_lo, n_lo[0]) if with_lo else (tr_out, n_tr[0]))

            tile = [slice(t * P, (t + 1) * P) for t in range(NT)]
            pe.wait_ge(silu_done, XM)
            for c in range(NT):
                one_transpose(lambda b: [(b[:, tile[m]], xcT[:, m, tile[c]], P) for m in range(4)])
            one_transpose(lambda b: [(b[:, tile[c]], xcT[:, 4, tile[c]], P) for c in range(NT)])
            pe.wait_ge(fox_ready, 1)
            for h in range(NF):
                for src in (qa, ka):
                    one_transpose(lambda b: [(b[0:HD, tile[t]], src[:, t, h, :], P) for t in range(NT)], True)
            pe.wait_ge(nsa_ready, 1)
            for h in range(6):
                one_transpose(lambda b: [(b[0:HD, tile[t]], qn[:, t, h, :], P) for t in range(NT)], True)
            one_transpose(lambda b: [(b[:, tile[t]], proj[:, t, C_KV:C_KV + P], P) for t in range(NT)])
            pe.wait_ge(c_ready, 1)
            for n in range(1 + NF):
                one_transpose(lambda b: [(b[0:NCR, tile[t]], c_src[:, t, n, :], P) for t in range(NT)])
            for sem_, count in read_by[-4:]:
                pe.wait_ge(sem_, count)

            for c in range(NT):
                pe.wait_ge(u_ready, c + 1)
                if c:
                    pe.wait_ge(ssd_m, c)
                for half in range(2):
                    mm(bank[2 + half][:], ones[:], u_dta[:, 4 * half:4 * half + 4, :], start=True, stop=False)
                    mm(bank[2 + half][:].rearrange("p (h l) -> p h l", h=4), ident_b[:],
                       bc(causal_tb[:].unsqueeze(1), 4, P), start=False, stop=True)
                for g in range(2):
                    gp = slice(g * HD, (g + 1) * HD)
                    last = mm(bank[4][:, g * P:(g + 1) * P], xcT[gp, 4, tile[c]], xcT[gp, 5, tile[c]],
                              start=True, stop=True)
                    if g == 0:
                        finish(last)
                last.then_inc(ssd_scores, 1)
                if c:
                    pe.wait_ge(state_ready, c)
                    for g in range(2):
                        gp = slice(g * HD, (g + 1) * HD)
                        last = mm(bank[5][:, g * 256:(g + 1) * 256], xcT[gp, 5, tile[c]], state[gp, :], start=True, stop=True)
                        if g == 0:
                            finish(last)
                pe.wait_ge(xdt_ready, c + 1)
                if c < NT - 1:
                    for g in range(2):
                        gp = slice(g * HD, (g + 1) * HD)
                        last = mm(bank[7][gp, 0:256], b_tok[:, c, gp], xdtd[c % 2][:, g * 256:(g + 1) * 256],
                                  start=True, stop=True)
                    last.then_inc(ssd_new, 1)
                if c == 0:
                    pe.wait_ge(pe_added, 2)
                    pe.wait_ge(wcmp_loaded, 32)
                    pe.wait_ge(tr_out, len(read_by))
                for j in range(c * CMP_BLK // NT, (c + 1) * CMP_BLK // NT):
                    for kv in range(2):
                        rows = slice(kv * HD, (kv + 1) * HD)
                        late = j // CMP_STRIDE
                        last = mm(bank[kv][0:NC, 0:HD], kv_pe[rows, late, late:late + NC, j % CMP_STRIDE],
                                  wcT[rows, j, :], start=j == 0, stop=j == CMP_BLK - 1)
                if c == NT - 1:
                    last.then_inc(kc_done, 1)
                pe.wait_ge(ssd_m, c + 1)
                if c:
                    pe.wait_ge(y_gated, c)
                for h in range(NS):
                    last = mm(bank[6][:, h * HD:(h + 1) * HD], decay[:, h, :], xdt[c % 2][:, h * HD:(h + 1) * HD],
                              start=True, stop=True)
                last.then_inc(ssd_y, 1)


            pe.wait_ge(tr_out, len(read_by))
            pe.wait_ge(tr_lo, 14)
            pe.wait_ge(kc_ms, 1)

            def scores(u):
                g, i, h, keys, _, _ = att[u]
                n = (i + 1) * P
                if u == 2:
                    pe.wait_ge(y_gated, NT)
                b = bank[s_bank[u % 3]]
                q_, kh, kl = (q_f[:, h], kh_f[:, h], kl_f[:, h]) if keys is None else (
                    q_n[:, h], kh_n[:, keys - 4], kl_n[:, keys - 4])
                mm(b[:, 0:n], q_[:, tile[i]], kh[:, 0:n], start=True, stop=False)
                mm(b[:, 0:n], q_[:, tile[i]], kl[:, 0:n], start=False, stop=False)
                if keys is None:
                    mm(b[:, 0:n], c_q[:, tile[i]], c_k[:, h, 0:n], start=False, stop=False)
                mm(b[:, n - P:n], ident_b[:], causal_b[:], start=False, stop=True).then_inc(scores_done, 1)

            def turn(u):
                pe.wait_ge(exp_done, u + 1)
                for j in range(att[u][1] + 1):
                    last = tr(bank[2 + u % 2][:, tile[j]], prob[:, u % 3, tile[j]], ident[:])
                last.then_inc(pT_done, 1)

            def weigh(u):
                g, i, h, _, vcol, place_ = att[u]
                pe.wait_ge(pT_out_act if by_act[u] else pT_out_dve, nth_out[u])
                if u == first_of[g] and g >= 2:
                    pe.wait_ge(o_read, g - 1)
                for j in range(i + 1):
                    last = mm(bank[6 + g % 2][:, place_:place_ + HD], probT[:, u % 2, tile[j]],
                              proj[:, j, vcol:vcol + HD], start=j == 0, stop=j == i)
                last.then_inc(o_done, 1)

            def cmp_scores(i):
                if i == 0:
                    pe.wait_ge(kcT_lo, 1)
                else:
                    pe.wait_ge(o_read, NT + i)
                for h in range(NQ):
                    o_ = bank[4][:, 256 + 32 * h:256 + 32 * (h + 1)]
                    mm(o_, q_n[:, h, tile[i]], kcT[:, 0, :], start=True, stop=False)
                    mm(o_, q_n[:, h, tile[i]], kcT[:, 1, :], start=False, stop=False)
                    last = mm(o_, ident_b[:], cmp_b[:, i, :], start=False, stop=True)
                last.then_inc(c_scores, 1)

            def cmp_turn(i):
                pe.wait_ge(c_prob, i + 1)
                for h in range(NQ):
                    last = tr(bank[4][0:NC, tile[h]], p_cmp[:, h, 0:NC], ident[:])
                last.then_inc(cT_done, 1)

            def cmp_weigh(i):
                pe.wait_ge(cT_out, i + 1)
                for h in range(NQ):
                    last = mm(bank[4][:, h * HD:(h + 1) * HD], pT_cmp[:, h, :], vc[:], start=True, stop=True)
                last.then_inc(c_out, 1)

            for u in range(NU + 4):
                if u < NU:
                    scores(u)
                if 2 <= u < NU + 2:
                    turn(u - 2)
                if u == 6:
                    pe.wait_ge(kc_ready, 1)
                    tr(bank[4][0:HD, 0:NC], kc_n[:], ident[0:NC, 0:NC]).then_inc(kcT_done, 1)
                if 3 <= u < NU + 3:
                    weigh(u - 3)
                for i in range(NT):
                    at = u - first_of[NT + i]
                    if at == 4:
                        cmp_scores(i)
                    if at == 8:
                        cmp_turn(i)
                    if at == 10:
                        cmp_weigh(i)

            pe.wait_ge(mixed, 9)
            transpose_tokens(XH, 0)
            pe.wait_ge(xt_lo, 2 * KT)
            for n in range(NW_OUT):
                j = NW_IN + n
                s = j % 2
                pe.wait_ge(w_lo_done, j + 1)
                for t in range(NT):
                    v = n * NT + t
                    if v >= 4:
                        pe.wait_ge(res_added, v - 3)
                    b = bank[2 + v % 4]
                    for k in range(KT):
                        last = three(b[:, 0:WO_N], hT_hi[:, k, tile[t]], hT_lo[:, k, tile[t]], w_hi[:, s, k, 0:WO_N],
                                     w_lo[:, s, k, 0:WO_N], k == 0, k == KT - 1)
                    last.then_inc(unit_done, 1)
            with pe.If(layer > 0):
                transpose_tokens(XH, NT, xt_hi)
                pe.wait_ge(xt_hi, 3 * KT)
                for t in range(NT):
                    for k in range(KT):
                        last = mm(bank[2][:, t * NE:(t + 1) * NE], hT_f[:, k, tile[t]], router_sb[:, k, :],
                                  start=k == 0, stop=k == KT - 1)
                last.then_inc(logits_done, 1)
                pe.wait_ge(routed, 1)
                flat = member[:].rearrange("p t e -> p (t e)")
                before = member_before[:].rearrange("p t e -> p (t e)")
                mm(bank[3][:, 0:32], supper[:], flat, start=True, stop=False)
                mm(bank[3][:, 0:32], ones[:], before[:, 0:32], start=False, stop=True)
                mm(bank[3][:, 32:40], ones[:], before[:, 32:40], start=True, stop=True).then_inc(ranks_done, 1)
                pe.nop()

            if do_ffn:
              pe.wait_ge(dest_ready, 1)
              for s_ in (f_used2, gT_done, *h13_done):
                  pe.sem_inc(s_, START)

              def turn_x(i, kk):
                  if kk == 0:
                      pe.wait_ge(x_gathered, (layer * (DENSE_ITEMS + 1) + i + 1) * 32)
                  if not isinstance(i, int):
                      pe.wait_ge(x_lo, i * (KT // 2) + kk)
                  elif kk >= 2:
                      pe.wait_ge(x_lo, kk - 1)
                  b_ = bank[x_bank(i, kk)]
                  for k in range(2):
                      for b in range(NB):
                          at = (k * NB + b) * P
                          last = tr(b_[:, at:at + P], xblk[:, b, (2 * kk + k) * P:(2 * kk + k + 1) * P], ident[:])
                  last.then_inc(x_tr, 1)

              def work(pair, odd, nb, small=False):
                  i = pair * 2 + odd
                  base_n = pair * PAIR + odd * NCH

                  def up(s, b, ks):
                      for k in ks:
                          if b and small:
                              both = xT_hi[:, k, b, :]
                              mm(bank[4 + b][:], both, f_w13_hi[:, s, k, :, :], start=k == 0, stop=False)
                              last = mm(bank[4 + b][:], both, f_w13_lo[:, s, k, :, :], start=False, stop=k == KT - 1)
                              continue
                          last = three(bank[4 + b][:], xT_hi[:, k, b, :], xT_lo[:, k, b, :],
                                       f_w13_hi[:, s, k, :, :], f_w13_lo[:, s, k, :, :], k == 0, k == KT - 1)
                      return last

                  def down(s, k, first_, last_):
                      for b in range(nb):
                          for half in range(2):
                              cs = slice(half * 512, (half + 1) * 512)
                              if b and small:
                                  both = gT_hi[:, b, k, :]
                                  mm(bank[2 * b + half][:], both, f_w2_hi[:, s, k, cs], start=first_ and k == 0, stop=False)
                                  lst = mm(bank[2 * b + half][:], both, f_w2_lo[:, s, k, cs], start=False,
                                           stop=last_ and k == FK - 1)
                                  continue
                              lst = three(bank[2 * b + half][:], gT_hi[:, b, k, :], gT_lo[:, b, k, :], f_w2_hi[:, s, k, cs],
                                          f_w2_lo[:, s, k, cs], first_ and k == 0, last_ and k == FK - 1)
                      return lst

                  def turn_g(n):
                      for b in range(nb):
                          pe.wait_ge(gu_ready[b], n + 1 + START)
                      for b in range(nb):
                          for k in range(FK):
                              at = (b * FK + k) * P
                              n_ = HD if b and small else P
                              last = tr(bank[6][:, at:at + n_], gate_up[0:n_, b, k * P:(k + 1) * P], ident[0:n_, 0:n_])
                      last.then_inc(gT_done, 1)

                  def chunk(c, s, first_=False, second=False, final=False):
                      n = base_n + c
                      if first_:
                          pe.wait_ge(x_lo, (i + 1) * (KT // 2))
                      pe.wait_ge(f_lo, n * 3 + 1 + START)
                      if not first_:
                          pe.wait_ge(gu_ready[0], n + START)
                      up(s, 0, range(0, KT // 2))
                      if not first_:
                          turn_g(n - 1)
                      pe.wait_ge(f_lo, n * 3 + 2 + START)
                      last = up(s, 0, range(KT // 2, KT))
                      last.then_inc(h13_done[0], 1)
                      if nb == 2:
                          if not first_:
                              pe.wait_ge(gu_ready[1], n + START)
                          elif small:
                              pe.wait_ge(x_stacked, i + 1)
                          up(s, 1, range(KT)).then_inc(h13_done[1], 1)
                      if final:
                          turn_x(i + 1, 0)
                      if not first_:
                          pe.wait_ge(gT_lo_done, n)
                          if second:
                              for b in range(2):
                                  pe.wait_ge(y_out[b], i + START)
                          pe.wait_ge(f_lo, n * 3 + START)
                          down(1 - s, 0, second, False)
                          down(1 - s, 1, second, False).then_inc(f_used2, 1)

                  chunk(0, odd, first_=True)
                  chunk(1, 1 - odd, second=True)
                  with pe.Fori(1, NCH // 2) as two:
                      chunk(two * 2, odd)
                      chunk(two * 2 + 1, 1 - odd)
                  chunk(NCH - 1, odd, final=True)
                  n = base_n + NCH - 1
                  turn_x(i + 1, 1)
                  turn_g(n)
                  turn_x(i + 1, 2)
                  pe.wait_ge(gT_lo_done, n + 1)
                  pe.wait_ge(f_lo, n * 3 + 3 + START)
                  down(odd, 0, False, True)
                  turn_x(i + 1, 3)
                  down(odd, 1, False, True).then_inc(f_used2, 1)
                  if nb == 1:
                      pe.sem_inc(h13_done[1], NCH)
                  pe.nop()

              for kk in range(KT // 2):
                  turn_x(0, kk)
              with pe.Fori(0, (layer * (MOE_ITEMS - DENSE_ITEMS) + DENSE_ITEMS) // 2) as pair:
                for odd in range(2):
                  tokens = pe.value_load(item[0:1, 2, bass.ds(pair * 2 + odd, 1)], min_val=0, max_val=SEQ)
                  with pe.If(tokens > P):
                      with pe.If(tokens > P + HD):
                          work(pair, odd, 2)
                      with pe.Else():
                          work(pair, odd, 2, True)
                      pe.nop()
                  with pe.Else():
                      with pe.If(tokens > 0):
                          work(pair, odd, 1)
                      pe.nop()
                  pe.nop()
            pe.sem_inc(layer_done, 1)
            pe.wait_ge(layer_go, layer + 1)
            pe.nop()

    @block.scalar
    def _(act):
        fn = nc.scalar.activation

        with act.Fori(0, depth) as layer:
            n_xt = [0]

            def heads(dst, before=lambda t: None):
                for t, half in TURNS:
                    if half == 0:
                        before(t)
                    n = n_xt[0]
                    act.wait_ge(xt_done, n + 1)
                    fn(dst[:, 4 * half:4 * half + 4, t * P:(t + 1) * P],
                       bank[xt_bank[n % 4]][:].rearrange("p (k q) -> p k q", k=4), ACT.Copy).then_inc(xt_hi, 1)
                    n_xt[0] += 1

            def split_hi(j):
                s = j % 2
                w = W_IN[j][1] if j < NW_IN else WO_N
                if j == 0:
                    act.wait_ge(w0_loaded, (layer + 1) * 16)
                else:
                    act.wait_ge(wraw_loaded[s], (j + 1) // 2 * 16)
                if NW_IN <= j < NW_IN + 2:
                    act.wait_ge(mixed, 9)
                elif j >= NW_IN + 2:
                    act.wait_ge(unit_done, len(units) + (j - NW_IN - 1) * NT)
                elif j >= 2:
                    act.wait_ge(unit_done, unit_of[j - 2][-1] + 1)
                src = w_raw[:, s, :, 0:w] if j < NW_IN else wo_raw[:, s]
                fn(w_hi[:, s, :, 0:w], src, ACT.Copy).then_inc(w_hi_done, 1)

            def move_units(j):
                for u in unit_of[j]:
                    _, m, channels, off, w = units[u]
                    act.wait_ge(unit_done, u + 1)
                    if channels:
                        fn(xbcT[:, off + m, 3:3 + SEQ], bank[2 + u % 4][:], ACT.Copy).then_inc(proj_out, 1)
                    else:
                        fn(proj[:, m, off:off + w], bank[2 + u % 4][:, 0:w], ACT.Copy).then_inc(proj_out, 1)

            with act.If(layer > 0):
                split_hi(0)
                act.nop()
            for t in range(NT):
                act.wait_ge(x_loaded[t], 16)
                fn(h_tok[:, t, :], XH[:, t, :], ACT.Square, accum_out=ss_x[:, t:t + 1]).then_inc(x_squared, 1)

            def first_weights(t):
                if t == 2:
                    with act.If(layer < 1):
                        split_hi(0)
                        act.nop()

            heads(hT_hi, first_weights)
            split_hi(1)
            move_units(0)
            split_hi(2)
            move_units(1)
            split_hi(3)
            for m in range(XM):
                act.wait_ge(conv_done, m + 1)
                fn(xcT[:, m, :], xcT[:, m, :], ACT.Silu).then_inc(silu_done, 1)
            move_units(2)
            split_hi(4)
            move_units(3)
            split_hi(5)
            act.wait_ge(params_loaded, N_PARAMS * 16)
            act.wait_ge(soft_in, 1)
            fn(neg_a[:], prow[:, 8:16], ACT.Exp).then_inc(soft_exp, 1)
            fn(e12[:], g12[:], ACT.Exp).then_inc(soft_exp, 1)
            act.wait_ge(soft_exp, 2)
            fn(e12[:], e12[:], ACT.Ln, bias=1.0).then_inc(soft_ln, 1)
            move_units(4)
            split_hi(6)
            move_units(5)
            move_units(6)
            n_tr = [0]

            def take(dst, rows):
                n = n_tr[0]
                act.wait_ge(tr_done, n + 1)
                fn(dst, bank[n % 4][0:rows, :], ACT.Copy).then_inc(tr_out, 1)
                n_tr[0] += 1

            def take_head(dst, gain, both):
                n = n_tr[0]
                act.wait_ge(tr_done, n + 1)
                if both:
                    fn(dst[HD:P], bank[n % 4][0:HD, :], ACT.Copy, scale=gain[0:HD])
                fn(dst[0:HD], bank[n % 4][0:HD, :], ACT.Copy, scale=gain[0:HD]).then_inc(tr_out, 1)
                n_tr[0] += 1

            for c in range(NT):
                take(xs_tok[:, c, :], P)
            take(b_tok[:].rearrange("p t n -> p (t n)"), P)
            act.wait_ge(acs_ready, 1)
            fn(c_hi[:], c_t[:], ACT.Copy)
            fn(e_acs[:], acs[:], ACT.Exp)
            fn(e_end[:], to_end[:], ACT.Exp)
            fn(e_tot[:].rearrange("p t h -> p (t h)"), bank[6][:, 32:64], ACT.Exp).then_inc(decays_ready, 1)
            act.wait_ge(cols_ready, 1)
            for h in range(NF):
                take_head(q_f[:, h, :], qcol[:, 1:2], False)
                take_head(kh_f[:, h, :], cols[:, R_KF:R_KF + 1], True)
            for h in range(6):
                if h < NQ:
                    take_head(q_n[:, h, :], qcol[:, 0:1], False)
                else:
                    take_head(kh_n[:, h - NQ, :], cols[:, R_KN:R_KN + 1], True)
            take(kvT[:], P)
            act.wait_ge(c_set, 1)
            take(c_q[0:NCR], NCR)
            for h in range(NF):
                take(c_k[0:NCR, h, :], NCR)
            act.wait_ge(proj_out, len(units))
            fn(proj[:, :, z_col], proj[:, :, z_col], ACT.Silu).then_inc(z_ready, 1)

            def square_y(c):
                act.wait_ge(y_gated, c + 1)
                if c:
                    act.wait_ge(y_squared, c)
                fn(y_sq[:], XH[:, c, 256:768], ACT.Square, accum_out=ss_y[:, c:c + 1]).then_inc(y_squared, 1)

            for c in range(NT):
                act.wait_ge(ssd_diff, c + 1)
                fn(decay[:], decay[:], ACT.Exp).then_inc(ssd_exp, 1)
                if c:
                    square_y(c - 1)
            square_y(NT - 1)
            act.wait_ge(y_squared, NT)
            fn(gate_e[:], proj[:, :, C_G:C_G + 12], ACT.Exp, scale=-1.0).then_inc(gate_exp, 1)
            def exps(u):
                g, i, h, keys, _, _ = att[u]
                n = (i + 1) * P
                act.wait_ge(max_ready, u + 1)
                if u >= 3:
                    act.wait_ge(pT_done, u - 2)
                total = sum_f[:, i, h:h + 1] if keys is None else sum_n[:, i, h, keys - 3:keys - 2]
                fn(prob[:, u % 3, 0:n], bank[s_bank[u % 3]][:, 0:n], ACT.Exp, bias=neg_max[:, u % 8:u % 8 + 1],
                   accum_out=total).then_inc(exp_done, 1)

            for u in range(NU + 4):
                if u < NU:
                    exps(u)
                if u == 8:
                    act.wait_ge(kcT_done, 1)
                    for rows in (slice(HD, P), slice(0, HD)):
                        last = fn(kcT[rows, 0, 0:NC], bank[4][0:HD, 0:NC], ACT.Copy, scale=cols[0:HD, R_KN:R_KN + 1])
                    last.then_inc(kcT_out, 1)
                v = u - 2
                if 0 <= v < NU and by_act[v]:
                    n = (att[v][1] + 1) * P
                    act.wait_ge(pT_done, v + 1)
                    if v >= 2:
                        act.wait_ge(o_done, v - 1)
                    fn(probT[:, v % 2, 0:n], bank[2 + v % 2][:, 0:n], ACT.Copy).then_inc(pT_out_act, 1)
                for i in range(NT):
                    at = u - first_of[NT + i]
                    if at == 6:
                        act.wait_ge(c_shift, i + 1)
                        fn(p_cmp[:, :, 0:NC], p_cmp[:, :, 0:NC], ACT.Exp).then_inc(c_exp, 1)
                    if at == 9:
                        act.wait_ge(cT_done, i + 1)
                        if i:
                            act.wait_ge(c_out, i)
                        fn(pT_cmp[:].rearrange("c h q -> c (h q)"), bank[4][0:NC, :], ACT.Copy).then_inc(cT_out, 1)

            split_hi(NW_IN)
            heads(hT_hi)
            split_hi(NW_IN + 1)
            split_hi(NW_IN + 2)
            split_hi(NW_IN + 3)
            for t in range(NT):
                act.wait_ge(res_added, (NW_OUT - 1) * NT + t + 1)
                fn(XH[:, t, :], x_new[:, t, :], ACT.Square, accum_out=ss_x[:, t:t + 1]).then_inc(x_squared, 1)
            with act.If(layer > 0):
                heads(hT_f)
                act.wait_ge(gate_diff, 1)
                fn(gates[:, :, 1], gates[:, :, 0], ACT.Exp).then_inc(gate_e2, 1)
                act.nop()

            if do_ffn:
              act.wait_ge(dest_ready, 1)
              act.sem_inc(y_out[0], START)

              def split(n, which, s, parts, nb=0):
                  for part in parts:
                      act.wait_ge(f_loaded[s][part], (which + 1) * (16 if part == 2 else 32))
                      if part == 0:
                          if not isinstance(n, int):
                              act.wait_ge(h13_done[nb - 1], n - 1 + START)
                      if part == 2:
                          if not isinstance(n, int):
                              act.wait_ge(f_used2, n - 1 + START)
                          else:
                              act.wait_ge(stored, 2 * NT * 16)
                          fn(f_w2_hi[:, s], f_w2[:, s], ACT.Copy).then_inc(f_hi, 1)
                      else:
                          ks = slice(part * KT // 2, (part + 1) * KT // 2)
                          fn(f_w13_hi[:, s, ks].rearrange("p k a n -> p (k a n)"),
                             f_w13[:, s, ks].rearrange("p k a n -> p (k a n)"), ACT.Copy).then_inc(f_hi, 1)

              def heads_x(i, kk):
                  act.wait_ge(x_tr, i * (KT // 2) + kk + 1)
                  fn(xT_hi[:, 2 * kk:2 * kk + 2].rearrange("p k b q -> p (k b q)"), bank[x_bank(i, kk)][:], ACT.Copy
                     ).then_inc(x_hi, 1)

              def work(pair, odd, nb, small=False):
                  i = pair * 2 + odd
                  base_n = pair * PAIR + odd * NCH

                  def turned(n):
                      act.wait_ge(gT_done, n + 1 + START)
                      act.wait_ge(f_used2, n + START)
                      whole = 1 if small else nb
                      last = fn(gT_hi[:, 0:whole].rearrange("p b k q -> p (b k q)"), bank[6][:, 0:whole * FFC], ACT.Copy)
                      if small:
                          last = fn(gT_hi[:, 1, :, 0:HD], bank[6][:, FFC:2 * FFC].rearrange("p (k q) -> p k q", k=FK)[:, :, 0:HD],
                                    ACT.Copy)
                      last.then_inc(gT_hi_done, 1)

                  def silu_of(n, b):
                      act.wait_ge(h13_done[b], n + 1 + START)
                      act.wait_ge(gu_ready[b], n + START)
                      if b and small:
                          fn(part_up[:], bank[4 + b][HD:P, :], ACT.Copy).then_inc(part_out, 1)
                          act.wait_ge(part_sum, n + 1)
                          fn(silu[0:HD, b, :], part_up[:, 0:FFC], ACT.Silu).then_inc(silu_out[b], 1)
                          return
                      fn(silu[:, b, :], bank[4 + b][:, 0:FFC], ACT.Silu).then_inc(silu_out[b], 1)

                  def chunk(c, s, which, final=False):
                      n = base_n + c
                      if not isinstance(c, int) or c:
                          turned(n - 1)
                      split(n + 1, which, 1 - s, (0,), nb)
                      silu_of(n, 0)
                      split(n + 1, which, 1 - s, (1,))
                      if nb == 2:
                          silu_of(n, 1)
                      if not final:
                          split(n + 1, which, 1 - s, (2,))

                  def slot_count(c):
                      return pair * NCH + (odd * NCH + c) // 2

                  chunk(0, odd, slot_count(1))
                  chunk(1, 1 - odd, slot_count(2))
                  with act.Fori(1, NCH // 2) as two:
                      chunk(two * 2, odd, slot_count(1) + two)
                      chunk(two * 2 + 1, 1 - odd, slot_count(2) + two)
                  chunk(NCH - 1, odd, slot_count(NCH), final=True)
                  n = base_n + NCH - 1
                  heads_x(i + 1, 0)
                  heads_x(i + 1, 1)
                  turned(n)
                  heads_x(i + 1, 2)
                  heads_x(i + 1, 3)
                  split(n + 1, slot_count(NCH), 1 - odd, (2,))
                  act.wait_ge(f_used2, n + 1 + START)
                  act.wait_ge(y_added, (layer * DENSE_ITEMS + i) * 32 + 16)
                  act.wait_ge(slots_taken, i + 1)
                  for b in range(1 if small else nb):
                      last = fn(y_sb[:, b, 0:512], bank[2 * b][:], ACT.Copy, scale=slots[:].bitcast(F32)[:, b, 1:2])
                  if small:
                      for half in range(2):
                          last = fn(y_sb[0:HD, 1, half * 512:(half + 1) * 512], bank[2 + half][HD:P, :], ACT.Copy)
                  last.then_inc(y_out[0], 1)
                  if not small:
                      act.sem_inc(part_out, NCH)
                  if nb == 1:
                      act.sem_inc(silu_out[1], NCH)
                  act.nop()

              split(0, 0, 0, (0, 1))
              for kk in range(KT // 2):
                  heads_x(0, kk)
              split(0, 0, 0, (2,))
              with act.Fori(0, (layer * (MOE_ITEMS - DENSE_ITEMS) + DENSE_ITEMS) // 2) as pair:
                for odd in range(2):
                  tokens = act.value_load(item[0:1, 2, bass.ds(pair * 2 + odd, 1)], min_val=0, max_val=SEQ)
                  with act.If(tokens > P):
                      with act.If(tokens > P + HD):
                          work(pair, odd, 2)
                      with act.Else():
                          work(pair, odd, 2, True)
                      act.nop()
                  with act.Else():
                      with act.If(tokens > 0):
                          work(pair, odd, 1)
                      act.nop()
                  act.nop()
            act.sem_inc(layer_done, 1)
            act.wait_ge(layer_go, layer + 1)
            act.nop()

    @block.vector
    def _(dve):
        tt, ts, stt = nc.vector.tensor_tensor, nc.vector.tensor_scalar, nc.vector.scalar_tensor_tensor
        copy, total = nc.vector.tensor_copy, nc.vector.tensor_reduce

        with dve.Fori(0, depth) as layer:
            n_step, n_xt = [0], [0]

            def link(ins):
                n_step[0] += 1
                ins.then_inc(dve_step, 1)
                dve.wait_ge(dve_step, n_step[0])

            def mean(ss, n, done):
                ts(ss, ss, 1.0 / n, EPS, ALU.mult, ALU.add).then_inc(done, 1)

            def remainders(before=lambda t: None):
                for t, half in TURNS:
                    if half == 0:
                        before(t)
                    n = n_xt[0]
                    at = (slice(None), slice(4 * half, 4 * half + 4), slice(t * P, (t + 1) * P))
                    dve.wait_ge(xt_hi, n + 1)
                    tt(hT_lo[at], bank[xt_bank[n % 4]][:].rearrange("p (k q) -> p k q", k=4), hT_hi[at].bitcast(F32),
                       ALU.subtract).then_inc(xt_lo, 1)
                    n_xt[0] += 1

            def split_lo(j):
                s = j % 2
                w = W_IN[j][1] if j < NW_IN else WO_N
                dve.wait_ge(w_hi_done, j + 1)
                src = w_raw[:, s, :, 0:w] if j < NW_IN else wo_raw[:, s]
                tt(w_lo[:, s, :, 0:w], src, w_hi[:, s, :, 0:w].bitcast(F32), ALU.subtract
                   ).then_inc(w_lo_done, 1)

            def conv(m):
                dve.wait_ge(proj_out, m + 1)
                for tap in range(3, -1, -1):
                    w_ = cols[:, R_CW + tap * 6 + m:R_CW + tap * 6 + m + 1]
                    if tap == 3:
                        link(ts(xcT[:, m, :], xbcT[:, m, 3:3 + SEQ], w_, cols[:, R_CB + m:R_CB + m + 1], ALU.mult, ALU.add))
                    else:
                        ins = stt(xcT[:, m, :], xbcT[:, m, tap:tap + SEQ], w_, xcT[:, m, :], ALU.mult, ALU.add)
                        if tap:
                            link(ins)
                ins.then_inc(conv_done, 1)

            link(nc.vector.memset(xbcT[:, :, 0:3], 0.0))
            def mean_of(t, before):
                dve.wait_ge(x_squared, before + t + 1)
                mean(ss_x[:, t:t + 1], DM, ms_ready)

            def h_of(t):
                dve.wait_ge(rs_ready, t + 1)
                dve.wait_ge(x_loaded[t], 16)
                stt(h_tok[:, t, :], XH[:, t, :], rs_x[:, t:t + 1], g_row[:], ALU.mult, ALU.mult).then_inc(h_ready, 1)

            mean_of(0, 0)
            mean_of(1, 0)
            dve.wait_ge(g0_loaded, (layer + 1) * 16)
            h_of(0)
            mean_of(2, 0)
            mean_of(3, 0)
            def before_turn(t):
                if t + 1 < NT:
                    h_of(t + 1)
                else:
                    dve.wait_ge(w_hi_done, 1)
                    part, w = slice(W0_POOL, KT), W_IN[0][1]
                    tt(w_lo[:, 0, part, 0:w], w_raw[:, 0, part, 0:w], w_hi[:, 0, part, 0:w].bitcast(F32),
                       ALU.subtract).then_inc(w0_rest, 1)

            remainders(before_turn)
            dve.wait_ge(w_lo_done, 1)
            split_lo(1)
            dve.wait_ge(cols_t, 1)
            link(copy(cols[:], bank[5][:, 0:NR]))
            for n, row in enumerate((R_QN, R_QF)):
                last = ts(qcol[:, n:n + 1], cols[:, row:row + 1], HD ** -0.5, None, ALU.mult)
            last.then_inc(cols_ready, 1)
            split_lo(2)
            for m in range(3):
                conv(m)
            split_lo(3)
            for m in range(3, XM):
                conv(m)
            split_lo(4)
            dve.wait_ge(params_loaded, N_PARAMS * 16)
            dve.wait_ge(proj_out, unit_of[3][-1] + 1)
            tt(dt_t[:], proj[:, :, O_DT:O_DT + NS], bc(prow[:, 0:8].unsqueeze(1), NT, NS), ALU.add)
            link(tt(logf[:], proj[:, :, O_FF:O_FF + NF], bc(prow[:, 24:28].unsqueeze(1), NT, NF), ALU.add))
            stt(g12[:, :, 0:8], dt_t[:], -1.0, dt_t[:], ALU.mult, ALU.min)
            stt(g12[:, :, 8:12], logf[:], -1.0, logf[:], ALU.mult, ALU.min).then_inc(soft_in, 1)
            split_lo(5)
            dve.wait_ge(head_sq, 1)
            link(total(ss_f[:], sq_f.rearrange("p t (h d) -> p t h d", d=HD), AX.X, ALU.add))
            mean(ss_f[:], HD, head_ms)
            dve.wait_ge(soft_exp, 2)
            dve.wait_ge(soft_ln, 1)
            stt(dt_t[:], dt_t[:], 0.0, e12[:, :, 0:8], ALU.max, ALU.add)
            link(stt(logf[:], logf[:], 0.0, e12[:, :, 8:12], ALU.min, ALU.subtract))
            stt(dta[:], dt_t[:], -1.0, bc(neg_a[:].unsqueeze(1), NT, NS), ALU.mult, ALU.mult)
            link(copy(logf_before[:, 1, :], logf[:, 0, :]))
            link(tt(logf_before[:, 2, :], logf_before[:, 1, :], logf[:, 1, :], ALU.add))
            tt(logf_before[:, 3, :], logf_before[:, 2, :], logf[:, 2, :], ALU.add).then_inc(soft_done, 1)
            dve.wait_ge(head_rs, 1)
            for n, (dst, off) in enumerate(((qa, O_QF), (ka, O_KF))):
                for t in range(NT):
                    last = tt(dst[:, t], proj[:, t, off:off + 256].rearrange("p (h d) -> p h d", d=HD),
                              bc(rs_f[:, t, 4 * n:4 * n + 4].unsqueeze(2), NF, HD), ALU.mult)
            last.then_inc(fox_ready, 1)
            split_lo(6)
            dve.wait_ge(head_sq, 2)
            link(total(ss_n[:], sq_n.rearrange("p t (h d) -> p t h d", d=HD), AX.X, ALU.add))
            mean(ss_n[:], HD, head_ms)
            dve.wait_ge(sums_done, 1)
            flat_th = "p t h -> p (t h)"
            link(copy(acs[:].rearrange(flat_th), bank[6][:, 0:32]))
            copy(c_t[:].rearrange(flat_th), bank[6][:, 64:80])
            tt(to_end[:].rearrange(flat_th), bank[6][:, 32:64], acs[:].rearrange(flat_th), ALU.subtract
               ).then_inc(acs_ready, 1)
            dve.wait_ge(head_rs, 2)
            for t in range(NT):
                tt(qn[:, t, 0:4, :], proj[:, t, 0:256].rearrange("p (h d) -> p h d", d=HD),
                   bc(rs_n[:, t, 0:4].unsqueeze(2), 4, HD), ALU.mult)
            for n in range(2):
                kv_ = C_KV + P * (n + 1)
                last = tt(qn[:, :, 4 + n, :], proj[:, :, kv_:kv_ + HD], bc(rs_n[:, :, 4 + n].unsqueeze(2), NT, HD), ALU.mult)
            last.then_inc(nsa_ready, 1)
            dve.wait_ge(decays_ready, 1)
            dve.wait_ge(c_set, 1)
            c_h = c_hi[:].bitcast(F32)
            copy(c_src[:, :, 0, 0:NF], c_h)
            tt(c_src[:, :, 0, NF:2 * NF], c_t[:], c_h, ALU.subtract)
            ts(c_src[:, :, 1:1 + NF, 2 * NF], c_h, -1.0, None, ALU.mult)
            tt(c_src[:, :, 1:1 + NF, 2 * NF + 1], c_h, c_t[:], ALU.subtract).then_inc(c_ready, 1)

            n_take = [NT + 1]

            def take_lo(dst, src, gain, both):
                dve.wait_ge(tr_out, n_take[0] + 1)
                b = bank[n_take[0] % 4]
                if both:
                    link(stt(dst[0:HD], b[0:HD, :], gain[0:HD], src[0:HD].bitcast(F32), ALU.mult, ALU.subtract))
                    copy(dst[HD:P], dst[0:HD].bitcast(F32)).then_inc(tr_lo, 1)
                else:
                    stt(dst[HD:P], b[0:HD, :], gain[0:HD], src[0:HD].bitcast(F32), ALU.mult, ALU.subtract
                        ).then_inc(tr_lo, 1)
                n_take[0] += 1

            for h in range(NF):
                take_lo(q_f[:, h, :], q_f[:, h, :], qcol[:, 1:2], False)
                take_lo(kl_f[:, h, :], kh_f[:, h, :], cols[:, R_KF:R_KF + 1], True)
            for h in range(6):
                if h < NQ:
                    take_lo(q_n[:, h, :], q_n[:, h, :], qcol[:, 0:1], False)
                else:
                    take_lo(kl_n[:, h - NQ, :], kh_n[:, h - NQ, :], cols[:, R_KN:R_KN + 1], True)

            def by_head(ap):
                return ap.rearrange("p (h d) -> p h d", h=NS)

            dve.wait_ge(tr_out, 20)
            for v in range(2):
                at = R_PE + CMP_STRIDE * v
                tt(kv_pe[:, v], kvT[:].rearrange("p (b j) -> p b j", j=CMP_STRIDE),
                   bc(cols[:, at:at + CMP_STRIDE].unsqueeze(1), CMP_BLK, CMP_STRIDE), ALU.add).then_inc(pe_added, 1)
            for c in range(NT):
                dve.wait_ge(ssd_scores, c + 1)
                if c:
                    dve.wait_ge(ssd_y, c)
                for half in range(2):
                    hs = slice(4 * half, 4 * half + 4)
                    last = tt(decay[:, hs, :], bank[2 + half][:].rearrange("p (h l) -> p h l", h=4),
                              bc(acs[:, c, hs].unsqueeze(2), 4, P), ALU.subtract)
                last.then_inc(ssd_diff, 1)
                dve.wait_ge(ssd_exp, c + 1)
                for g in range(2):
                    hs = slice(4 * g, 4 * g + 4)
                    last = tt(decay[:, hs, :], decay[:, hs, :], bc(bank[4][:, g * P:(g + 1) * P].unsqueeze(1), 4, P),
                              ALU.mult)
                last.then_inc(ssd_m, 1)
                if c < NT - 1:
                    dve.wait_ge(ssd_new, c + 1)
                else:
                    dve.wait_ge(kc_done, 1)
                    copy(vc[:], bank[1][0:NC, 0:HD])
                    link(copy(kc_n[:], bank[0][0:NC, 0:HD]))
                    link(tt(kc_sq[:], kc_n[:], kc_n[:], ALU.mult))
                    link(total(ss_c[:], kc_sq[:], AX.X, ALU.add))
                    mean(ss_c[:], HD, kc_ms)
                    dve.wait_ge(ssd_y, c + 1)
                if c:
                    link(tt(by_head(y_t[:]), by_head(bank[5][:]), bc(e_acs[:, c, :].unsqueeze(2), NS, HD), ALU.mult))
                if c < NT - 1:
                    if c == 0:
                        copy(state[:], bank[7][:, 0:256]).then_inc(state_ready, 1)
                    else:
                        for g in range(2):
                            gp = slice(g * HD, (g + 1) * HD)
                            e_ = e_tot[gp, c, 4 * g:4 * g + 4].unsqueeze(2).to_broadcast([HD, 4, HD])
                            last = tt(state[gp, :].rearrange("p (h d) -> p h d", h=4),
                                      state[gp, :].rearrange("p (h d) -> p h d", h=4), e_, ALU.mult)
                        link(last)
                        tt(state[:], state[:], bank[7][:, 0:256], ALU.add).then_inc(state_ready, 1)
                dve.wait_ge(xdt_ready, c + 1)
                dve.wait_ge(ssd_y, c + 1)
                if c:
                    link(tt(y_t[:], y_t[:], xs_d[c % 2][:], ALU.add))
                    link(tt(y_t[:], bank[6][:], y_t[:], ALU.add))
                else:
                    link(tt(y_t[:], bank[6][:], xs_d[c % 2][:], ALU.add))
                dve.wait_ge(z_ready, 1)
                tt(XH[:, c, 256:768], y_t[:], proj[:, c, z_col], ALU.mult).then_inc(y_gated, 1)
            dve.wait_ge(y_squared, NT)
            mean(ss_y[:], 512, y_ms)
            def finalize(g):
                i = g % NT
                dve.wait_ge(o_done, last_of[g] + 1)
                b = bank[6 + g % 2]

                def heads_of(ap):
                    return ap.rearrange("p (h d) -> p h d", h=NQ)
                if g < NT:
                    link(ts(coef[:, :, 0], sum_f[:, i, :], TINY, None, ALU.max))
                    link(nc.vector.reciprocal(coef[:, :, 0], coef[:, :, 0]))
                    last = tt(heads_of(XH[:, i, 768:1024]), heads_of(b[:, 0:256]), bc(coef[:, :, 0].unsqueeze(2), NF, HD),
                              ALU.mult)
                else:
                    dve.wait_ge(c_out, i + 1)
                    link(ts(coef[:], sum_n[:, i], TINY, None, ALU.max))
                    link(nc.vector.reciprocal(coef[:], coef[:]))
                    link(tt(coef[:], coef[:], gate_e[:, i, :].rearrange("p (h b) -> p h b", b=3), ALU.mult))
                    for dst, src, br in ((o_acc[:], bank[4][:, 0:256], 0), (o_part[:], b[:, 0:256], 1)):
                        ins = tt(heads_of(dst), heads_of(src), bc(coef[:, :, br].unsqueeze(2), NQ, HD), ALU.mult)
                    link(ins)
                    link(tt(o_acc[:], o_acc[:], o_part[:], ALU.add))
                    link(tt(heads_of(o_part[:]), heads_of(b[:, 256:512]), bc(coef[:, :, 2].unsqueeze(2), NQ, HD), ALU.mult))
                    last = tt(XH[:, i, 0:256], o_acc[:], o_part[:], ALU.add)
                last.then_inc(o_read, 1)
                dve.wait_ge(o_read, g + 1)
                dve.sem_inc(mixed, 1)

            for u in range(NU + 5):
                if u < NU:
                    n = (att[u][1] + 1) * P
                    dve.wait_ge(scores_done, u + 1)
                    total(neg_max[:, u % 8:u % 8 + 1], bank[s_bank[u % 3]][:, 0:n], AX.X, ALU.max, negate=True
                          ).then_inc(max_ready, 1)
                if u == 4:
                    dve.wait_ge(kc_rs, 1)
                    ts(kc_n[:], kc_n[:], rs_c[:], None, ALU.mult).then_inc(kc_ready, 1)
                if u == 5:
                    dve.wait_ge(gate_exp, 1)
                    link(ts(gate_e[:], gate_e[:], 1.0, None, ALU.add))
                    link(nc.vector.reciprocal(gate_e[:], gate_e[:]))
                if u == 6:
                    dve.wait_ge(y_rs, 1)
                    for c in range(NT):
                        last = stt(XH[:, c, 256:768], XH[:, c, 256:768], rs_y[:, c:c + 1], ssd_g[:], ALU.mult, ALU.mult)
                    last.then_inc(mixed, 1)
                if u == 9:
                    dve.wait_ge(kcT_out, 1)
                    link(stt(kcT[0:HD, 1, 0:NC], bank[4][0:HD, 0:NC], cols[0:HD, R_KN:R_KN + 1],
                             kcT[0:HD, 0, 0:NC].bitcast(F32), ALU.mult, ALU.subtract))
                    copy(kcT[HD:P, 1, 0:NC], kcT[0:HD, 1, 0:NC].bitcast(F32)).then_inc(kcT_lo, 1)
                v = u - 2
                if 0 <= v < NU and not by_act[v]:
                    n = (att[v][1] + 1) * P
                    dve.wait_ge(pT_done, v + 1)
                    if v >= 2:
                        dve.wait_ge(o_done, v - 1)
                    copy(probT[:, v % 2, 0:n], bank[2 + v % 2][:, 0:n]).then_inc(pT_out_dve, 1)
                for i in range(NT):
                    at = u - first_of[NT + i]
                    s_c = bank[4][:, 256:384].rearrange("p (h c) -> p h c", h=NQ)[:, :, 0:NC]
                    pc = p_cmp[:, :, 0:NC]
                    if at == 5:
                        dve.wait_ge(c_scores, i + 1)
                        if i:
                            dve.wait_ge(cT_done, i)
                        link(total(neg_max_c[:], s_c, AX.X, ALU.max, negate=True))
                        tt(pc, s_c, bc(neg_max_c[:].unsqueeze(2), NQ, NC), ALU.add).then_inc(c_shift, 1)
                    if at == 7:
                        dve.wait_ge(c_exp, i + 1)
                        link(tt(pc, pc, bc(cmp_01[:, i, 0:NC].unsqueeze(1), NQ, NC), ALU.mult))
                        total(sum_n[:, i, :, 0], pc, AX.X, ALU.add).then_inc(c_prob, 1)
                for g in range(2 * NT):
                    if u == last_of[g] + 4:
                        finalize(g)

            split_lo(NW_IN)
            remainders()
            split_lo(NW_IN + 1)
            dve.wait_ge(grow_loaded, 16)

            def h2_of(t):
                dve.wait_ge(rs_ready, NT + t + 1)
                stt(XH[:, t, :], x_new[:, t, :], rs_x[:, t:t + 1], g_row[:], ALU.mult, ALU.mult).then_inc(h_ready, 1)

            for n in range(NW_OUT):
                for t in range(NT):
                    v = n * NT + t
                    dve.wait_ge(unit_done, len(units) + v + 1)
                    if n == 0:
                        dve.wait_ge(x_again[t], 16)
                    cs = slice(n * WO_N, (n + 1) * WO_N)
                    tt(x_new[:, t, cs], x_new[:, t, cs], bank[2 + v % 4][:, 0:WO_N], ALU.add).then_inc(res_added, 1)
                    if n == NW_OUT - 1 and t >= 1:
                        mean_of(t - 1, NT)
                    if n == NW_OUT - 1 and t >= 2:
                        h2_of(t - 2)
                if n < 2:
                    split_lo(NW_IN + 2 + n)
            mean_of(NT - 1, NT)
            h2_of(NT - 2)
            h2_of(NT - 1)

            with dve.If(layer > 0):
                r_step = [0]

                def rlink(ins):
                    r_step[0] += 1
                    ins.then_inc(route_step, 1)
                    dve.wait_ge(route_step, r_step[0])

                dve.wait_ge(logits_done, 1)
                rlink(copy(lg[:].rearrange("p t e -> p (t e)"), bank[2][:, 0:NT * NE]))
                iota_b = bc(iota_m[:].unsqueeze(1), NT, NE)
                for c, oh in enumerate((oh1, oh2)):
                    rlink(total(top_v[:, :, c], lg[:], AX.X, ALU.max))
                    rlink(tt(eq[:], lg[:], bc(top_v[:, :, c].unsqueeze(2), NT, NE), ALU.is_equal))
                    rlink(tt(eq[:], eq[:], iota_b, ALU.mult))
                    rlink(total(first[:, :, c], eq[:], AX.X, ALU.min))
                    rlink(tt(oh[:], iota_b, bc(first[:, :, c].unsqueeze(2), NT, NE), ALU.is_equal))
                    if c == 0:
                        rlink(stt(lg[:], oh[:], -3e38, lg[:], ALU.mult, ALU.add))
                tt(gates[:, :, 0], top_v[:, :, 1], top_v[:, :, 0], ALU.subtract).then_inc(gate_diff, 1)
                rlink(tt(member[:], oh1[:], oh2[:], ALU.add))
                for t in range(NT):
                    rlink(tt(member_before[:, t + 1, :], member_before[:, t, :], member[:, t, :], ALU.add))
                dve.sem_inc(routed, 1)
                dve.wait_ge(gate_e2, 1)
                rlink(ts(gates[:, :, 0], gates[:, :, 1], 1.0, None, ALU.add))
                rlink(nc.vector.reciprocal(gates[:, :, 0], gates[:, :, 0]))
                rlink(tt(gates[:, :, 1], gates[:, :, 1], gates[:, :, 0], ALU.mult))
                for c in range(2):
                    copy(rows_i[:].bitcast(F32)[:, c, :, 1], gates[:, :, c])
                dve.wait_ge(ranks_done, 1)
                rlink(tt(place_e[:], bank[3][:, 0:NT * NE].rearrange("p (t e) -> p t e", e=NE),
                        bc(base_e[:].unsqueeze(1), NT, NE), ALU.add))
                for c, oh in enumerate((oh1, oh2)):
                    rlink(tt(eq[:], place_e[:], oh[:], ALU.mult))
                    rlink(total(dest[:, :, c], eq[:], AX.X, ALU.add))
                copy(dest_i[:].rearrange("p c t -> p t c"), dest[:]).then_inc(slots_known, 1)
                rlink(tt(left[:], bc(bank[3][:, 32:40].unsqueeze(2), NE, 2), base_p[:], ALU.subtract))
                rlink(ts(left[:], left[:], 0.0, None, ALU.max))
                left_s = left[:].rearrange("p e h -> p (e h)")

                def along_items(ap):
                    return bc(ap.unsqueeze(1), NSEG, NSEG)

                rlink(ts(has[:], left_s, 0.0, None, ALU.is_gt))
                rlink(total(count_f[:], has[:], AX.X, ALU.add))
                copy(n_items[:], count_f[:])
                rlink(tt(sel_v[:], seg_before[:], along_items(has[:]), ALU.mult))
                rlink(total(pos[:], sel_v[:], AX.X, ALU.add))
                rlink(tt(sel[:], along_items(pos[:]), bc(seg[:, 0, :].unsqueeze(2), NSEG, NSEG), ALU.is_equal))
                rlink(tt(sel[:], sel[:], along_items(has[:]), ALU.mult))
                for n, value in enumerate((seg[:, 2, :], seg[:, 1, :], left_s)):
                    rlink(tt(sel_v[:], sel[:], along_items(value), ALU.mult))
                    rlink(total(item_f[:, n, :], sel_v[:], AX.X, ALU.add))
                rlink(ts(item_f[:, 0, :], item_f[:, 0, :], float(SLOTS // P), None, ALU.add))
                copy(item[:], item_f[:]).then_inc(dest_ready, 1)
                dve.nop()
            with dve.Else():
                dve.sem_inc(dest_ready, 1)
            dve.nop()

            if do_ffn:
              dve.wait_ge(dest_ready, 1)
              for s_ in (f_lo, *gu_ready, y_out[1]):
                  dve.sem_inc(s_, START)

              def split(n, s, parts):
                  for part in parts:
                      dve.wait_ge(f_hi, n * 3 + part + 1)
                      if part == 2:
                          tt(f_w2_lo[:, s], f_w2[:, s], f_w2_hi[:, s].bitcast(F32), ALU.subtract).then_inc(f_lo, 1)
                      else:
                          ks = slice(part * KT // 2, (part + 1) * KT // 2)
                          flat = "p k a n -> p (k a n)"
                          tt(f_w13_lo[:, s, ks].rearrange(flat), f_w13[:, s, ks].rearrange(flat),
                             f_w13_hi[:, s, ks].bitcast(F32).rearrange(flat), ALU.subtract).then_inc(f_lo, 1)

              def remainders_x(i, kk):
                  dve.wait_ge(x_hi, i * (KT // 2) + kk + 1)
                  tt(xT_lo[:, 2 * kk:2 * kk + 2].rearrange("p k b q -> p (k b q)"), bank[x_bank(i, kk)][:],
                     xT_hi[:, 2 * kk:2 * kk + 2].bitcast(F32).rearrange("p k b q -> p (k b q)"), ALU.subtract
                     ).then_inc(x_lo, 1)

              def work(pair, odd, nb, small=False):
                  i = pair * 2 + odd
                  base_n = pair * PAIR + odd * NCH

                  def turned(n):
                      dve.wait_ge(gT_hi_done, n + 1)
                      whole = 1 if small else nb
                      last = tt(gT_lo[:, 0:whole].rearrange("p b k q -> p (b k q)"), bank[6][:, 0:whole * FFC],
                                gT_hi[:, 0:whole].bitcast(F32).rearrange("p b k q -> p (b k q)"), ALU.subtract)
                      if small:
                          last = tt(gT_hi[:, 1, :, HD:P],
                                    bank[6][:, FFC:2 * FFC].rearrange("p (k q) -> p k q", k=FK)[:, :, 0:HD],
                                    gT_hi[:, 1, :, 0:HD].bitcast(F32), ALU.subtract)
                      last.then_inc(gT_lo_done, 1)

                  def gate(n, b):
                      if b and small:
                          dve.wait_ge(part_out, n + 1)
                          tt(part_up[:], bank[4 + b][0:HD, :], part_up[:], ALU.add).then_inc(part_sum, 1)
                          dve.wait_ge(silu_out[b], n + 1)
                          dve.wait_ge(gT_done, n + START)
                          tt(gate_up[0:HD, b, :], silu[0:HD, b, :], part_up[:, FFC:2 * FFC], ALU.mult
                             ).then_inc(gu_ready[b], 1)
                          return
                      dve.wait_ge(silu_out[b], n + 1)
                      dve.wait_ge(gT_done, n + START)
                      tt(gate_up[:, b, :], silu[:, b, :], bank[4 + b][:, FFC:2 * FFC], ALU.mult).then_inc(gu_ready[b], 1)

                  def chunk(c, s, final=False):
                      n = base_n + c
                      if not isinstance(c, int) or c:
                          turned(n - 1)
                      split(n + 1, 1 - s, (0,))
                      gate(n, 0)
                      split(n + 1, 1 - s, (1,))
                      if nb == 2:
                          gate(n, 1)
                      if not final:
                          split(n + 1, 1 - s, (2,))

                  if small:
                      dve.wait_ge(x_lo, (i + 1) * (KT // 2))
                      copy(xT_hi[:, :, 1, HD:P], xT_lo[:, :, 1, 0:HD].bitcast(F32)).then_inc(x_stacked, 1)
                  chunk(0, odd)
                  chunk(1, 1 - odd)
                  dve.wait_ge(slots_loaded, (layer * (DENSE_ITEMS + 1) + i + 1) * 16)
                  dve.wait_ge(y_added, (layer * DENSE_ITEMS + i) * 32 + 16)
                  copy(slots[:], slots_next[:]).then_inc(slots_taken, 1)
                  with dve.Fori(1, NCH // 2) as two:
                      chunk(two * 2, odd)
                      chunk(two * 2 + 1, 1 - odd)
                  chunk(NCH - 1, odd, final=True)
                  n = base_n + NCH - 1
                  remainders_x(i + 1, 0)
                  remainders_x(i + 1, 1)
                  turned(n)
                  remainders_x(i + 1, 2)
                  remainders_x(i + 1, 3)
                  dve.wait_ge(f_used2, n + 1 + START)
                  for b in range(1 if small else nb):
                      last = ts(y_sb[:, b, 512:DM], bank[2 * b + 1][:], slots[:].bitcast(F32)[:, b, 1:2], None, ALU.mult)
                  if small:
                      dve.wait_ge(y_out[0], i + 1 + START)
                      for half in range(2):
                          y_ = y_sb[0:HD, 1, half * 512:(half + 1) * 512]
                          last = tt(y_, bank[2 + half][0:HD, :], y_, ALU.add)
                      last.then_inc(y_step, 1)
                      dve.wait_ge(y_step, i + 1)
                      last = ts(y_sb[0:HD, 1, :], y_sb[0:HD, 1, :], slots[:].bitcast(F32)[0:HD, 1, 1:2], None, ALU.mult)
                  last.then_inc(y_out[1], 1)
                  split(n + 1, 1 - odd, (2,))
                  if not small:
                      for s_, by in ((x_stacked, 1), (part_sum, NCH), (y_step, 1)):
                          dve.sem_inc(s_, by)
                  if nb == 1:
                      dve.sem_inc(gu_ready[1], NCH)
                  dve.nop()

              split(0, 0, (0, 1))
              for kk in range(KT // 2):
                  remainders_x(0, kk)
              split(0, 0, (2,))
              with dve.Fori(0, (layer * (MOE_ITEMS - DENSE_ITEMS) + DENSE_ITEMS) // 2) as pair:
                for odd in range(2):
                  tokens = dve.value_load(item[0:1, 2, bass.ds(pair * 2 + odd, 1)], min_val=0, max_val=SEQ)
                  with dve.If(tokens > P):
                      with dve.If(tokens > P + HD):
                          work(pair, odd, 2)
                      with dve.Else():
                          work(pair, odd, 2, True)
                      dve.nop()
                  with dve.Else():
                      with dve.If(tokens > 0):
                          work(pair, odd, 1)
                      dve.nop()
                  dve.nop()
            dve.sem_inc(layer_done, 1)
            dve.wait_ge(layer_go, layer + 1)
            dve.nop()

    block_cm.__exit__(None, None, None)


_INS = ['x', 'attn_norm', 'w_in', 'nsa_q_norm', 'nsa_k_norm', 'nsa_cmp_pe_k', 'nsa_cmp_pe_v', 'nsa_cmp_w_k',
        'nsa_cmp_w_v', 'ssd_conv_w', 'ssd_conv_b', 'ssd_dt_bias', 'ssd_a_log', 'ssd_d', 'ssd_norm', 'fox_q_norm',
        'fox_k_norm', 'fox_f_bias', 'w_out', 'ffn_norm', 'ffn_w1', 'ffn_w3', 'ffn_w2', 'moe_router', 'moe_w1',
        'moe_w3', 'moe_w2']


def kernel(**inputs):
    import numpy as _np
    import concourse.bacc as _bacc
    from concourse import mybir as _mybir
    from concourse.bass_utils import run_bass_kernel_spmd as _run

    nc = _bacc.Bacc("TRN2", target_bir_lowering=False, num_devices=1)
    arrays, args = {}, []
    for name in _INS:
        a = _np.ascontiguousarray(inputs[name])
        if name == 'x':
            a = a.reshape(SEQ, DM)
        arrays[f"in_{name}_dram"] = a
        args.append(nc.dram_tensor(f"in_{name}_dram", a.shape, _mybir.dt.from_np(a.dtype), kind="ExternalInput").ap())
    args.append(nc.dram_tensor("out_0_dram", (SEQ, DM), _mybir.dt.float32, kind="ExternalOutput").ap())
    build_program(nc, *args)
    r = _run(nc, [arrays], core_ids=[0])
    return r.results[0]["out_0_dram"].reshape(1, SEQ, DM)
```
